# Optimizing a Trainium2 kernel written in Bass

```python
import jax, jax.numpy as jnp
from jax import lax
import numpy as np

D_MODEL = 1024
BATCH = 1
SEQ = 512
DEPTH = 1

MLA_HEADS = 8
QK_NOPE_DIM = 128
QK_ROPE_DIM = 64
V_HEAD_DIM = 128
Q_LORA_RANK = 256
KV_LORA_RANK = 256
ROPE_THETA = 10000.0
Q_BLOCK = 128
SSM_D_INNER = 2 * D_MODEL
SSM_HEAD_DIM = 64
SSM_HEADS = SSM_D_INNER // SSM_HEAD_DIM
SSM_GROUPS = 8
SSM_HEADS_PER_GROUP = SSM_HEADS // SSM_GROUPS
SSM_STATE = 128
CONV_WIDTH = 4
SSD_CHUNK = 128
CONV_CH = SSM_D_INNER + 2 * SSM_GROUPS * SSM_STATE
D_FF = 4 * D_MODEL
EPS = 1e-6
IN_SIZES = (Q_LORA_RANK, KV_LORA_RANK, QK_ROPE_DIM, SSM_D_INNER, CONV_CH, SSM_HEADS, D_MODEL, D_MODEL)
IN_COLS = Q_LORA_RANK + KV_LORA_RANK + QK_ROPE_DIM + SSM_D_INNER + CONV_CH + SSM_HEADS + 2 * D_MODEL

kernel_name = "hybrid_mla_ssd_gated_block"

def rms_norm(x, g):
    xf = x.astype(jnp.float32)
    y = xf * lax.rsqrt(jnp.mean(xf * xf, axis=-1, keepdims=True) + EPS)
    return (y * g.astype(jnp.float32)).astype(x.dtype)

def split_cols(t, sizes):
    idx = [int(v) for v in np.cumsum(sizes)[:-1]]
    return jnp.split(t, idx, axis=-1)

def rope_tables(positions):
    half = QK_ROPE_DIM // 2
    inv = ROPE_THETA ** (-jnp.arange(half, dtype=jnp.float32) / half)
    ang = positions.astype(jnp.float32)[..., None] * inv
    return jnp.cos(ang), jnp.sin(ang)

def apply_rope(t, cos, sin):
    half = QK_ROPE_DIM // 2
    t1, t2 = t[..., :half], t[..., half:]
    return jnp.concatenate([t1 * cos - t2 * sin, t1 * sin + t2 * cos], axis=-1).astype(t.dtype)

def mla_attention(q_lat, kv_lat, k_rope, positions, g_q, g_kv, w_uq, w_ukv):
    B, S, _ = q_lat.shape
    q = (rms_norm(q_lat, g_q) @ w_uq).reshape(B, S, MLA_HEADS, QK_NOPE_DIM + QK_ROPE_DIM)
    q_nope, q_rope = q[..., :QK_NOPE_DIM], q[..., QK_NOPE_DIM:]
    kv = (rms_norm(kv_lat, g_kv) @ w_ukv).reshape(B, S, MLA_HEADS, QK_NOPE_DIM + V_HEAD_DIM)
    k_nope, v = kv[..., :QK_NOPE_DIM], kv[..., QK_NOPE_DIM:]
    cos, sin = rope_tables(positions)
    q_rope = apply_rope(q_rope, cos[:, :, None, :], sin[:, :, None, :])
    k_rope = apply_rope(k_rope, cos, sin)
    scale = (QK_NOPE_DIM + QK_ROPE_DIM) ** -0.5
    outs = []
    for i in range(S // Q_BLOCK):
        q0, q1 = i * Q_BLOCK, (i + 1) * Q_BLOCK
        s = (jnp.einsum('bqhd,bkhd->bhqk', q_nope[:, q0:q1], k_nope[:, :q1]).astype(jnp.float32)
             + jnp.einsum('bqhr,bkr->bhqk', q_rope[:, q0:q1], k_rope[:, :q1]).astype(jnp.float32)) * scale
        causal = jnp.arange(q1)[None, :] <= jnp.arange(q0, q1)[:, None]
        p = jax.nn.softmax(jnp.where(causal, s, -jnp.inf), axis=-1).astype(v.dtype)
        outs.append(jnp.einsum('bhqk,bkhd->bqhd', p, v[:, :q1]))
    return jnp.concatenate(outs, axis=1).reshape(B, S, MLA_HEADS * V_HEAD_DIM)

def causal_depthwise_conv(u, w, b):
    S = u.shape[1]
    up = jnp.pad(u, ((0, 0), (CONV_WIDTH - 1, 0), (0, 0)))
    out = b
    for k in range(CONV_WIDTH):
        out = out + up[:, k:k + S] * w[k]
    return out

def ssd_chunked(xh, dt, A, Bm, Cm):
    Bsz, S, G, Hg, P = xh.shape
    N = Bm.shape[-1]
    L = SSD_CHUNK
    nc = S // L
    xdt = (xh * dt[..., None]).reshape(Bsz, nc, L, G, Hg, P)
    a_cum = jnp.cumsum((dt * A).reshape(Bsz, nc, L, G, Hg), axis=2)
    Bc = Bm.reshape(Bsz, nc, L, G, N).astype(jnp.float32)
    Cc = Cm.reshape(Bsz, nc, L, G, N).astype(jnp.float32)
    seg = a_cum[:, :, :, None] - a_cum[:, :, None, :]
    tri = jnp.tril(jnp.ones((L, L), dtype=bool))[:, :, None, None]
    decay = jnp.exp(jnp.where(tri, seg, -jnp.inf))
    cb = jnp.einsum('bclgn,bcsgn->bclsg', Cc, Bc)
    y_diag = jnp.einsum('bclsg,bclsgh,bcsghp->bclghp', cb, decay, xdt)
    decay_to_end = jnp.exp(a_cum[:, :, -1:] - a_cum)
    states = jnp.einsum('bclgn,bclgh,bclghp->bcghpn', Bc, decay_to_end, xdt)
    chunk_decay = jnp.exp(a_cum[:, :, -1])

    def step(h, inp):
        s_c, d_c = inp
        return h * d_c[..., None, None] + s_c, h

    h0 = jnp.zeros((Bsz, G, Hg, P, N), dtype=states.dtype)
    _, h_prev = lax.scan(step, h0, (jnp.moveaxis(states, 1, 0), jnp.moveaxis(chunk_decay, 1, 0)))
    h_prev = jnp.moveaxis(h_prev, 0, 1)
    y_off = jnp.einsum('bclgn,bcghpn,bclgh->bclghp', Cc, h_prev, jnp.exp(a_cum))
    return (y_diag + y_off).reshape(Bsz, S, G, Hg, P)

def mamba2_mixer(z, xbc, dt_raw, conv_w, conv_b, dt_bias, a_log, d_skip, g_ssm_out):
    B, S, _ = z.shape
    xbc = jax.nn.silu(causal_depthwise_conv(xbc, conv_w, conv_b))
    xs, Bm, Cm = split_cols(xbc, (SSM_D_INNER, SSM_GROUPS * SSM_STATE, SSM_GROUPS * SSM_STATE))
    xh = xs.reshape(B, S, SSM_GROUPS, SSM_HEADS_PER_GROUP, SSM_HEAD_DIM)
    Bm = Bm.reshape(B, S, SSM_GROUPS, SSM_STATE)
    Cm = Cm.reshape(B, S, SSM_GROUPS, SSM_STATE)
    dt = jax.nn.softplus(dt_raw.astype(jnp.float32).reshape(B, S, SSM_GROUPS, SSM_HEADS_PER_GROUP)
                         + dt_bias.astype(jnp.float32).reshape(SSM_GROUPS, SSM_HEADS_PER_GROUP))
    A = -jnp.exp(a_log.astype(jnp.float32)).reshape(SSM_GROUPS, SSM_HEADS_PER_GROUP)
    y = ssd_chunked(xh, dt, A, Bm, Cm)
    y = y + d_skip.reshape(SSM_GROUPS, SSM_HEADS_PER_GROUP)[:, :, None] * xh
    y = y.reshape(B, S, SSM_D_INNER).astype(z.dtype)
    yg = (y * jax.nn.silu(z)).reshape(B, S, SSM_GROUPS, SSM_D_INNER // SSM_GROUPS)
    yg = rms_norm(yg, g_ssm_out.reshape(SSM_GROUPS, SSM_D_INNER // SSM_GROUPS))
    return yg.reshape(B, S, SSM_D_INNER)

def setup_inputs(seed: int = 0) -> dict:
    key = jax.random.key(seed)
    ks = jax.random.split(key, 32)
    f32 = jnp.float32

    def nrm(k, shape, scale):
        return jax.random.normal(k, shape, f32) * scale

    def gain(k, shape):
        return 1.0 + 0.05 * jax.random.normal(k, shape, f32)

    Ld = DEPTH
    x = jax.random.normal(ks[0], (BATCH, SEQ, D_MODEL), f32)
    c = jax.random.normal(ks[1], (BATCH, D_MODEL), f32)
    offs = jax.random.randint(ks[2], (BATCH, 1), 0, 2048, dtype=jnp.int32)
    positions = (offs + jnp.arange(SEQ, dtype=jnp.int32)[None, :]).astype(jnp.int32)
    dt0 = jnp.exp(jax.random.uniform(ks[16], (Ld, SSM_HEADS), f32, np.log(1e-3), np.log(1e-1)))
    return {
        "x": x,
        "c": c,
        "positions": positions,
        "w_ada": nrm(ks[3], (Ld, D_MODEL, 6 * D_MODEL), 0.5 * D_MODEL ** -0.5),
        "b_ada": nrm(ks[4], (Ld, 6 * D_MODEL), 0.01),
        "g_pre_mix": gain(ks[5], (Ld, D_MODEL)),
        "g_post_mix": gain(ks[6], (Ld, D_MODEL)),
        "w_in": nrm(ks[7], (Ld, D_MODEL, IN_COLS), D_MODEL ** -0.5),
        "g_q_lat": gain(ks[8], (Ld, Q_LORA_RANK)),
        "g_kv_lat": gain(ks[9], (Ld, KV_LORA_RANK)),
        "w_uq": nrm(ks[10], (Ld, Q_LORA_RANK, MLA_HEADS * (QK_NOPE_DIM + QK_ROPE_DIM)), Q_LORA_RANK ** -0.5),
        "w_ukv": nrm(ks[11], (Ld, KV_LORA_RANK, MLA_HEADS * (QK_NOPE_DIM + V_HEAD_DIM)), KV_LORA_RANK ** -0.5),
        "w_o_attn": nrm(ks[12], (Ld, MLA_HEADS * V_HEAD_DIM, D_MODEL), (MLA_HEADS * V_HEAD_DIM) ** -0.5),
        "conv_w": nrm(ks[13], (Ld, CONV_WIDTH, CONV_CH), CONV_WIDTH ** -0.5),
        "conv_b": nrm(ks[14], (Ld, CONV_CH), 0.01),
        "dt_bias": dt0 + jnp.log(-jnp.expm1(-dt0)),
        "a_log": jnp.log(jax.random.uniform(ks[17], (Ld, SSM_HEADS), f32, 1.0, 16.0)),
        "d_skip": gain(ks[18], (Ld, SSM_HEADS)),
        "g_ssm_out": gain(ks[19], (Ld, SSM_D_INNER)),
        "w_o_ssm": nrm(ks[20], (Ld, SSM_D_INNER, D_MODEL), SSM_D_INNER ** -0.5),
        "w_out": nrm(ks[21], (Ld, D_MODEL, D_MODEL), D_MODEL ** -0.5),
        "g_pre_mlp": gain(ks[22], (Ld, D_MODEL)),
        "g_post_mlp": gain(ks[23], (Ld, D_MODEL)),
        "w_ff1": nrm(ks[24], (Ld, D_MODEL, D_FF), D_MODEL ** -0.5),
        "w_ff2": nrm(ks[25], (Ld, D_FF, D_MODEL), D_FF ** -0.5),
    }

def reference(x, c, positions, w_ada, b_ada, g_pre_mix, g_post_mix, w_in, g_q_lat, g_kv_lat,
              w_uq, w_ukv, w_o_attn, conv_w, conv_b, dt_bias, a_log, d_skip, g_ssm_out,
              w_o_ssm, w_out, g_pre_mlp, g_post_mlp, w_ff1, w_ff2):
    sc = jax.nn.silu(c)
    for l in range(DEPTH):
        mod = sc @ w_ada[l] + b_ada[l]
        shift1, scale1, gate1, shift2, scale2, gate2 = [m[:, None, :] for m in jnp.split(mod, 6, axis=-1)]
        h = rms_norm(x, g_pre_mix[l]) * (1.0 + scale1) + shift1
        q_lat, kv_lat, k_rope, z, xbc, dt_raw, gate_a, gate_b = split_cols(h @ w_in[l], IN_SIZES)
        attn = mla_attention(q_lat, kv_lat, k_rope, positions, g_q_lat[l], g_kv_lat[l], w_uq[l], w_ukv[l]) @ w_o_attn[l]
        ssm = mamba2_mixer(z, xbc, dt_raw, conv_w[l], conv_b[l], dt_bias[l], a_log[l], d_skip[l], g_ssm_out[l]) @ w_o_ssm[l]
        merged = jax.nn.sigmoid(gate_a) * attn + jax.nn.sigmoid(gate_b) * ssm
        x = x + gate1 * rms_norm(merged @ w_out[l], g_post_mix[l])
        h2 = rms_norm(x, g_pre_mlp[l]) * (1.0 + scale2) + shift2
        ff = jnp.square(jax.nn.relu(h2 @ w_ff1[l])) @ w_ff2[l]
        x = x + gate2 * rms_norm(ff, g_post_mlp[l])
    return x


_drawn_inputs = setup_inputs


def setup_inputs(seed=0):
    import zlib

    import numpy as np

    out = dict(_drawn_inputs(seed))
    spreads = {}
    factors = {'b_ada': 3.651,
     'g_post_mix': 3.511,
     'g_q_lat': 8.0,
     'g_kv_lat': 8.0,
     'conv_b': 8.0,
     'd_skip': 24.35,
     'g_ssm_out': 12.615,
     'g_pre_mlp': 3.61,
     'g_post_mlp': 3.835,
     'a_log': 2.68}
    for name, (base, spread) in spreads.items():
        noise = np.random.default_rng([zlib.crc32(name.encode()), seed]).standard_normal(out[name].shape)
        drawn = base * np.exp(spread * noise) if base else spread * noise
        out[name] = __import__('jax').numpy.asarray(drawn.astype(out[name].dtype))
    for name, factor in factors.items():
        out[name] = (out[name] * factor).astype(out[name].dtype)
    return out
```

```python
from contextlib import ExitStack

import numpy as np
import concourse.bass as bass
from concourse import mybir

P = 128
D = 1024
T = 512
TB = T // P
KC = D // P
HEADS = 8
NOPE = 128
ROPE = 64
RANK = 256
THETA = 10000.0
SSM_IN = 2 * D
SH = 32
GROUPS = 8
GH = SH // GROUPS
HD = SSM_IN // SH
GF = GH * HD
XBC = SSM_IN + 2 * GROUPS * P
TAPS = 4
FF = 4 * D
EPS = 1e-6
SCALE = float(NOPE + ROPE) ** -0.5
RAW = 4

COL_Q = 0
COL_KV = RANK
COL_KR = 2 * RANK
COL_Z = COL_KR + ROPE
COL_X = COL_Z + SSM_IN
COL_B = COL_X + SSM_IN
COL_C = COL_B + GROUPS * P
COL_DT = COL_X + XBC
COL_GA = COL_DT + SH
COL_GB = COL_GA + D

VEC = {}
VEC_ROWS = 0
for _name, _n in (("b_ada", 48), ("c", 8), ("g_pre_mix", 8), ("g_post_mix", 8), ("g_q_lat", 2),
                  ("g_kv_lat", 2), ("g_pre_mlp", 8), ("g_post_mlp", 8), ("g_ssm_out", 16)):
    VEC[_name] = (VEC_ROWS, _n)
    VEC_ROWS += _n

CON_IDENT, CON_TRI, CON_STRICT, CON_ONES, CON_MASK = (P * _i for _i in range(5))
CON_FREQ = 5 * P
CON_SIGN = CON_FREQ + 1
CON_COLS = CON_SIGN + 1

F32 = mybir.dt.float32
F32R = mybir.dt.float32r
I32 = mybir.dt.int32
ALU = mybir.AluOpType
ACT = mybir.ActivationFunctionType
AX = mybir.AxisListType

R_ADA, R_LAT, R_ATT, R_OA, R_SSM, R_OS, R_OUT, R_FF = 0, 16, 23, 71, 79, 143, 159, 167
R_END = R_FF + 64
B_LAT, B_ATT, B_OA, B_SSM, B_OS, B_OUT, B_FF = 0, 7, 23, 31, 95, 111, 119
G_LAT, G_ATT, G_OA, G_SSM, G_OS, G_OUT, G_FF = 16, 23, 95, 103, 167, 183, 191
G_PER_R = G_OA - R_OA
J_LAT, J_ATT, J_OA, J_SSM, J_OS, J_OUT, J_FF = 0, 7, 63, 71, 135, 143, 151
J_HALF = 24
SET_TRIG = 16
ROPE_DMAS = 16 * 5
SMALL = 16 * 15
MAGIC = 1.5 * 2.0 ** 23
TWO_PI_1 = 6.28125
TWO_PI_2 = float((np.float32(2 * np.pi - TWO_PI_1).view(np.uint32) & np.uint32(0xFFFFE000))
                 .view(np.float32))
TWO_PI_3 = float(2 * np.pi - TWO_PI_1 - TWO_PI_2)
PI_IN = 3.1415925
RMS_X, RMS_Q, RMS_KV, RMS_G, RMS_MIX, RMS_MLP, RMS_FF = 0, 1, 2, 3, 11, 12, 13


def constants():
    j = np.arange(P)[:, None]
    l = np.arange(P)[None, :]
    con = np.zeros((P, CON_COLS), np.float32)
    con[:, CON_IDENT:CON_IDENT + P] = j == l
    con[:, CON_TRI:CON_TRI + P] = j <= l
    con[:, CON_STRICT:CON_STRICT + P] = j > l
    con[:, CON_ONES:CON_ONES + P] = 1.0
    con[:, CON_MASK:CON_MASK + P] = np.where(l > j, -1e30, 0.0)
    half = ROPE // 2
    freq = np.float32(THETA) ** (-np.arange(half, dtype=np.float32) / np.float32(half))
    con[:, CON_FREQ] = np.tile(freq.astype(np.float32), P // half)
    con[:, CON_SIGN] = np.where(np.arange(P) % ROPE < half, -1.0, 1.0)
    return con


def at(tensor, i):
    if isinstance(i, int):
        return tensor[:, i, :]
    return tensor[:, bass.ds(i, 1), :].rearrange("p a n -> p (a n)")


def cols(tensor, i, n):
    if isinstance(i, int):
        return tensor[:, i:i + n]
    return tensor[:, bass.ds(i, n)]


def wait(eng, semaphore, value):
    if not (isinstance(value, int) and value <= 0):
        eng.wait_ge(semaphore, value)


def last_peeled(eng, count, body):
    with eng.Fori(0, count - 1) as i:
        body(i, False)
    body(count - 1, True)


def build(nc, a):
    with ExitStack() as ctx:
        Program(nc, a, ctx)


def Program(nc, a, ctx):
    def sb(name, shape, dt=F32, stack=ctx):
        return stack.enter_context(nc.sbuf_tensor(name, shape, dt))

    def sem(name):
        return ctx.enter_context(nc.semaphore(name))

    raw = sb("raw", [P, RAW, KC * P])
    whi = sb("whi", [P, 2, KC * P], F32R)
    wlo = sb("wlo", [P, 2, KC * P], F32R)
    ahi = sb("ahi", [P, KC, T], F32R)
    alo = sb("alo", [P, KC, T], F32R)
    fhi = sb("fhi", [P, 2 * KC, T], F32R)
    flo = sb("flo", [P, 2 * KC, T], F32R)
    buf1 = sb("buf1", [P, KC, T])
    buf2 = sb("buf2", [P, KC, T])
    sq = sb("sq", [P, 2, T])
    tt = sb("tt", [P, 2, T])
    uu = sb("uu", [P, 2, T])
    diag = sb("diag", [P, T])

    con = sb("con", [P, CON_COLS])
    strict_r = sb("strict_r", [P, P], F32R)
    vec = sb("vec", [P, VEC_ROWS])
    convb = sb("convb", [P, XBC // P])
    convw = sb("convw", [P, TAPS * XBC // P])
    silu_c = sb("silu_c", [P, KC])
    mod = sb("mod", [P, 48])
    g_mix = sb("g_mix", [P, KC])
    g_mlp = sb("g_mlp", [P, KC])
    gp_mix = sb("gp_mix", [P, KC])
    gp_mlp = sb("gp_mlp", [P, KC])
    minus_half = sb("minus_half", [P, TB])
    ms = sb("ms", [P, TB])
    rstd = sb("rstd", [P, TB])
    rowmax = sb("rowmax", [P, 2 * TB])
    negmax = sb("negmax", [P, 2 * TB])
    rowsum = sb("rowsum", [P, 2 * TB])
    rowinv = sb("rowinv", [P, 2 * TB])
    dt_bias = sb("dt_bias", [P, SH])
    a_log = sb("a_log", [P, SH])
    d_half = sb("d_half", [P, SH])
    dt_half = sb("dt_half", [P, TB * SH])
    dta = sb("dta", [P, TB * SH])
    dta_hi = sb("dta_hi", [P, TB * SH], F32R)
    dta_lo = sb("dta_lo", [P, TB * SH])
    dt_end = sb("dt_end", [P, TB * SH])
    decay = sb("decay", [P, 3, TB * SH])
    ident = con[:, CON_IDENT:CON_IDENT + P]
    tri = con[:, CON_TRI:CON_TRI + P]
    strict = con[:, CON_STRICT:CON_STRICT + P]
    ones = con[:, CON_ONES:CON_ONES + P]
    mask = con[:, CON_MASK:CON_MASK + P]

    with ExitStack() as att:
        lathi = sb("lathi", [P, 4, T], F32R, att)
        latlo = sb("latlo", [P, 4, T], F32R, att)
        pthi = sb("pthi", [P, 2, T], F32R, att)
        ptlo = sb("ptlo", [P, 2, T], F32R, att)
    ssm = ctx.enter_context(ExitStack())
    c_t = sb("c_t", [P, T], F32, ssm)
    b_t = sb("b_t", [P, T], F32, ssm)
    b_tok = sb("b_tok", [P, T], F32, ssm)
    x_tok = sb("x_tok", [P, TB, GF], F32, ssm)
    zs = sb("zs", [P, 2, T], F32, ssm)
    cbm = sb("cbm", [P, P], F32, ssm)
    rm_hi = sb("rm_hi", [P, GH * P], F32R, ssm)
    rm_lo = sb("rm_lo", [P, GH * P], F32R, ssm)
    xdt = sb("xdt", [P, GF], F32, ssm)
    xend = sb("xend", [P, GF], F32, ssm)
    xd = sb("xd", [P, GF], F32, ssm)
    state = sb("state", [P, GF], F32, ssm)
    y = sb("y", [P, GF], F32, ssm)
    ssum = c_t[:, :]

    x_tok_all = buf1[:, :, :].rearrange("p (a k) n -> p a (k n)", a=TB)
    xt = buf2
    lat = buf2[:, 0:4, :]
    cos, sin, rope1, rope2 = (buf2[:, i, :] for i in range(4, 8))
    probs = buf1[:, :, :].rearrange("p (a b) n -> p a b n", a=2)
    qn_hi, kn_hi, v_hi = fhi[:, 8:10, :], fhi[:, 10:12, :], fhi[:, 12:14, :]
    qn_lo, kn_lo, v_lo = flo[:, 8:10, :], flo[:, 10:12, :], flo[:, 12:14, :]
    q_rope = fhi[:, 14:16, :]
    kr_hi, kr_lo = flo[:, 14, :], flo[:, 15, :]
    dtx = tt[:, 0, 0:TB * SH]
    dtneg = tt[:, 1, 0:TB * SH]
    pos_i = buf2[:, 6, :].bitcast(I32)
    ost = [sq[:, 0, :], sq[:, 1, :], uu[:, 0, :], uu[:, 1, :]]
    vec_rows = uu[0:VEC_ROWS, 0, 0:P]
    convb_rows = uu[0:XBC // P, 0, P:2 * P]
    convw_rows = uu[:, 0, 2 * P:3 * P]

    bank = [ctx.enter_context(nc.psum_tensor(f"bank{i}", [P, T], F32)) for i in range(8)]
    G = bank[6:8]

    small_in = sem("small_in")
    x_in = sem("x_in")
    raw_in = [sem(f"raw_in{i}") for i in range(RAW)]
    rope_in = [sem(f"rope_in{i}") for i in range(2)]
    krope_in = sem("krope_in")
    pos_in = sem("pos_in")
    stash = sem("stash")
    xt_in = sem("xt_in")
    out_sent = [sem(f"out_sent{i}") for i in range(4)]
    w_hi = sem("w_hi")
    w_lo = sem("w_lo")
    gemm_done = sem("gemm_done")
    g_free = [sem(f"g_free{i}") for i in range(2)]
    vec_t = sem("vec_t")
    vec_c = sem("vec_c")
    silu_done = sem("silu_done")
    setup = sem("setup")
    pool_setup = sem("pool_setup")
    trig = sem("trig")
    xt_full = sem("xt_full")
    xt_copied = sem("xt_copied")
    sq_full = sem("sq_full")
    sq_zero = sem("sq_zero")
    sq_added = sem("sq_added")
    ssq_done = sem("ssq_done")
    ms_done = sem("ms_done")
    rstd_done = sem("rstd_done")
    diag_done = sem("diag_done")
    rep_done = sem("rep_done")
    nm_t, nm_u, nm_h, nm_l = (sem(n) for n in ("nm_t", "nm_u", "nm_h", "nm_l"))
    lat_sq = sem("lat_sq")
    lat_u, lat_h, lat_l = (sem(n) for n in ("lat_u", "lat_h", "lat_l"))
    kr_v = sem("kr_v")
    kr_h = sem("kr_h")
    dt_v, dt_a = sem("dt_v"), sem("dt_a")
    dt_mm = sem("dt_mm")
    proj_h = sem("proj_h")
    proj_l = sem("proj_l")
    rot = sem("rot")
    s_full = sem("s_full")
    s_masked = sem("s_masked")
    s_max = sem("s_max")
    s_neg = sem("s_neg")
    s_exp = sem("s_exp")
    s_inv = sem("s_inv")
    p_norm = sem("p_norm")
    pt_full = sem("pt_full")
    pt_h = sem("pt_h")
    pt_l = sem("pt_l")
    pv_done = sem("pv_done")
    o_h = sem("o_h")
    mod_done = sem("mod_done")
    cv_acc = sem("cv_acc")
    cv_tap = sem("cv_tap")
    cv_tanh = sem("cv_tanh")
    cv_out = sem("cv_out")
    tin_done = sem("tin_done")
    tin_copied = sem("tin_copied")
    z_tanh = sem("z_tanh")
    z_out = sem("z_out")
    ga_tanh = sem("ga_tanh")
    ga_out = sem("ga_out")
    rm_done = sem("rm_done")
    cb_done = sem("cb_done")
    seg_done = sem("seg_done")
    cbm_done = sem("cbm_done")
    e_done = sem("e_done")
    m_done = sem("m_done")
    xd_done = sem("xd_done")
    yd_done = sem("yd_done")
    s_done = sem("s_done")
    h_scaled = sem("h_scaled")
    h_done = sem("h_done")
    y_part = sem("y_part")
    y_done = sem("y_done")
    yt_done = sem("yt_done")
    gt_done = sem("gt_done")
    gsq_done = sem("gsq_done")
    yg_u, yg_h = sem("yg_u"), sem("yg_h")
    yg_l = sem("yg_l")
    mg_t, mg_u, mg_h = sem("mg_t"), sem("mg_u"), sem("mg_h")
    mg_l = sem("mg_l")
    mix_out = sem("mix_out")
    x1_t, x1_done = sem("x1_t"), sem("x1_done")
    ff_r = sem("ff_r")
    ff_q = sem("ff_q")
    ff_h = sem("ff_h")
    ff_l = sem("ff_l")
    ff_half = sem("ff_half")
    ff_sum = sem("ff_sum")
    fin_t, fin_done = sem("fin_t"), sem("fin_done")
    fin_tr = sem("fin_tr")
    fin_copy = sem("fin_copy")

    xt_dram = nc.dram_tensor("xt_stash", (P, KC * T), F32, kind="Internal").ap()

    w_k = {n: a[n].rearrange("l (k p) n -> p (l k) n", p=P)
           for n in ("w_ada", "w_in", "w_uq", "w_ukv", "w_o_attn", "w_o_ssm", "w_out", "w_ff1", "w_ff2")}
    block = ctx.enter_context(nc.Block())

    def unit_dst(r, kc, n):
        return raw[:, r % RAW, 0:kc * n].rearrange("p (k n) -> p k n", k=kc)

    def loads_of(sp, phase, i, u):
        first = {"ada": R_ADA, "lat": R_LAT, "att": R_ATT, "oa": R_OA, "ssm": R_SSM, "os": R_OS,
                 "out": R_OUT}
        r = (R_FF + 16 * phase[1] if isinstance(phase, tuple) else first[phase]) + u
        slot, landed = r % RAW, raw_in[r % RAW]

        def whole(name, row, col):
            sp.dma_start(unit_dst(r, KC, P),
                         w_k[name][:, row:row + KC, bass.ds(col, P)]).then_inc(landed, 16)

        if phase == "ada":
            whole("w_ada", 0, u * P)
        elif phase == "lat":
            if u < 4:
                whole("w_in", 0, u * P)
            elif u < 6:
                dst = raw[:, slot, :].rearrange("p (k d n) -> p k d n", k=KC, d=2)
                src = w_k["w_in"][:, :, COL_KR:COL_KR + ROPE]
                halves = [(0, 0)] if u == 4 else [(0, 32), (32, 0)]
                width = ROPE if u == 4 else ROPE // 2
                n = 0
                for to, of in halves:
                    for d in range(2):
                        sp.dma_start(dst[:, :, d, to:to + width], src[:, :, of:of + width])\
                          .then_inc(landed if n == 0 else krope_in, 16)
                        n += 1
            else:
                sp.dma_start(unit_dst(r, KC, P)[:, :, 0:SH],
                             w_k["w_in"][:, :, COL_DT:COL_DT + SH]).then_inc(landed, 16)
        elif phase == "att":
            if u in (0, 2):
                h = 2 * i + u // 2
                extra = rope_in[u // 2]
                dst = unit_dst(r, 2, 3 * P)
                col = h * (NOPE + ROPE)
                sp.dma_start(dst[:, :, 0:NOPE + ROPE],
                             w_k["w_uq"][:, :, bass.ds(col, NOPE + ROPE)]).then_inc(landed, 16)
                sp.dma_start(dst[:, :, NOPE + ROPE:2 * P],
                             w_k["w_uq"][:, :, bass.ds(col + NOPE, ROPE)]).then_inc(extra, 16)
                for to, of in ((0, 32), (32, 0), (64, 32), (96, 0)):
                    sp.dma_start(dst[:, :, 2 * P + to:2 * P + to + 32],
                                 w_k["w_uq"][:, :, bass.ds(col + NOPE + of, 32)]).then_inc(extra, 16)
            elif u in (1, 3):
                h = 2 * i + u // 2
                sp.dma_start(unit_dst(r, 2, 2 * P),
                             w_k["w_ukv"][:, :, bass.ds(h * 2 * P, 2 * P)]).then_inc(landed, 16)
            else:
                whole("w_ada", 0, (16 + 8 * i + (u - 4)) * P)
        elif phase == "oa":
            whole("w_o_attn", 0, (4 * i + u) * P)
        elif phase == "ssm":
            col = (COL_C + i * P, COL_B + i * P, COL_X + i * GF, COL_X + i * GF + P,
                   COL_Z + i * GF, COL_Z + i * GF + P, COL_GA + i * P, COL_GB + i * P)[u]
            whole("w_in", 0, col)
        elif phase == "os":
            whole("w_o_ssm", KC * (u % 2), (2 * i + u // 2) * P)
        elif phase == "out":
            whole("w_out", 0, (4 * i + u) * P)
        else:
            _, part = phase
            if part % 2 == 0:
                whole("w_ff1", 0, (16 * (part // 2) + 4 * i + u) * P)
            else:
                whole("w_ff2", 2 * KC * (part // 2) + KC * (u % 2), (2 * i + u // 2) * P)

    ATT_STEPS = (3, 5, 8, 10) + tuple(range(11, 19))
    STREAM = [("ada", 1, 16), ("lat", 1, 7), ("att", 4, 12), ("oa", 2, 4), ("ssm", 8, 8), ("os", 4, 4),
              ("out", 2, 4)] + [(("ff", part), 4, 4) for part in range(4)]

    def used_up(phase, i, u):
        if phase in ("ada", "lat"):
            return (R_ADA if phase == "ada" else R_LAT) + u + 1
        if phase == "att":
            return G_ATT + 18 * i + ATT_STEPS[u]
        first = {"oa": G_OA, "ssm": G_SSM, "os": G_OS, "out": G_OUT}
        g = G_FF + 16 * phase[1] if isinstance(phase, tuple) else first[phase]
        return g + (8 if phase == "ssm" else 4) * i + u + 1

    @block.sync
    def _(sp):
        sp.dma_start(x_tok_all, a["x"][0].rearrange("(b p) n -> p b n", p=P)).then_inc(x_in, 16)
        for u in range(RAW):
            loads_of(sp, "ada", 0, u)
        for n, (phase, count, units) in enumerate(STREAM):
            following = STREAM[n + 1] if n + 1 < len(STREAM) else None

            def ahead(i, last, phase=phase, units=units, following=following):
                for u in range(units):
                    if u + RAW < units:
                        to = (phase, i, u + RAW)
                    elif not last:
                        to = (phase, i + 1, u + RAW - units)
                    elif following:
                        to = (following[0], 0, u + RAW - units)
                    else:
                        continue
                    sp.wait_ge(gemm_done, used_up(phase, i, u))
                    loads_of(sp, *to)

            if count == 1:
                ahead(0, True)
            else:
                last_peeled(sp, count, ahead)
        for c in range(KC):
            sp.wait_ge(fin_copy, c + 1)
            sp.dma_start(a["out"][0, :, c * P:(c + 1) * P].rearrange("(b p) n -> p b n", p=P),
                         ost[c % 4].rearrange("p (b n) -> p b n", b=TB)).then_inc(out_sent[c % 4], 16)
        for k in range(4):
            sp.wait_ge(out_sent[k], 16 * (KC // 4))

    class Unit:

        def __init__(self, r0, b0, i, r_per, b_per, ru, bu):
            assert r_per % RAW == 0 and b_per % 2 == 0
            self.slot = (r0 + ru) % RAW
            self.landed = 16 * (i * (r_per // RAW) + (r0 + ru) // RAW + 1)
            self.par = (b0 + bu) % 2
            self.b = b0 + bu + i * b_per

    def hi_of(act, unit):
        act.wait_ge(raw_in[unit.slot], unit.landed)
        act.activation(whi[:, unit.par, :], raw[:, unit.slot, :], ACT.Copy).then_inc(w_hi, 1)

    def lo_of(dve, unit):
        dve.wait_ge(w_hi, unit.b + 1)
        dve.tensor_tensor(wlo[:, unit.par, :], raw[:, unit.slot, :], whi[:, unit.par, :].bitcast(F32),
                          ALU.subtract).then_inc(w_lo, 1)

    def u_lat(bu):
        return Unit(R_LAT, B_LAT, 0, 4, 2, bu, bu)

    def u_att(i, bu):
        ru = bu if bu < 4 else 12 + bu - 4
        return Unit(R_ATT, B_ATT, i, 12, 4, ru, bu)

    def u_run(r0, b0, per, i, bu):
        return Unit(r0, b0, i, per, per, bu, bu)

    def conv_chunk(i, k):
        return (SSM_IN // P + GROUPS + i, SSM_IN // P + i, 2 * i, 2 * i + 1)[k]

    def conv_dst(k):
        return (c_t[:, :], b_t[:, :], uu[:, 0, :], uu[:, 1, :])[k]

    def product(pe, out, pairs, first=True, last=True):
        n = 3 * len(pairs)
        k = 0
        for sh, sl, mh, ml in pairs:
            for s, m in ((sh, mh), (sh, ml), (sl, mh)):
                ins = pe.matmul(out, s, m, start=first and k == 0, stop=last and k == n - 1)
                k += 1
        return ins

    def weights(par, k, n=P):
        return whi[:, par, k * P:k * P + n], wlo[:, par, k * P:k * P + n]

    def gemm(pe, job, b, par, moving, first=True, last=True):
        pe.wait_ge(w_lo, b + 1)
        if first:
            free_job(pe, job)
        pairs = [weights(par, k) + (moving[0][:, k, :], moving[1][:, k, :]) for k in range(KC)]
        product(pe, G[job_bank(job)][:, :], pairs, first, last).then_inc(gemm_done, 1)

    class Job:

        def __init__(self, j0, i, per, k):
            assert per % 2 == 0
            self.bank = (j0 + k) % 2
            self.before = i * (per // 2) + (j0 + k) // 2

    def job_bank(job):
        return job.bank

    def free_job(pe, job):
        wait(pe, g_free[job.bank], job.before)

    def g_of(job):
        return G[job.bank]

    def rms_pe(pe, r, rbank, sources, waits):
        for w in waits:
            pe.wait_ge(*w)
        for n, s in enumerate(sources):
            for tb in range(TB):
                ins = pe.matmul(rbank[:, tb:tb + 1], s[:, tb * P:(tb + 1) * P], ones[:, 0:1],
                                start=(n == 0 and tb == 0), stop=(n == len(sources) - 1),
                                skip_group_check=True)
        ins.then_inc(ssq_done, 1)

    def rms_rep(pe, r, rbank):
        pe.wait_ge(diag_done, 4 * r + 4)
        pe.matmul(rbank[:, :], ones, diag[:, :], start=True, stop=True).then_inc(rep_done, 1)

    def rms_dve(dve, r, rbank, n):
        dve.wait_ge(ssq_done, r + 1)
        dve.tensor_scalar(ms[:, :], rbank[:, 0:TB], 1.0 / n, EPS, ALU.mult, ALU.add).then_inc(ms_done, 1)
        wait(dve, rep_done, r)
        dve.wait_ge(rstd_done, r + 1)
        for tb in range(TB):
            dve.tensor_scalar(diag[:, tb * P:(tb + 1) * P], ident, rstd[:, tb:tb + 1], None, ALU.mult)\
               .then_inc(diag_done, 1)

    def rms_pool(pool, r):
        pool.wait_ge(ms_done, r + 1)
        pool.tensor_tensor(rstd[:, :], ms[:, :], minus_half[:, :], ALU.pow).then_inc(rstd_done, 1)

    def square_into(act, q, par, source):
        wait(act, sq_added, q - 1)
        act.activation(sq[:, par, :], source, ACT.Square).then_inc(sq_full, 1)

    def clear_sum(pool, n):
        wait(pool, ssq_done, n)
        pool.memset(ssum, 0.0).then_inc(sq_zero, 1)

    def add_square(pool, q, par, cleared=0):
        wait(pool, sq_zero, cleared)
        wait(pool, sq_added, q)
        pool.wait_ge(sq_full, q + 1)
        pool.tensor_tensor(ssum, ssum, sq[:, par, :], ALU.add).then_inc(sq_added, 1)

    def modulate_dve(dve, m, source, rbank):
        for c in range(KC):
            n = m * KC + c
            wait(dve, nm_u, n - 1)
            dve.tensor_tensor(tt[:, c % 2, :], source[:, c, :], rbank[:, :], ALU.mult).then_inc(nm_t, 1)
            if c:
                lo_mod(dve, n - 1, c - 1)
        lo_mod(dve, m * KC + KC - 1, KC - 1)

    def lo_mod(dve, n, c):
        dve.wait_ge(nm_h, n + 1)
        dve.tensor_tensor(alo[:, c, :], uu[:, c % 2, :], ahi[:, c, :].bitcast(F32), ALU.subtract)\
           .then_inc(nm_l, 1)

    def modulate_act(act, m, gain, shift):
        for c in range(KC):
            n = m * KC + c
            act.wait_ge(nm_t, n + 1)
            wait(act, nm_l, n - 1)
            act.activation(uu[:, c % 2, :], tt[:, c % 2, :], ACT.Identity, scale=gain[:, c:c + 1],
                           bias=mod[:, shift + c:shift + c + 1]).then_inc(nm_u, 1)
            act.wait_ge(nm_u, n + 1)
            act.activation(ahi[:, c, :], uu[:, c % 2, :], ACT.Copy).then_inc(nm_h, 1)

    @block.tensor
    def _(pe):
        pe.wait_ge(small_in, SMALL)
        pe.transpose(bank[7][:, 0:VEC_ROWS], vec_rows, ident[0:VEC_ROWS, 0:VEC_ROWS])
        pe.transpose(bank[7][:, P:P + XBC // P], convb_rows, ident[0:XBC // P, 0:XBC // P])
        pe.transpose(bank[7][:, 2 * P:3 * P], convw_rows, ident).then_inc(vec_t, 1)
        pe.wait_ge(x_in, 16)
        for c in range(KC):
            wait(pe, sq_full, c - 3)
            for tb in range(TB):
                ins = pe.transpose(bank[1 + c % 4][:, tb * P:(tb + 1) * P],
                                   x_tok_all[:, tb, c * P:(c + 1) * P], ident)
            ins.then_inc(xt_full, 1)
        pe.wait_ge(silu_done, 1)
        for u in range(16):
            pe.wait_ge(raw_in[u % RAW], 16 * (u // RAW + 1))
            for k in range(KC):
                ins = pe.matmul(bank[5][:, u:u + 1], raw[:, u % RAW, k * P:(k + 1) * P],
                                silu_c[:, k:k + 1], start=(k == 0), stop=(k == KC - 1))
            ins.then_inc(gemm_done, 1)
        rms_pe(pe, RMS_X, bank[0], [ssum], [(sq_added, KC)])
        rms_rep(pe, RMS_X, bank[0])

        h_act = (ahi, alo)
        pe.wait_ge(nm_l, KC)
        for k in range(4):
            gemm(pe, Job(J_LAT, 0, 2, k), B_LAT + k, k % 2, h_act)
        gemm(pe, Job(J_LAT, 0, 2, 4), B_LAT + 4, 0, h_act)
        rms_pe(pe, RMS_Q, bank[0], [sq[:, 0, :], sq[:, 1, :]], [(lat_sq, 2)])
        gemm(pe, Job(J_LAT, 0, 2, 5), B_LAT + 5, 1, h_act)
        rms_rep(pe, RMS_Q, bank[0])
        rms_pe(pe, RMS_KV, bank[1], [tt[:, 0, :], tt[:, 1, :]], [(lat_sq, 4)])
        pe.wait_ge(w_lo, B_LAT + 7)
        job = Job(J_LAT, 0, 2, 6)
        free_job(pe, job)
        for tb in range(TB):
            pairs = [(ahi[:, k, tb * P:(tb + 1) * P], alo[:, k, tb * P:(tb + 1) * P]) + weights(0, k, SH)
                     for k in range(KC)]
            ins = product(pe, g_of(job)[:, tb * SH:(tb + 1) * SH], pairs)
        ins.then_inc(gemm_done, 1)
        rms_rep(pe, RMS_KV, bank[1])
        pe.wait_ge(dt_v, 3)
        for n, left in enumerate((tri, strict, ones)):
            for ch in range(TB):
                ins = pe.matmul(bank[2][:, n * P + ch * SH:n * P + (ch + 1) * SH], left,
                                dta[:, ch * SH:(ch + 1) * SH], start=True, stop=True)
        ins.then_inc(dt_mm, 1)

        pe.wait_ge(lat_l, 4)
        pe.wait_ge(kr_v, 2)
        pe.sem_inc(pv_done, 2)

        def att(i, last):
            jobs = [Job(J_ATT, i, 14, k) for k in range(14)]

            def project(e):
                j = jobs[5 * e:5 * e + 5]
                b = B_ATT + 4 * i + 2 * e
                pq, pk = (B_ATT + 2 * e) % 2, (B_ATT + 2 * e + 1) % 2
                pe.wait_ge(w_lo, b + 1)
                for k in range(3):
                    free_job(pe, j[k])
                    pairs = [(whi[:, pq, c * 3 * P + k * P:c * 3 * P + (k + 1) * P],
                              wlo[:, pq, c * 3 * P + k * P:c * 3 * P + (k + 1) * P],
                              lathi[:, c, :], latlo[:, c, :]) for c in range(2)]
                    product(pe, g_of(j[k])[:, :], pairs).then_inc(gemm_done, 1)
                pe.wait_ge(w_lo, b + 2)
                free_job(pe, j[3])
                pairs = [(whi[:, pk, c * 2 * P:c * 2 * P + P], wlo[:, pk, c * 2 * P:c * 2 * P + P],
                          lathi[:, 2 + c, :], latlo[:, 2 + c, :]) for c in range(2)]
                product(pe, g_of(j[3])[:, :], pairs).then_inc(gemm_done, 1)
                free_job(pe, j[4])
                for tb in range(TB):
                    pairs = [(lathi[:, 2 + c, tb * P:(tb + 1) * P], latlo[:, 2 + c, tb * P:(tb + 1) * P],
                              whi[:, pk, c * 2 * P + P:(c + 1) * 2 * P],
                              wlo[:, pk, c * 2 * P + P:(c + 1) * 2 * P]) for c in range(2)]
                    ins = product(pe, g_of(j[4])[:, tb * P:(tb + 1) * P], pairs)
                ins.then_inc(gemm_done, 1)

            def scores(e):
                h = 2 * i + e
                pe.wait_ge(proj_l, h + 1)
                for k in (2, 3):
                    pe.wait_ge(g_free[jobs[5 * e + k].bank], jobs[5 * e + k].before + 1)
                for qb in range(TB):
                    n = (qb + 1) * P
                    pe.wait_ge(s_exp, 4 * h + qb + 1)
                    out = bank[qb][:, 0:n]
                    blk = slice(qb * P, n)
                    product(pe, out, [(qn_hi[:, e, blk], qn_lo[:, e, blk], kn_hi[:, e, 0:n],
                                       kn_lo[:, e, 0:n])], last=False)
                    pe.matmul(out, q_rope[:, e, blk], kr_hi[:, 0:n], start=False, stop=False)
                    pe.matmul(out, q_rope[:, e, blk], kr_lo[:, 0:n], start=False, stop=True)\
                      .then_inc(s_full, 1)

            def attend(e):
                h = 2 * i + e
                job = jobs[10 if e == 0 else 13]

                def turn(j):
                    t = 4 * h + j
                    pe.wait_ge(pt_l, t + 1)
                    for qb in range(j, TB):
                        ins = pe.transpose(bank[4 + j % 2][:, qb * P:(qb + 1) * P],
                                           probs[:, e, qb, j * P:(j + 1) * P], ident)
                    ins.then_inc(pt_full, 1)

                def values(j):
                    t = 4 * h + j
                    pe.wait_ge(pt_l, t + 3)
                    if j == 0:
                        free_job(pe, job)
                    kb = slice(j * P, (j + 1) * P)
                    product(pe, g_of(job)[:, j * P:T],
                            [(v_hi[:, e, kb], v_lo[:, e, kb], pthi[:, j % 2, j * P:T],
                              ptlo[:, j % 2, j * P:T])], first=(j == 0), last=(j == TB - 1))\
                        .then_inc(pv_done, 1)

                pe.wait_ge(p_norm, 4 * h + 4)
                turn(0)
                turn(1)
                values(0)
                turn(2)
                values(1)
                turn(3)
                values(2)
                values(3)

            def ada(k):
                job = jobs[11 + k]
                free_job(pe, job)
                for n in range(4):
                    unit = Unit(R_ATT, 0, i, 12, 4, 4 + 4 * k + n, 0)
                    pe.wait_ge(raw_in[unit.slot], unit.landed)
                    for c in range(KC):
                        ins = pe.matmul(g_of(job)[:, n:n + 1], raw[:, unit.slot, c * P:(c + 1) * P],
                                        silu_c[:, c:c + 1], start=(c == 0), stop=(c == KC - 1))
                    ins.then_inc(gemm_done, 1)

            project(0)
            scores(0)
            project(1)
            scores(1)
            attend(0)
            ada(0)
            ada(1)
            attend(1)

        last_peeled(pe, HEADS // 2, att)

        final = Job(J_ATT, 3, 14, 13)
        pe.wait_ge(g_free[final.bank], final.before + 1)

        def oa(i, last):
            for k in range(4):
                gemm(pe, Job(J_OA, i, 4, k), B_OA + 4 * i + k, (B_OA + k) % 2,
                     (fhi[:, 0:KC, :], flo[:, 0:KC, :]))

        last_peeled(pe, 2, oa)

        pe.sem_inc(seg_done, 1)
        pe.sem_inc(yd_done, 2)
        pe.sem_inc(yt_done, 1)

        def group(i, last):
            def blk(k):
                gemm(pe, Job(J_SSM, i, 8, k), B_SSM + 8 * i + k, (B_SSM + k) % 2, h_act)

            def turn_in(n, source, to, conv):
                pe.wait_ge(cv_out, 2 + 4 * i + conv + 1)
                for ch in range(TB):
                    ins = pe.transpose(to[:, ch * P:(ch + 1) * P], source[:, ch * P:(ch + 1) * P], ident)
                ins.then_inc(tin_done, 1)

            def decays(ch):
                n = 4 * i + ch
                blk_ = slice(ch * P, (ch + 1) * P)
                pe.wait_ge(cbm_done, n + 1)
                if ch == 0:
                    pe.wait_ge(yg_l, 2 * i + 1)
                pe.matmul(bank[1][:, 0:P], b_t[:, blk_], c_t[:, blk_], start=True, stop=True)\
                  .then_inc(cb_done, 1)
                pe.wait_ge(rm_done, n + 1)
                pe.wait_ge(e_done, n + 1)
                pe.matmul(bank[0][:, :], strict_r[:, :], rm_hi[:, :], start=True, stop=False)
                pe.matmul(bank[0][:, :], strict_r[:, :], rm_lo[:, :], start=False, stop=True)\
                  .then_inc(seg_done, 1)

            def outputs(ch):
                n = 4 * i + ch
                pe.wait_ge(y_done, n + 1)
                if ch:
                    pe.wait_ge(h_done, 3 * i + ch + 1)
                    pe.matmul(bank[2][:, 0:GF], c_t[:, ch * P:(ch + 1) * P], state[:, :],
                              start=True, stop=True)
                pe.wait_ge(m_done, n + 2)
                pe.wait_ge(xd_done, n + 1)
                for h in range(GH):
                    ins = pe.matmul(bank[2][:, GF + h * HD:GF + (h + 1) * HD],
                                    sq[:, ch % 2, h * P:(h + 1) * P], xdt[:, h * HD:(h + 1) * HD],
                                    start=True, stop=True)
                ins.then_inc(yd_done, 1)
                if ch < TB - 1:
                    pe.wait_ge(h_done, 3 * i + ch + 1)
                    pe.matmul(bank[3][:, 0:GF], b_tok[:, ch * P:(ch + 1) * P], xend[:, :],
                              start=True, stop=True).then_inc(s_done, 1)

            def turn_y(ch):
                pe.wait_ge(y_done, 4 * i + ch + 2)
                if ch == 0:
                    pe.wait_ge(tin_copied, 3 * i + 3)
                for f in range(2):
                    ins = pe.transpose(bank[4 + f][:, ch * P:(ch + 1) * P], y[:, f * P:(f + 1) * P], ident)
                ins.then_inc(yt_done, 1)

            blk(0)
            blk(1)
            blk(2)
            pe.wait_ge(gt_done, 2 * i + 1)
            turn_in(0, b_t, bank[4], 1)
            blk(3)
            turn_in(1, uu[:, 0, :], bank[5], 2)
            decays(0)
            blk(4)
            pe.wait_ge(tin_copied, 3 * i + 1)
            turn_in(2, uu[:, 1, :], bank[4], 3)
            decays(1)
            blk(5)
            pe.wait_ge(tin_copied, 3 * i + 3)
            outputs(0)
            decays(2)
            blk(6)
            turn_y(0)
            outputs(1)
            decays(3)
            blk(7)
            turn_y(1)
            outputs(2)
            turn_y(2)
            outputs(3)
            turn_y(3)
            rms_pe(pe, None, bank[1], [sq[:, 0, :], sq[:, 1, :]], [(gsq_done, 2 * i + 2)])
            rms_rep(pe, RMS_G + i, bank[1])

        last_peeled(pe, GROUPS, group)

        pe.wait_ge(yg_l, 1 + 2 * GROUPS)

        def os_(i, last):
            for c in range(2):
                job = Job(J_OS, i, 2, c)
                for half in range(2):
                    k = 2 * c + half
                    gemm(pe, job, B_OS + 4 * i + k, (B_OS + k) % 2,
                         (fhi[:, KC * half:KC * (half + 1), :], flo[:, KC * half:KC * (half + 1), :]),
                         first=(half == 0), last=(half == 1))

        last_peeled(pe, 4, os_)

        pe.wait_ge(mg_l, 1 + KC)

        def out_(i, last):
            for k in range(4):
                gemm(pe, Job(J_OUT, i, 4, k), B_OUT + 4 * i + k, (B_OUT + k) % 2, h_act)

        last_peeled(pe, 2, out_)
        rms_pe(pe, RMS_MIX, bank[0], [ssum], [(sq_added, 2 * KC)])
        rms_rep(pe, RMS_MIX, bank[0])
        rms_pe(pe, RMS_MLP, bank[1], [ssum], [(sq_added, 3 * KC)])
        rms_rep(pe, RMS_MLP, bank[1])

        pe.wait_ge(nm_l, 2 * KC)
        for half in range(2):
            b0 = B_FF + 32 * half
            j0 = J_FF + J_HALF * half

            def up(i, last, b0=b0, j0=j0):
                for k in range(4):
                    gemm(pe, Job(j0, i, 4, k), b0 + 4 * i + k, (b0 + k) % 2, h_act)

            last_peeled(pe, 4, up)
            pe.wait_ge(ff_l, 1 + 16 * (half + 1))

            def down(i, last, b0=b0 + 16, j0=j0 + 16):
                for c in range(2):
                    job = Job(j0, i, 2, c)
                    for part in range(2):
                        k = 2 * c + part
                        gemm(pe, job, b0 + 4 * i + k, (b0 + k) % 2,
                             (fhi[:, KC * part:KC * (part + 1), :], flo[:, KC * part:KC * (part + 1), :]),
                             first=(part == 0), last=(part == 1))

            last_peeled(pe, 4, down)
        rms_pe(pe, RMS_FF, bank[0], [ssum], [(sq_added, 4 * KC)])
        rms_rep(pe, RMS_FF, bank[0])
        for c in range(KC):
            pe.wait_ge(fin_done, c + 1)
            wait(pe, fin_copy, c - 1)
            for tb in range(TB):
                ins = pe.transpose(bank[2 + c % 2][:, tb * P:(tb + 1) * P],
                                   buf2[:, c, tb * P:(tb + 1) * P], ident)
            ins.then_inc(fin_tr, 1)


    @block.scalar
    def _(act):
        act.sem_inc(s_exp, 4)
        act.sem_inc(e_done, 1)
        act.dma_start(con[:, :], a["con"]).then_inc(small_in, 16)
        for name, (row, rows) in VEC.items():
            act.dma_start(uu[row:row + rows, 0, 0:P], a[name].rearrange("l (r n) -> (l r) n", n=P))\
               .then_inc(small_in, 16)
        act.dma_start(convb_rows, a["conv_b"].rearrange("l (r n) -> (l r) n", n=P)).then_inc(small_in, 16)
        act.dma_start(convw_rows, a["conv_w"].rearrange("l k (r n) -> (l k r) n", n=P))\
           .then_inc(small_in, 16)
        for dst, name in ((dt_bias, "dt_bias"), (a_log, "a_log"), (d_half, "d_skip")):
            act.dma_start(dst[:, :], a[name].broadcast_to([P, SH])).then_inc(small_in, 16)
        act.wait_ge(vec_t, 1)
        act.activation(vec[:, :], bank[7][:, 0:VEC_ROWS], ACT.Copy).then_inc(vec_c, 1)
        act.activation(convb[:, :], bank[7][:, P:P + XBC // P], ACT.Copy).then_inc(vec_c, 1)
        act.activation(convw[:, :], bank[7][:, 2 * P:3 * P], ACT.Copy).then_inc(vec_c, 1)
        act.wait_ge(vec_c, 1)
        row, rows = VEC["c"]
        act.activation(silu_c[:, :], vec[:, row:row + rows], ACT.Silu).then_inc(silu_done, 1)
        for c in range(KC):
            act.wait_ge(xt_full, c + 1)
            act.activation(xt[:, c, :], bank[1 + c % 4][:, :], ACT.Copy).then_inc(xt_copied, 1)
            square_into(act, c, c % 2, bank[1 + c % 4][:, :])
        act.wait_ge(xt_copied, KC)
        act.dma_start(xt_dram, buf2[:, :, :].rearrange("p k n -> p (k n)")).then_inc(stash, 16)
        for k in range(2):
            hi_of(act, u_lat(k))
        act.wait_ge(setup, 4)
        modulate_act(act, 0, g_mix, 0)
        act.wait_ge(stash, 16)
        act.wait_ge(nm_l, KC)
        act.dma_start(pos_i, a["positions"].broadcast_to([P, T])).then_inc(pos_in, 16)

        for k in range(4):
            job = Job(J_LAT, 0, 2, k)
            act.wait_ge(gemm_done, G_LAT + k + 1)
            if k == 0:
                act.wait_ge(sq_added, KC)
            act.activation(sq[:, k, :] if k < 2 else tt[:, k - 2, :], g_of(job)[:, :], ACT.Square)\
               .then_inc(lat_sq, 1)
            act.activation(lat[:, k, :], g_of(job)[:, :], ACT.Copy).then_inc(g_free[job.bank], 1)
            if k == 2:
                act.wait_ge(krope_in, 16 * 4)
            hi_of(act, u_lat(k + 2))
        act.wait_ge(setup, 4 + SET_TRIG)
        act.activation(sin, sin, ACT.Sin).then_inc(trig, 1)
        act.activation(cos, cos, ACT.Sin).then_inc(trig, 1)
        act.wait_ge(gemm_done, G_LAT + 5)
        hi_of(act, u_lat(6))
        act.wait_ge(gemm_done, G_LAT + 6)
        act.wait_ge(rope_in[0], ROPE_DMAS)
        hi_of(act, u_att(0, 0))
        for k in range(4):
            if k == 2:
                act.wait_ge(gemm_done, G_LAT + 7)
                hi_of(act, u_att(0, 1))
            act.wait_ge(lat_u, k + 1)
            act.activation(lathi[:, k, :], uu[:, k % 2, :], ACT.Copy).then_inc(lat_h, 1)
        act.wait_ge(kr_v, 1)
        act.activation(kr_hi, rope1, ACT.Copy).then_inc(kr_h, 1)
        act.activation(a_log[:, :], a_log[:, :], ACT.Exp).then_inc(dt_a, 1)
        act.wait_ge(dt_v, 1)
        act.activation(dtneg, dtneg, ACT.Exp).then_inc(dt_a, 1)
        act.wait_ge(dt_a, 2)
        act.activation(dtneg, dtneg, ACT.Ln, bias=1.0).then_inc(dt_a, 1)
        act.wait_ge(dt_mm, 1)
        act.activation(decay[:, :, :].rearrange("p a n -> p (a n)"), bank[2][:, 0:3 * P], ACT.Exp)\
           .then_inc(dt_a, 1)

        def att(i, last):
            jobs = [Job(J_ATT, i, 14, k) for k in range(14)]

            def project(e):
                h, g, j = 2 * i + e, G_ATT + 18 * i + 5 * e, jobs[5 * e:5 * e + 5]
                act.wait_ge(gemm_done, g + 1)
                act.activation(qn_hi[:, e, :], g_of(j[0])[:, :], ACT.Copy).then_inc(proj_h, 1)
                if e == 0:
                    act.wait_ge(gemm_done, g + 3)
                    act.wait_ge(rope_in[1], ROPE_DMAS * (i + 1))
                    hi_of(act, u_att(i, 2))
                act.wait_ge(rot, h + 1)
                act.activation(q_rope[:, e, :], rope1, ACT.Copy).then_inc(proj_h, 1)
                act.wait_ge(gemm_done, g + 4)
                act.activation(kn_hi[:, e, :], g_of(j[3])[:, :], ACT.Copy).then_inc(proj_h, 1)
                act.wait_ge(gemm_done, g + 5)
                act.activation(v_hi[:, e, :], g_of(j[4])[:, :], ACT.Copy).then_inc(proj_h, 1)
                if e == 0:
                    hi_of(act, u_att(i, 3))

            def exps(e):
                h = 2 * i + e
                act.wait_ge(s_neg, h + 1)
                for qb in range(TB):
                    n, c = (qb + 1) * P, e * TB + qb
                    act.activation(probs[:, e, qb, 0:n], bank[qb][:, 0:n], ACT.Exp, scale=SCALE,
                                   bias=negmax[:, c:c + 1], accum_out=rowsum[:, c:c + 1])\
                       .then_inc(s_exp, 1)

            def attend(e):
                h = 2 * i + e
                for j in range(TB):
                    t = 4 * h + j
                    act.wait_ge(pt_full, t + 1)
                    act.wait_ge(pv_done, t + 1)
                    act.activation(pthi[:, j % 2, j * P:T], bank[4 + j % 2][:, j * P:T], ACT.Copy)\
                       .then_inc(pt_h, 1)
                    if e == 1 and j >= 2:
                        if j == 2 and not last:
                            act.wait_ge(rope_in[0], ROPE_DMAS * (i + 2))
                        hi_of(act, u_att(i, 2 + j))
                act.wait_ge(pv_done, 2 + 4 * h + 4)
                act.activation(at(fhi, h), g_of(jobs[10 if e == 0 else 13])[:, :], ACT.Copy)\
                   .then_inc(o_h, 1)

            project(0)
            exps(0)
            project(1)
            exps(1)
            attend(0)
            attend(1)

        last_peeled(act, HEADS // 2, att)

        def oa(i, last):
            for k in range(4):
                job = Job(J_OA, i, 4, k)
                act.wait_ge(gemm_done, G_OA + 4 * i + k + 1)
                act.activation(at(buf1, 4 * i + k), g_of(job)[:, :], ACT.Copy, scale=0.5)\
                   .then_inc(g_free[job.bank], 1)
                hi_of(act, u_run(R_OA, B_OA, 4, i, k + 2))

        last_peeled(act, 2, oa)

        def group(i, last):
            def stream(k):
                act.wait_ge(gemm_done, G_SSM + 8 * i + k + 1)
                return Job(J_SSM, i, 8, k)

            def refill(k):
                hi_of(act, u_run(R_SSM, B_SSM, 8, i, k + 2))

            def conv(k):
                v = 4 * i + k
                cc = conv_chunk(i, k)
                job = stream(k)
                act.wait_ge(cv_out, v + 1)
                act.activation(tt[:, k % 2, :], g_of(job)[:, :], ACT.Identity,
                               scale=cols(convw, (TAPS - 1) * (XBC // P) + cc, 1),
                               bias=cols(convb, cc, 1)).then_inc(cv_acc, 1)
                refill(k)
                act.wait_ge(g_free[job.bank], job.before + 1)
                if k == 2:
                    act.wait_ge(yg_l, 2 * i + 1)
                act.activation(conv_dst(k), tt[:, k % 2, :], ACT.Tanh, scale=0.5).then_inc(cv_tanh, 1)

            def copy_in(n, dst, src):
                act.wait_ge(tin_done, 3 * i + n + 1)
                act.activation(dst, src, ACT.Copy).then_inc(tin_copied, 1)

            def exp_decay(ch):
                n = 4 * i + ch
                act.wait_ge(seg_done, n + 2)
                act.wait_ge(yd_done, n + 1)
                act.activation(sq[:, ch % 2, :], bank[0][:, :], ACT.Exp).then_inc(e_done, 1)

            def z_gate(f):
                job = stream(4 + f)
                act.activation(zs[:, f, :], g_of(job)[:, :], ACT.Tanh, scale=0.5).then_inc(z_tanh, 1)
                refill(4 + f)

            conv(0)
            conv(1)
            conv(2)
            copy_in(0, b_tok[:, :], bank[4][:, :])
            conv(3)
            copy_in(1, x_tok[:, :, 0:P], bank[5][:, :].rearrange("p (a n) -> p a n", a=TB))
            exp_decay(0)
            z_gate(0)
            copy_in(2, x_tok[:, :, P:GF], bank[4][:, :].rearrange("p (a n) -> p a n", a=TB))
            exp_decay(1)
            z_gate(1)
            exp_decay(2)
            job = stream(6)
            act.activation(uu[:, 0, :], g_of(job)[:, :], ACT.Tanh, scale=0.5).then_inc(g_free[job.bank], 1)
            refill(6)
            exp_decay(3)
            job = stream(7)
            act.activation(at(buf2, i), g_of(job)[:, :], ACT.Tanh, scale=0.5).then_inc(g_free[job.bank], 1)
            refill(7)
            for f in range(2):
                act.wait_ge(gt_done, 2 * i + f + 2)
                act.activation(sq[:, f, :], zs[:, f, :], ACT.Square).then_inc(gsq_done, 1)
            for f in range(2):
                act.wait_ge(yg_u, 2 * i + f + 1)
                act.activation(at(fhi, 2 * i + f), uu[:, f, :], ACT.Copy).then_inc(yg_h, 1)

        last_peeled(act, GROUPS, group)

        def os_(i, last):
            for c in range(2):
                for half in range(2):
                    k = 2 * c + half
                    act.wait_ge(gemm_done, G_OS + 4 * i + k + 1)
                    hi_of(act, u_run(R_OS, B_OS, 4, i, k + 2))
                act.wait_ge(mg_u, 2 * i + c + 1)
                act.activation(at(ahi, 2 * i + c), uu[:, c, :], ACT.Copy).then_inc(mg_h, 1)

        last_peeled(act, 4, os_)
        act.wait_ge(mg_l, 1 + KC)
        act.dma_start(buf1[:, :, :].rearrange("p k n -> p (k n)"), xt_dram).then_inc(xt_in, 16)

        def out_(i, last):
            for k in range(4):
                c = 4 * i + k
                job = Job(J_OUT, i, 4, k)
                act.wait_ge(gemm_done, G_OUT + c + 1)
                square_into(act, KC + c, k % 2, g_of(job)[:, :])
                act.activation(at(buf2, c), g_of(job)[:, :], ACT.Copy).then_inc(g_free[job.bank], 1)
                hi_of(act, u_run(R_OUT, B_OUT, 4, i, k + 2))

        last_peeled(act, 2, out_)
        for c in range(KC):
            act.wait_ge(x1_done, c + 1)
            square_into(act, 2 * KC + c, c % 2, buf1[:, c, :])
        modulate_act(act, 1, g_mlp, 24)

        for half in range(2):
            r0, b0, g0, j0 = R_FF + 32 * half, B_FF + 32 * half, G_FF + 32 * half, J_FF + J_HALF * half

            def up(i, last, r0=r0, b0=b0, g0=g0, j0=j0, half=half):
                for k in range(4):
                    f = 16 * half + 4 * i + k
                    job = Job(j0, i, 4, k)
                    act.wait_ge(gemm_done, g0 + 4 * i + k + 1)
                    act.wait_ge(ff_q, f + 1)
                    act.activation(tt[:, k % 2, :], g_of(job)[:, :], ACT.Relu).then_inc(g_free[job.bank], 1)
                    hi_of(act, u_run(r0, b0, 4, i, k + 2))
                    act.wait_ge(ff_q, f + 2)
                    act.activation(at(fhi, 4 * i + k), uu[:, k % 2, :], ACT.Copy).then_inc(ff_h, 1)

            last_peeled(act, 4, up)

            def down(i, last, r0=r0 + 16, b0=b0 + 16, g0=g0 + 16, j0=j0 + 16, half=half):
                for c in range(2):
                    job = Job(j0, i, 2, c)
                    for part in range(2):
                        k = 2 * c + part
                        act.wait_ge(gemm_done, g0 + 4 * i + k + 1)
                        if not (half == 1 and last and k >= 2):
                            hi_of(act, u_run(r0, b0, 4, i, k + 2))
                    if half == 0:
                        act.activation(at(buf2, 2 * i + c), g_of(job)[:, :], ACT.Copy)\
                           .then_inc(g_free[job.bank], 1)
                    else:
                        act.wait_ge(g_free[job.bank], job.before + 1)
                        square_into(act, 3 * KC + 2 * i + c, c % 2, at(buf2, 2 * i + c))

            last_peeled(act, 4, down)
        for c in range(KC):
            act.wait_ge(fin_tr, c + 1)
            if c >= 4:
                act.wait_ge(out_sent[c % 4], 16 * (c // 4))
            act.activation(ost[c % 4], bank[2 + c % 2][:, :], ACT.Copy).then_inc(fin_copy, 1)

    @block.vector
    def _(dve):
        dve.sem_inc(pt_l, 2)
        dve.sem_inc(cv_out, 2)
        for s in (cbm_done, m_done, h_done, y_done, gt_done, yg_l, mg_l, ff_l):
            dve.sem_inc(s, 1)
        dve.wait_ge(small_in, SMALL)
        dve.tensor_copy(strict_r[:, :], strict).then_inc(setup, 1)
        dve.tensor_scalar(d_half[:, :], d_half[:, :], 0.5, None, ALU.mult).then_inc(setup, 1)
        dve.wait_ge(vec_c, 3)
        dve.wait_ge(gemm_done, 16)
        dve.tensor_tensor(mod[:, 0:16], bank[5][:, 0:16], vec[:, 0:16], ALU.add).then_inc(setup, 1)
        dve.wait_ge(setup, 3)
        row = VEC["g_pre_mix"][0]
        dve.scalar_tensor_tensor(g_mix[:, :], mod[:, 8:16], 1.0, vec[:, row:row + 8], ALU.add, ALU.mult)\
           .then_inc(setup, 1)
        for k in range(2):
            lo_of(dve, u_lat(k))
        rms_dve(dve, RMS_X, bank[0], D)
        dve.wait_ge(xt_copied, KC)
        dve.wait_ge(rep_done, RMS_X + 1)
        modulate_dve(dve, 0, xt, bank[0])

        step = [4]

        def chain(ins):
            ins.then_inc(setup, 1)
            step[0] += 1
            dve.wait_ge(setup, step[0])

        def reduced(out, quarter):
            turns = rope2
            chain(dve.tensor_scalar(turns, rope1, 1.0 / (2 * np.pi), quarter, ALU.mult, ALU.add))
            chain(dve.tensor_scalar(turns, turns, MAGIC, -MAGIC, ALU.add, ALU.add))
            chain(dve.scalar_tensor_tensor(out, turns, -TWO_PI_1, rope1, ALU.mult, ALU.add))
            chain(dve.scalar_tensor_tensor(out, turns, -TWO_PI_2, out, ALU.mult, ALU.add))
            chain(dve.scalar_tensor_tensor(out, turns, -TWO_PI_3, out, ALU.mult, ALU.add))
            chain(dve.tensor_scalar(out, out, quarter * 2 * np.pi, PI_IN, ALU.add, ALU.min))
            chain(dve.tensor_scalar(out, out, -PI_IN, None, ALU.max))

        lo_of(dve, u_lat(2))
        dve.wait_ge(pos_in, 16)
        chain(dve.tensor_copy(rope2, pos_i))
        chain(dve.tensor_scalar(rope1, rope2, con[:, CON_FREQ:CON_FREQ + 1], None, ALU.mult))
        lo_of(dve, u_lat(3))
        reduced(sin, 0.0)
        lo_of(dve, u_lat(4))
        reduced(cos, 0.25)
        assert step[0] == 4 + SET_TRIG
        lo_of(dve, u_lat(5))
        dve.wait_ge(trig, 2)
        chain(dve.tensor_scalar(sin, sin, con[:, CON_SIGN:CON_SIGN + 1], None, ALU.mult))

        job = Job(J_LAT, 0, 2, 4)
        dve.wait_ge(gemm_done, G_LAT + 5)
        dve.tensor_tensor(rope1, g_of(job)[:, :], cos, ALU.mult).then_inc(g_free[job.bank], 1)
        rms_dve(dve, RMS_Q, bank[0], RANK)
        lo_of(dve, u_lat(6))
        job = Job(J_LAT, 0, 2, 5)
        dve.wait_ge(gemm_done, G_LAT + 6)
        dve.tensor_tensor(rope2, g_of(job)[:, :], sin, ALU.mult).then_inc(g_free[job.bank], 1)
        dve.wait_ge(g_free[1], 3)
        dve.wait_ge(g_free[0], 3)
        dve.tensor_tensor(rope1, rope1, rope2, ALU.add).then_inc(kr_v, 1)
        lo_of(dve, u_att(0, 0))

        def latents(k0, gain, rbank, r):
            dve.wait_ge(rep_done, r + 1)
            row = VEC[gain][0]
            for k in range(k0, k0 + 2):
                wait(dve, lat_l, k - 1)
                dve.scalar_tensor_tensor(uu[:, k % 2, :], lat[:, k, :], vec[:, row + k - k0:row + k - k0 + 1],
                                         rbank[:, :], ALU.mult, ALU.mult).then_inc(lat_u, 1)
            for k in range(k0, k0 + 2):
                dve.wait_ge(lat_h, k + 1)
                dve.tensor_tensor(latlo[:, k, :], uu[:, k % 2, :], lathi[:, k, :].bitcast(F32),
                                  ALU.subtract).then_inc(lat_l, 1)

        latents(0, "g_q_lat", bank[0], RMS_Q)
        rms_dve(dve, RMS_KV, bank[1], RANK)
        job = Job(J_LAT, 0, 2, 6)
        dve.wait_ge(gemm_done, G_LAT + 7)
        dve.tensor_tensor(dtx.rearrange("p (a n) -> p a n", a=TB),
                          g_of(job)[:, 0:TB * SH].rearrange("p (a n) -> p a n", a=TB),
                          dt_bias[:, :].unsqueeze(1).broadcast_to([P, TB, SH]), ALU.add)\
           .then_inc(g_free[job.bank], 1)
        dve.wait_ge(g_free[job.bank], job.before + 1)
        dve.scalar_tensor_tensor(dtneg, dtx, -1.0, dtx, ALU.mult, ALU.min).then_inc(dt_v, 1)
        lo_of(dve, u_att(0, 1))
        latents(2, "g_kv_lat", bank[1], RMS_KV)
        dve.wait_ge(kr_h, 1)
        dve.tensor_tensor(kr_lo, rope1, kr_hi.bitcast(F32), ALU.subtract).then_inc(kr_v, 1)
        dve.wait_ge(dt_a, 3)
        dve.scalar_tensor_tensor(dtx, dtx, 0.0, dtneg, ALU.max, ALU.add).then_inc(dt_v, 1)
        dve.wait_ge(dt_v, 2)
        dve.scalar_tensor_tensor(dta[:, :].rearrange("p (a n) -> p a n", a=TB),
                                 dtx.rearrange("p (a n) -> p a n", a=TB), -1.0,
                                 a_log[:, :].unsqueeze(1).broadcast_to([P, TB, SH]), ALU.mult, ALU.mult)\
           .then_inc(dt_v, 1)
        dve.tensor_scalar(dt_half[:, :], dtx, 0.5, None, ALU.mult).then_inc(dt_v, 1)
        dve.wait_ge(dt_v, 4)
        dve.tensor_copy(dta_hi[:, :], dta[:, :]).then_inc(dt_v, 1)
        dve.wait_ge(dt_v, 5)
        dve.tensor_tensor(dta_lo[:, :], dta[:, :], dta_hi[:, :].bitcast(F32), ALU.subtract)\
           .then_inc(dt_v, 1)
        dve.wait_ge(dt_a, 4)
        dve.scalar_tensor_tensor(dt_end[:, :], dt_half[:, :], 0.5, decay[:, 1, :], ALU.mult, ALU.mult)\
           .then_inc(dt_v, 1)
        dve.tensor_scalar(decay[:, 0, :], decay[:, 0, :], 0.5, None, ALU.mult).then_inc(dt_v, 1)

        def att(i, last):
            jobs = [Job(J_ATT, i, 14, k) for k in range(14)]

            def project(e):
                h, g, j = 2 * i + e, G_ATT + 18 * i + 5 * e, jobs[5 * e:5 * e + 5]

                def low(dst, job, hi, n):
                    dve.wait_ge(proj_h, 4 * h + n)
                    return dve.tensor_tensor(dst, g_of(job)[:, :], hi.bitcast(F32), ALU.subtract)

                low(qn_lo[:, e, :], j[0], qn_hi[:, e, :], 1).then_inc(g_free[j[0].bank], 1)
                dve.wait_ge(gemm_done, g + 2)
                dve.tensor_tensor(rope1, g_of(j[1])[:, :], cos, ALU.mult).then_inc(g_free[j[1].bank], 1)
                dve.wait_ge(gemm_done, g + 3)
                dve.tensor_tensor(rope2, g_of(j[2])[:, :], sin, ALU.mult).then_inc(g_free[j[2].bank], 1)
                dve.wait_ge(g_free[j[1].bank], j[1].before + 1)
                dve.wait_ge(g_free[j[2].bank], j[2].before + 1)
                dve.tensor_tensor(rope1, rope1, rope2, ALU.add).then_inc(rot, 1)
                if e == 0:
                    lo_of(dve, u_att(i, 2))
                dve.wait_ge(proj_h, 4 * h + 2)
                dve.tensor_tensor(q_rope[ROPE:P, e, :], rope1[ROPE:P], q_rope[ROPE:P, e, :].bitcast(F32),
                                  ALU.subtract).then_inc(proj_l, 1)
                low(kn_lo[:, e, :], j[3], kn_hi[:, e, :], 3).then_inc(g_free[j[3].bank], 1)
                low(v_lo[:, e, :], j[4], v_hi[:, e, :], 4).then_inc(g_free[j[4].bank], 1)
                if e == 0:
                    lo_of(dve, u_att(i, 3))

            def softmax(e):
                h = 2 * i + e
                for qb in range(TB):
                    dve.wait_ge(s_full, 4 * h + qb + 1)
                    blk = bank[qb][:, qb * P:(qb + 1) * P]
                    dve.tensor_tensor(blk, blk, mask, ALU.add).then_inc(s_masked, 1)
                for qb in range(TB):
                    c = e * TB + qb
                    dve.wait_ge(s_masked, 4 * h + qb + 1)
                    dve.tensor_reduce(rowmax[:, c:c + 1], bank[qb][:, 0:(qb + 1) * P], AX.X, ALU.max)\
                       .then_inc(s_max, 1)
                dve.wait_ge(s_max, 4 * h + 4)
                dve.tensor_scalar(negmax[:, e * TB:(e + 1) * TB], rowmax[:, e * TB:(e + 1) * TB], -SCALE,
                                  None, ALU.mult).then_inc(s_neg, 1)

            def inverse(e):
                h = 2 * i + e
                dve.wait_ge(s_exp, 4 + 4 * h + 4)
                dve.reciprocal(rowinv[:, e * TB:(e + 1) * TB], rowsum[:, e * TB:(e + 1) * TB])\
                   .then_inc(s_inv, 1)

            def attend(e):
                h = 2 * i + e
                for j in range(TB):
                    dve.wait_ge(pt_h, 4 * h + j + 1)
                    dve.tensor_tensor(ptlo[:, j % 2, j * P:T], bank[4 + j % 2][:, j * P:T],
                                      pthi[:, j % 2, j * P:T].bitcast(F32), ALU.subtract).then_inc(pt_l, 1)
                    if e == 1 and j >= 2:
                        lo_of(dve, u_att(i, 2 + j))
                job = jobs[10 if e == 0 else 13]
                dve.wait_ge(o_h, h + 1)
                dve.tensor_tensor(at(flo, h), g_of(job)[:, :], at(fhi, h).bitcast(F32), ALU.subtract)\
                   .then_inc(g_free[job.bank], 1)

            def modulation(k):
                job = jobs[11 + k]
                col = 16 + 8 * i + 4 * k
                dve.wait_ge(gemm_done, G_ATT + 18 * i + 10 + 4 * (k + 1))
                dve.tensor_tensor(cols(mod, col, 4), g_of(job)[:, 0:4], cols(vec, col, 4), ALU.add)\
                   .then_inc(g_free[job.bank], 1)

            project(0)
            softmax(0)
            project(1)
            inverse(0)
            softmax(1)
            inverse(1)
            attend(0)
            modulation(0)
            modulation(1)
            attend(1)

        last_peeled(dve, HEADS // 2, att)

        final = Job(J_ATT, 3, 14, 12)
        dve.wait_ge(g_free[final.bank], final.before + 1)
        final = Job(J_ATT, 3, 14, 11)
        dve.wait_ge(g_free[final.bank], final.before + 1)
        row = VEC["g_pre_mlp"][0]
        dve.scalar_tensor_tensor(g_mlp[:, :], mod[:, 32:40], 1.0, vec[:, row:row + 8], ALU.add, ALU.mult)\
           .then_inc(mod_done, 1)
        row = VEC["g_post_mix"][0]
        dve.tensor_tensor(gp_mix[:, :], mod[:, 16:24], vec[:, row:row + 8], ALU.mult).then_inc(mod_done, 1)
        row = VEC["g_post_mlp"][0]
        dve.tensor_tensor(gp_mlp[:, :], mod[:, 40:48], vec[:, row:row + 8], ALU.mult).then_inc(mod_done, 1)

        def oa(i, last):
            for k in range(4):
                lo_of(dve, u_run(R_OA, B_OA, 4, i, k + 2))

        last_peeled(dve, 2, oa)

        def group(i, last):
            def heads(table, ch):
                return cols(table, ch * SH + GH * i, GH)

            def refill(k):
                lo_of(dve, u_run(R_SSM, B_SSM, 8, i, k + 2))

            def conv(k):
                v = 4 * i + k
                cc = conv_chunk(i, k)
                job = Job(J_SSM, i, 8, k)
                acc, src = tt[:, k % 2, :], g_of(job)
                dve.wait_ge(cv_acc, v + 1)
                for n, tap in enumerate((2, 1, 0)):
                    s = TAPS - 1 - tap
                    if n:
                        dve.wait_ge(cv_tap, 2 * v + n)
                    ins = dve.scalar_tensor_tensor(acc[:, s:T], src[:, 0:T - s],
                                                   cols(convw, tap * (XBC // P) + cc, 1), acc[:, s:T],
                                                   ALU.mult, ALU.add)
                    if n < 2:
                        ins.then_inc(cv_tap, 1)
                    else:
                        ins.then_inc(g_free[job.bank], 1)
                refill(k)
                dve.wait_ge(cv_tanh, v + 1)
                dve.scalar_tensor_tensor(conv_dst(k), conv_dst(k), 1.0, acc, ALU.add, ALU.mult)\
                   .then_inc(cv_out, 1)

            def masked(ch):
                n = 4 * i + ch
                dve.wait_ge(cb_done, n + 1)
                dve.wait_ge(m_done, n + 1)
                dve.scalar_tensor_tensor(cbm[:, :], bank[1][:, 0:P], 0.25, tri, ALU.mult, ALU.mult)\
                   .then_inc(cbm_done, 1)
                dve.wait_ge(cbm_done, n + 2)
                dve.wait_ge(e_done, n + 2)
                e = sq[:, ch % 2, :].rearrange("p (h l) -> p h l", h=GH)
                dve.tensor_tensor(e, e, cbm[:, :].unsqueeze(1).broadcast_to([P, GH, P]), ALU.mult)\
                   .then_inc(m_done, 1)

            def outputs(ch):
                n = 4 * i + ch
                off, diag_ = bank[2][:, 0:GF], bank[2][:, GF:2 * GF]
                dve.wait_ge(yd_done, 2 + n + 1)
                dve.wait_ge(yt_done, n + 1)
                if ch == 0:
                    dve.wait_ge(xd_done, n + 1)
                    dve.tensor_tensor(y[:, :], diag_, xd[:, :], ALU.add).then_inc(y_done, 1)
                else:
                    m = 6 * i + 2 * (ch - 1)
                    dve.tensor_tensor(y[:, :].rearrange("p (h d) -> p h d", h=GH),
                                      off.rearrange("p (h d) -> p h d", h=GH),
                                      heads(decay[:, 0, :], ch).unsqueeze(2).broadcast_to([P, GH, HD]),
                                      ALU.mult).then_inc(y_part, 1)
                    dve.wait_ge(y_part, m + 1)
                    dve.tensor_tensor(y[:, :], diag_, y[:, :], ALU.add).then_inc(y_part, 1)
                    dve.wait_ge(y_part, m + 2)
                    dve.tensor_tensor(y[:, :], y[:, :], xd[:, :], ALU.add).then_inc(y_done, 1)

            def advance(ch):
                dve.wait_ge(s_done, 3 * i + ch + 1)
                if ch == 0:
                    dve.tensor_copy(state[:, :], bank[3][:, 0:GF]).then_inc(h_done, 1)
                else:
                    st = state[:, :].rearrange("p (h d) -> p h d", h=GH)
                    dve.tensor_tensor(st, st, heads(decay[:, 2, :], ch).unsqueeze(2)
                                      .broadcast_to([P, GH, HD]), ALU.mult).then_inc(h_scaled, 1)
                    dve.wait_ge(h_scaled, 2 * i + ch)
                    dve.tensor_tensor(state[:, :], bank[3][:, 0:GF], state[:, :], ALU.add)\
                       .then_inc(h_done, 1)

            def z_gate(f):
                job = Job(J_SSM, i, 8, 4 + f)
                dve.wait_ge(z_tanh, 2 * i + f + 1)
                dve.scalar_tensor_tensor(zs[:, f, :], zs[:, f, :], 1.0, g_of(job)[:, :], ALU.add, ALU.mult)\
                   .then_inc(g_free[job.bank], 1)
                refill(4 + f)

            for k in range(4):
                conv(k)
            masked(0)
            z_gate(0)
            masked(1)
            z_gate(1)
            outputs(0)
            advance(0)
            masked(2)
            job = Job(J_SSM, i, 8, 6)
            dve.wait_ge(g_free[job.bank], job.before + 1)
            dve.scalar_tensor_tensor(at(buf1, i), uu[:, 0, :], 1.0, at(buf1, i), ALU.add, ALU.mult)\
               .then_inc(ga_out, 1)
            refill(6)
            outputs(1)
            advance(1)
            masked(3)
            refill(7)
            outputs(2)
            advance(2)
            outputs(3)
            for f in range(2):
                if f == 0:
                    dve.wait_ge(yt_done, 1 + 4 * i + 4)
                dve.scalar_tensor_tensor(zs[:, f, :], bank[4 + f][:, :], 0.5, zs[:, f, :], ALU.mult,
                                         ALU.mult).then_inc(gt_done, 1)
            rms_dve(dve, RMS_G + i, bank[1], GF)
            dve.wait_ge(rep_done, RMS_G + i + 1)
            dve.wait_ge(ga_out, i + 1)
            row = VEC["g_ssm_out"][0]
            for f in range(2):
                dve.scalar_tensor_tensor(uu[:, f, :], zs[:, f, :], cols(vec, row + 2 * i + f, 1),
                                         bank[1][:, :], ALU.mult, ALU.mult).then_inc(yg_u, 1)
            for f in range(2):
                dve.wait_ge(yg_h, 2 * i + f + 1)
                dve.tensor_tensor(at(flo, 2 * i + f), uu[:, f, :], at(fhi, 2 * i + f).bitcast(F32),
                                  ALU.subtract).then_inc(yg_l, 1)

        last_peeled(dve, GROUPS, group)

        def os_(i, last):
            for c in range(2):
                n = 2 * i + c
                job = Job(J_OS, i, 2, c)
                for half in range(2):
                    lo_of(dve, u_run(R_OS, B_OS, 4, i, 2 * c + half + 2))
                dve.wait_ge(gemm_done, G_OS + 4 * i + 2 * c + 2)
                dve.wait_ge(mg_l, n + 1)
                dve.scalar_tensor_tensor(tt[:, c, :], at(buf2, n), 1.0, g_of(job)[:, :], ALU.add,
                                         ALU.mult).then_inc(g_free[job.bank], 1)
                dve.wait_ge(g_free[job.bank], job.before + 1)
                dve.scalar_tensor_tensor(uu[:, c, :], tt[:, c, :], 0.5, at(buf1, n), ALU.mult, ALU.add)\
                   .then_inc(mg_u, 1)
                dve.wait_ge(mg_h, n + 1)
                dve.tensor_tensor(at(alo, n), uu[:, c, :], at(ahi, n).bitcast(F32), ALU.subtract)\
                   .then_inc(mg_l, 1)

        last_peeled(dve, 4, os_)

        def out_(i, last):
            for k in range(4):
                lo_of(dve, u_run(R_OUT, B_OUT, 4, i, k + 2))

        last_peeled(dve, 2, out_)
        rms_dve(dve, RMS_MIX, bank[0], D)
        dve.wait_ge(rep_done, RMS_MIX + 1)
        dve.wait_ge(xt_in, 16)
        dve.wait_ge(mod_done, 3)
        for c in range(KC):
            dve.scalar_tensor_tensor(tt[:, c % 2, :], buf2[:, c, :], gp_mix[:, c:c + 1], bank[0][:, :],
                                     ALU.mult, ALU.mult).then_inc(x1_t, 1)
            dve.wait_ge(x1_t, c + 1)
            dve.tensor_tensor(buf1[:, c, :], tt[:, c % 2, :], buf1[:, c, :], ALU.add).then_inc(x1_done, 1)
            dve.wait_ge(x1_done, c + 1)
        rms_dve(dve, RMS_MLP, bank[1], D)
        dve.wait_ge(rep_done, RMS_MLP + 1)
        modulate_dve(dve, 1, buf1, bank[1])

        for half in range(2):
            r0, b0, g0, j0 = R_FF + 32 * half, B_FF + 32 * half, G_FF + 32 * half, J_FF + J_HALF * half

            def up(i, last, r0=r0, b0=b0, half=half):
                for k in range(4):
                    f = 16 * half + 4 * i + k
                    lo_of(dve, u_run(r0, b0, 4, i, k + 2))
                    dve.wait_ge(ff_h, f + 1)
                    dve.tensor_tensor(at(flo, 4 * i + k), uu[:, k % 2, :], at(fhi, 4 * i + k).bitcast(F32),
                                      ALU.subtract).then_inc(ff_l, 1)

            last_peeled(dve, 4, up)

            def down(i, last, r0=r0 + 16, b0=b0 + 16, g0=g0 + 16, j0=j0 + 16, half=half):
                for c in range(2):
                    job = Job(j0, i, 2, c)
                    for part in range(2):
                        if not (half == 1 and last and c == 1):
                            lo_of(dve, u_run(r0, b0, 4, i, 2 * c + part + 2))
                    if half == 1:
                        dve.wait_ge(gemm_done, g0 + 4 * i + 2 * c + 2)
                        dve.tensor_tensor(at(buf2, 2 * i + c), g_of(job)[:, :], at(buf2, 2 * i + c),
                                          ALU.add).then_inc(g_free[job.bank], 1)

            last_peeled(dve, 4, down)
        rms_dve(dve, RMS_FF, bank[0], D)
        dve.wait_ge(rep_done, RMS_FF + 1)
        for c in range(KC):
            dve.scalar_tensor_tensor(tt[:, c % 2, :], buf2[:, c, :], gp_mlp[:, c:c + 1], bank[0][:, :],
                                     ALU.mult, ALU.mult).then_inc(fin_t, 1)
            dve.wait_ge(fin_t, c + 1)
            dve.tensor_tensor(buf2[:, c, :], tt[:, c % 2, :], buf1[:, c, :], ALU.add).then_inc(fin_done, 1)
            dve.wait_ge(fin_done, c + 1)

    @block.gpsimd
    def _(pool):
        pool.sem_inc(ff_q, 1)
        pool.memset(minus_half[:, :], -0.5).then_inc(pool_setup, 1)
        pool.wait_ge(pool_setup, 1)
        clear_sum(pool, 0)
        for c in range(KC):
            add_square(pool, c, c % 2, 1)
        for r in (RMS_X, RMS_Q, RMS_KV):
            rms_pool(pool, r)

        def att(i, last):
            for e in range(2):
                h = 2 * i + e
                pool.wait_ge(s_inv, h + 1)
                for qb in range(TB):
                    blk = probs[:, e, qb, 0:(qb + 1) * P]
                    inv = rowinv[:, e * TB + qb:e * TB + qb + 1]
                    if qb == 0:
                        ins = pool.tensor_tensor(blk, blk, inv.broadcast_to([P, P]), ALU.mult)
                    else:
                        ins = pool.tensor_scalar(blk, blk, inv, 1.0, ALU.mult, ALU.mult)
                    ins.then_inc(p_norm, 1)

        last_peeled(pool, HEADS // 2, att)
        pool.wait_ge(gemm_done, G_SSM)
        pool.wait_ge(dt_v, 8)

        def group(i, last):
            def ramps(ch):
                pool.wait_ge(seg_done, 4 * i + ch + 1)
                for dst, table in ((rm_hi, dta_hi), (rm_lo, dta_lo)):
                    col = cols(table, ch * SH + GH * i, GH)
                    if table is dta_hi:
                        col = col.bitcast(F32)
                    ins = pool.tensor_tensor(dst[:, :].rearrange("p (h l) -> p h l", h=GH),
                                             tri.unsqueeze(1).broadcast_to([P, GH, P]),
                                             col.unsqueeze(2).broadcast_to([P, GH, P]), ALU.mult)
                ins.then_inc(rm_done, 1)

            def scaled(ch):
                if ch == 0:
                    pool.wait_ge(tin_copied, 3 * i + 3)
                else:
                    pool.wait_ge(s_done, 3 * i + ch)
                    pool.wait_ge(y_done, 4 * i + ch + 1)
                src = x_tok[:, ch, :].rearrange("p (h d) -> p h d", h=GH)
                for dst, table in ((xdt, cols(dt_half, ch * SH + GH * i, GH)),
                                   (xend, cols(dt_end, ch * SH + GH * i, GH)),
                                   (xd, cols(d_half, GH * i, GH))):
                    ins = pool.tensor_tensor(dst[:, :].rearrange("p (h d) -> p h d", h=GH), src,
                                             table.unsqueeze(2).broadcast_to([P, GH, HD]), ALU.mult)
                ins.then_inc(xd_done, 1)

            ramps(0)
            ramps(1)
            scaled(0)
            ramps(2)
            scaled(1)
            ramps(3)
            scaled(2)
            scaled(3)
            rms_pool(pool, RMS_G + i)

        last_peeled(pool, GROUPS, group)

        clear_sum(pool, RMS_G + GROUPS)

        def out_(i, last):
            for k in range(4):
                add_square(pool, KC + 4 * i + k, k % 2, 2)

        last_peeled(pool, 2, out_)
        rms_pool(pool, RMS_MIX)
        clear_sum(pool, RMS_MIX + 1)
        for c in range(KC):
            add_square(pool, 2 * KC + c, c % 2, 3)
        rms_pool(pool, RMS_MLP)
        for half in range(2):
            def up(i, last, half=half):
                for k in range(4):
                    f = 16 * half + 4 * i + k
                    job = Job(J_FF + J_HALF * half, i, 4, k)
                    pool.wait_ge(g_free[job.bank], job.before + 1)
                    pool.wait_ge(ff_l, f + 1)
                    pool.tensor_tensor(uu[:, k % 2, :], tt[:, k % 2, :], tt[:, k % 2, :], ALU.mult)\
                        .then_inc(ff_q, 1)

            last_peeled(pool, 4, up)
        clear_sum(pool, RMS_MLP + 1)

        def down(i, last):
            for c in range(2):
                add_square(pool, 3 * KC + 2 * i + c, c, 4)

        last_peeled(pool, 4, down)
        rms_pool(pool, RMS_FF)


NAMES = ("x", "c", "positions", "w_ada", "b_ada", "g_pre_mix", "g_post_mix", "w_in", "g_q_lat",
         "g_kv_lat", "w_uq", "w_ukv", "w_o_attn", "conv_w", "conv_b", "dt_bias", "a_log", "d_skip",
         "g_ssm_out", "w_o_ssm", "w_out", "g_pre_mlp", "g_post_mlp", "w_ff1", "w_ff2")


def kernel(**inputs):
    import concourse.bacc as bacc
    from concourse.bass_utils import run_bass_kernel_spmd

    nc = bacc.Bacc("TRN2", target_bir_lowering=False, num_devices=1)
    arrays = {f"in_{n}": np.ascontiguousarray(inputs[n]) for n in NAMES}
    arrays["in_con"] = constants()
    aps = {}
    for n, v in arrays.items():
        aps[n[3:]] = nc.dram_tensor(n, v.shape, mybir.dt.from_np(v.dtype), kind="ExternalInput").ap()
    aps["out"] = nc.dram_tensor("out", (1, T, D), F32, kind="ExternalOutput").ap()
    build(nc, aps)
    r = run_bass_kernel_spmd(nc, [arrays], core_ids=[0])
    return r.results[0]["out"]
```

```python
from contextlib import ExitStack

import numpy as np
import concourse.bass as bass
from concourse import mybir

P = 128
D = 1024
T = 512
TB = T // P
KC = D // P
HEADS = 8
NOPE = 128
ROPE = 64
RANK = 256
THETA = 10000.0
SSM_IN = 2 * D
SH = 32
GROUPS = 8
GH = SH // GROUPS
HD = SSM_IN // SH
GF = GH * HD
XBC = SSM_IN + 2 * GROUPS * P
TAPS = 4
FF = 4 * D
EPS = 1e-6
SCALE = float(NOPE + ROPE) ** -0.5
RAW = 4

COL_Q = 0
COL_KV = RANK
COL_KR = 2 * RANK
COL_Z = COL_KR + ROPE
COL_X = COL_Z + SSM_IN
COL_B = COL_X + SSM_IN
COL_C = COL_B + GROUPS * P
COL_DT = COL_X + XBC
COL_GA = COL_DT + SH
COL_GB = COL_GA + D

VEC = {}
VEC_ROWS = 0
for _name, _n in (("b_ada", 48), ("c", 8), ("g_pre_mix", 8), ("g_post_mix", 8), ("g_q_lat", 2),
                  ("g_kv_lat", 2), ("g_pre_mlp", 8), ("g_post_mlp", 8), ("g_ssm_out", 16)):
    VEC[_name] = (VEC_ROWS, _n)
    VEC_ROWS += _n

CON_IDENT, CON_TRI, CON_STRICT, CON_ONES, CON_MASK = (P * _i for _i in range(5))
CON_FREQ = 5 * P
CON_SIGN = CON_FREQ + 1
CON_COLS = CON_SIGN + 1

F32 = mybir.dt.float32
F32R = mybir.dt.float32r
I32 = mybir.dt.int32
ALU = mybir.AluOpType
ACT = mybir.ActivationFunctionType
AX = mybir.AxisListType

ADA_BESIDE = 4
R_ADA, R_LAT, R_ATT, R_OA, R_SSM, R_OS, R_OUT, R_FF = 0, 12, 19, 35, 43, 139, 155, 163
R_END = R_FF + 64
B_LAT, B_ATT, B_OA, B_SSM, B_OS, B_OUT, B_FF = 0, 7, 23, 31, 95, 111, 119
G_LAT, G_ATT, G_OA, G_SSM, G_OS, G_OUT, G_FF = 12, 19, 59, 67, 163, 179, 187
J_LAT, J_ATT, J_OA, J_SSM, J_OS, J_OUT, J_FF = 0, 7, 55, 63, 127, 135, 143
J_TURNS = J_ATT + 10
J_HALF = 24
SSM_UNITS = (0, 1, 2, 4, 5, 7, 9, 10)
ADA_UNITS = (3, 6, 8, 11)
SET_TRIG = 16
ROPE_DMAS = 16 * 5
SMALL = 16 * 10
TABLES = 16 * 5
MAGIC = 1.5 * 2.0 ** 23
TWO_PI_1 = 6.28125
TWO_PI_2 = float((np.float32(2 * np.pi - TWO_PI_1).view(np.uint32) & np.uint32(0xFFFFE000))
                 .view(np.float32))
TWO_PI_3 = float(2 * np.pi - TWO_PI_1 - TWO_PI_2)
PI_IN = 3.1415925
RMS_X, RMS_Q, RMS_KV, RMS_G, RMS_MIX, RMS_MLP, RMS_FF = 0, 1, 2, 3, 11, 12, 13


def constants():
    j = np.arange(P)[:, None]
    l = np.arange(P)[None, :]
    con = np.zeros((P, CON_COLS), np.float32)
    con[:, CON_IDENT:CON_IDENT + P] = j == l
    con[:, CON_TRI:CON_TRI + P] = j <= l
    con[:, CON_STRICT:CON_STRICT + P] = j > l
    con[:, CON_ONES:CON_ONES + P] = 1.0
    con[:, CON_MASK:CON_MASK + P] = np.where(l > j, -1e30, 0.0)
    half = ROPE // 2
    freq = np.float32(THETA) ** (-np.arange(half, dtype=np.float32) / np.float32(half))
    con[:, CON_FREQ] = np.tile(freq.astype(np.float32), P // half)
    con[:, CON_SIGN] = np.where(np.arange(P) % ROPE < half, -1.0, 1.0)
    return con


def at(tensor, i):
    if isinstance(i, int):
        return tensor[:, i, :]
    return tensor[:, bass.ds(i, 1), :].rearrange("p a n -> p (a n)")


def cols(tensor, i, n):
    if isinstance(i, int):
        return tensor[:, i:i + n]
    return tensor[:, bass.ds(i, n)]


def wait(eng, semaphore, value):
    if not (isinstance(value, int) and value <= 0):
        eng.wait_ge(semaphore, value)


def last_peeled(eng, count, body):
    with eng.Fori(0, count - 1) as i:
        body(i, False)
    body(count - 1, True)


def build(nc, a):
    with ExitStack() as ctx:
        Program(nc, a, ctx)


def Program(nc, a, ctx):
    def sb(name, shape, dt=F32, stack=ctx):
        return stack.enter_context(nc.sbuf_tensor(name, shape, dt))

    def sem(name):
        return ctx.enter_context(nc.semaphore(name))

    raw = sb("raw", [P, RAW, KC * P])
    whi = sb("whi", [P, 2, KC * P], F32R)
    wlo = sb("wlo", [P, 2, KC * P], F32R)
    ahi = sb("ahi", [P, KC, T], F32R)
    alo = sb("alo", [P, KC, T], F32R)
    fhi = sb("fhi", [P, 2 * KC, T], F32R)
    flo = sb("flo", [P, 2 * KC, T], F32R)
    buf1 = sb("buf1", [P, KC, T])
    buf2 = sb("buf2", [P, KC, T])
    sq = sb("sq", [P, 2, T])
    tt = sb("tt", [P, 2, T])
    uu = sb("uu", [P, 2, T])
    diag = sb("diag", [P, T])

    con = sb("con", [P, CON_COLS])
    strict_r = sb("strict_r", [P, P], F32R)
    vec = sb("vec", [P, VEC_ROWS])
    convb = sb("convb", [P, XBC // P])
    convw = sb("convw", [P, TAPS * XBC // P])
    silu_c = sb("silu_c", [P, KC])
    mod = sb("mod", [P, 48])
    g_mix = sb("g_mix", [P, KC])
    g_mlp = sb("g_mlp", [P, KC])
    gp_mix = sb("gp_mix", [P, KC])
    gp_mlp = sb("gp_mlp", [P, KC])
    minus_half = sb("minus_half", [P, TB])
    ms = sb("ms", [P, TB])
    rstd = sb("rstd", [P, TB])
    rowmax = sb("rowmax", [P, 2 * TB])
    negmax = sb("negmax", [P, 2 * TB])
    rowsum = sb("rowsum", [P, 2 * TB])
    rowinv = sb("rowinv", [P, 2 * TB])
    dt_bias = sb("dt_bias", [P, SH])
    a_log = sb("a_log", [P, SH])
    d_half = sb("d_half", [P, SH])
    dt_half = sb("dt_half", [P, TB * SH])
    dta = sb("dta", [P, TB * SH])
    dta_hi = sb("dta_hi", [P, TB * SH], F32R)
    dta_lo = sb("dta_lo", [P, TB * SH])
    dt_end = sb("dt_end", [P, TB * SH])
    decay = sb("decay", [P, 3, TB * SH])
    ident = con[:, CON_IDENT:CON_IDENT + P]
    tri = con[:, CON_TRI:CON_TRI + P]
    strict = con[:, CON_STRICT:CON_STRICT + P]
    ones = con[:, CON_ONES:CON_ONES + P]
    mask = con[:, CON_MASK:CON_MASK + P]

    with ExitStack() as att:
        lathi = sb("lathi", [P, 4, T], F32R, att)
        latlo = sb("latlo", [P, 4, T], F32R, att)
        pthi = sb("pthi", [P, 2, T], F32R, att)
        ptlo = sb("ptlo", [P, 2, T], F32R, att)
    with ExitStack() as start:
        sb("ssum_room", [P, T], F32, start)
        beside = sb("beside", [P, ADA_BESIDE, KC * P], F32, start)
    ssm = ctx.enter_context(ExitStack())
    c_t = sb("c_t", [P, T], F32, ssm)
    b_t = sb("b_t", [P, T], F32, ssm)
    b_tok = sb("b_tok", [P, T], F32, ssm)
    x_tok = sb("x_tok", [P, TB, GF], F32, ssm)
    zs = sb("zs", [P, 2, T], F32, ssm)
    cbm = sb("cbm", [P, P], F32, ssm)
    rm_hi = sb("rm_hi", [P, GH * P], F32R, ssm)
    rm_lo = sb("rm_lo", [P, GH * P], F32R, ssm)
    xdt = sb("xdt", [P, GF], F32, ssm)
    xend = sb("xend", [P, GF], F32, ssm)
    xd = sb("xd", [P, GF], F32, ssm)
    state = sb("state", [P, GF], F32, ssm)
    y = sb("y", [P, GF], F32, ssm)
    ssum = c_t[:, :]

    x_tok_all = buf1[:, :, :].rearrange("p (a k) n -> p a (k n)", a=TB)
    xt = buf2
    lat = buf2[:, 0:4, :]
    cos, sin, rope1, rope2 = (buf2[:, i, :] for i in range(4, 8))
    probs = buf1[:, :, :].rearrange("p (a b) n -> p a b n", a=2)
    qn_hi, kn_hi, v_hi = fhi[:, 8:10, :], fhi[:, 10:12, :], fhi[:, 12:14, :]
    qn_lo, kn_lo, v_lo = flo[:, 8:10, :], flo[:, 10:12, :], flo[:, 12:14, :]
    q_rope = fhi[:, 14:16, :]
    kr_hi, kr_lo = flo[:, 14, :], flo[:, 15, :]
    dt_feat = tt[0:SH, 0, :]
    dtx = tt[:, 1, 0:TB * SH]
    dtneg = tt[:, 1, TB * SH:2 * TB * SH]
    pos_i = buf2[:, 6, :].bitcast(I32)
    ost = [sq[:, 0, :], sq[:, 1, :], uu[:, 0, :], uu[:, 1, :]]
    vec_rows = uu[0:VEC_ROWS, 0, 0:P]
    convb_rows = uu[0:XBC // P, 0, P:2 * P]
    convw_rows = uu[:, 0, 2 * P:3 * P]

    bank = [ctx.enter_context(nc.psum_tensor(f"bank{i}", [P, T], F32)) for i in range(8)]
    G = bank[6:8]

    small_in = sem("small_in")
    tables_in = sem("tables_in")
    x_in = sem("x_in")
    beside_in = sem("beside_in")
    raw_in = [sem(f"raw_in{i}") for i in range(RAW)]
    rope_in = [sem(f"rope_in{i}") for i in range(2)]
    krope_in = sem("krope_in")
    pos_in = sem("pos_in")
    stash = sem("stash")
    xt_in = sem("xt_in")
    out_sent = [sem(f"out_sent{i}") for i in range(4)]
    w_hi = sem("w_hi")
    w_lo = sem("w_lo")
    gemm_done = sem("gemm_done")
    g_free = [sem(f"g_free{i}") for i in range(2)]
    vec_t = sem("vec_t")
    vec_c = sem("vec_c")
    silu_done = sem("silu_done")
    ada_step = sem("ada_step")
    beside_done = sem("beside_done")
    ada_part = sem("ada_part")
    ada_sum = sem("ada_sum")
    ada_out = sem("ada_out")
    setup = sem("setup")
    pool_setup = sem("pool_setup")
    trig = sem("trig")
    xt_full = sem("xt_full")
    xt_copied = sem("xt_copied")
    sq_full = sem("sq_full")
    sq_zero = sem("sq_zero")
    sq_added = sem("sq_added")
    ssq_done = sem("ssq_done")
    ms_done = sem("ms_done")
    rstd_done = sem("rstd_done")
    diag_done = sem("diag_done")
    rep_done = sem("rep_done")
    nm_t, nm_u, nm_h, nm_l = (sem(n) for n in ("nm_t", "nm_u", "nm_h", "nm_l"))
    lat_sq = sem("lat_sq")
    lat_u, lat_h, lat_l = (sem(n) for n in ("lat_u", "lat_h", "lat_l"))
    kr_v = sem("kr_v")
    kr_h = sem("kr_h")
    dt_x = sem("dt_x")
    dt_v, dt_a = sem("dt_v"), sem("dt_a")
    dt_copied = sem("dt_copied")
    dt_tok = sem("dt_tok")
    dt_mm = sem("dt_mm")
    proj_h = sem("proj_h")
    proj_l = sem("proj_l")
    rot = sem("rot")
    s_full = sem("s_full")
    s_masked = sem("s_masked")
    s_max = sem("s_max")
    s_neg = sem("s_neg")
    s_exp = sem("s_exp")
    s_inv = sem("s_inv")
    p_norm = sem("p_norm")
    pt_full = sem("pt_full")
    pt_h = sem("pt_h")
    pt_l = sem("pt_l")
    pv_done = sem("pv_done")
    o_h = sem("o_h")
    mod_done = sem("mod_done")
    cv_acc = sem("cv_acc")
    cv_tap = sem("cv_tap")
    cv_tanh = sem("cv_tanh")
    cv_out = sem("cv_out")
    tin_done = sem("tin_done")
    tin_copied = sem("tin_copied")
    z_tanh = sem("z_tanh")
    z_out = sem("z_out")
    ga_tanh = sem("ga_tanh")
    ga_out = sem("ga_out")
    rm_done = sem("rm_done")
    cb_done = sem("cb_done")
    seg_done = sem("seg_done")
    cbm_done = sem("cbm_done")
    e_done = sem("e_done")
    m_done = sem("m_done")
    xd_done = sem("xd_done")
    yd_done = sem("yd_done")
    s_done = sem("s_done")
    h_scaled = sem("h_scaled")
    h_done = sem("h_done")
    y_part = sem("y_part")
    y_done = sem("y_done")
    yt_done = sem("yt_done")
    gt_done = sem("gt_done")
    gsq_done = sem("gsq_done")
    yg_u, yg_h = sem("yg_u"), sem("yg_h")
    yg_l = sem("yg_l")
    mg_t, mg_u, mg_h = sem("mg_t"), sem("mg_u"), sem("mg_h")
    mg_l = sem("mg_l")
    mix_out = sem("mix_out")
    x1_t, x1_done = sem("x1_t"), sem("x1_done")
    ff_r = sem("ff_r")
    ff_q = sem("ff_q")
    ff_h = sem("ff_h")
    ff_l = sem("ff_l")
    ff_half = sem("ff_half")
    ff_sum = sem("ff_sum")
    fin_t = sem("fin_t")
    fin_done = [sem("fin_done0"), sem("fin_done1")]
    fin_tr = sem("fin_tr")
    fin_copy = sem("fin_copy")

    xt_dram = nc.dram_tensor("xt_stash", (P, KC * T), F32, kind="Internal").ap()

    w_k = {n: a[n].rearrange("l (k p) n -> p (l k) n", p=P)
           for n in ("w_ada", "w_in", "w_uq", "w_ukv", "w_o_attn", "w_o_ssm", "w_out", "w_ff1", "w_ff2")}
    block = ctx.enter_context(nc.Block())

    def unit_dst(r, kc, n):
        return raw[:, r % RAW, 0:kc * n].rearrange("p (k n) -> p k n", k=kc)

    def loads_of(sp, phase, i, u):
        first = {"ada": R_ADA, "lat": R_LAT, "att": R_ATT, "oa": R_OA, "ssm": R_SSM, "os": R_OS,
                 "out": R_OUT}
        r = (R_FF + 16 * phase[1] if isinstance(phase, tuple) else first[phase]) + u
        slot, landed = r % RAW, raw_in[r % RAW]

        def whole(name, row, col):
            sp.dma_start(unit_dst(r, KC, P),
                         w_k[name][:, row:row + KC, bass.ds(col, P)]).then_inc(landed, 16)

        if phase == "ada":
            whole("w_ada", 0, u * P)
        elif phase == "lat":
            if u < 4:
                whole("w_in", 0, u * P)
            elif u < 6:
                dst = raw[:, slot, :].rearrange("p (k d n) -> p k d n", k=KC, d=2)
                src = w_k["w_in"][:, :, COL_KR:COL_KR + ROPE]
                halves = [(0, 0)] if u == 4 else [(0, 32), (32, 0)]
                width = ROPE if u == 4 else ROPE // 2
                n = 0
                for to, of in halves:
                    for d in range(2):
                        sp.dma_start(dst[:, :, d, to:to + width], src[:, :, of:of + width])\
                          .then_inc(landed if n == 0 else krope_in, 16)
                        n += 1
            else:
                sp.dma_start(unit_dst(r, KC, P)[:, :, 0:SH],
                             w_k["w_in"][:, :, COL_DT:COL_DT + SH]).then_inc(landed, 16)
        elif phase == "att":
            if u in (0, 2):
                h = 2 * i + u // 2
                extra = rope_in[u // 2]
                dst = unit_dst(r, 2, 3 * P)
                col = h * (NOPE + ROPE)
                sp.dma_start(dst[:, :, 0:NOPE + ROPE],
                             w_k["w_uq"][:, :, bass.ds(col, NOPE + ROPE)]).then_inc(landed, 16)
                sp.dma_start(dst[:, :, NOPE + ROPE:2 * P],
                             w_k["w_uq"][:, :, bass.ds(col + NOPE, ROPE)]).then_inc(extra, 16)
                for to, of in ((0, 32), (32, 0), (64, 32), (96, 0)):
                    sp.dma_start(dst[:, :, 2 * P + to:2 * P + to + 32],
                                 w_k["w_uq"][:, :, bass.ds(col + NOPE + of, 32)]).then_inc(extra, 16)
            else:
                h = 2 * i + u // 2
                sp.dma_start(unit_dst(r, 2, 2 * P),
                             w_k["w_ukv"][:, :, bass.ds(h * 2 * P, 2 * P)]).then_inc(landed, 16)
        elif phase == "oa":
            whole("w_o_attn", 0, (4 * i + u) * P)
        elif phase == "ssm":
            if u in ADA_UNITS:
                whole("w_ada", 0, (16 + 4 * i + ADA_UNITS.index(u)) * P)
            else:
                col = (COL_C + i * P, COL_B + i * P, COL_X + i * GF, COL_X + i * GF + P, COL_Z + i * GF,
                       COL_Z + i * GF + P, COL_GA + i * P, COL_GB + i * P)[SSM_UNITS.index(u)]
                whole("w_in", 0, col)
        elif phase == "os":
            whole("w_o_ssm", KC * (u % 2), (2 * i + u // 2) * P)
        elif phase == "out":
            whole("w_out", 0, (4 * i + u) * P)
        else:
            _, part = phase
            if part % 2 == 0:
                whole("w_ff1", 0, (16 * (part // 2) + 4 * i + u) * P)
            else:
                whole("w_ff2", 2 * KC * (part // 2) + KC * (u % 2), (2 * i + u // 2) * P)

    ATT_STEPS = (3, 5, 8, 10)
    STREAM = [("ada", 1, R_LAT), ("lat", 1, 7), ("att", 4, 4), ("oa", 2, 4), ("ssm", 8, 12), ("os", 4, 4),
              ("out", 2, 4)] + [(("ff", part), 4, 4) for part in range(4)]

    def used_up(phase, i, u):
        if phase in ("ada", "lat"):
            return (R_ADA if phase == "ada" else R_LAT) + u + 1
        if phase == "att":
            return G_ATT + 10 * i + ATT_STEPS[u]
        first = {"oa": G_OA, "ssm": G_SSM, "os": G_OS, "out": G_OUT}
        g = G_FF + 16 * phase[1] if isinstance(phase, tuple) else first[phase]
        return g + (12 if phase == "ssm" else 4) * i + u + 1

    def load_vector(eng, name):
        row, rows = VEC[name]
        eng.dma_start(uu[row:row + rows, 0, 0:P], a[name].rearrange("l (r n) -> (l r) n", n=P))\
           .then_inc(small_in, 16)

    @block.sync
    def _(sp):
        sp.dma_start(con[:, :], a["con"]).then_inc(small_in, 16)
        for name in list(VEC)[0::2]:
            load_vector(sp, name)
        for u in range(2):
            loads_of(sp, "ada", 0, u)
        sp.dma_start(x_tok_all, a["x"][0].rearrange("(b p) n -> p b n", p=P)).then_inc(x_in, 16)
        for u in range(2, RAW):
            loads_of(sp, "ada", 0, u)
        for n in range(ADA_BESIDE):
            sp.dma_start(beside[:, n, :].rearrange("p (k n) -> p k n", k=KC),
                         w_k["w_ada"][:, :, (R_LAT + n) * P:(R_LAT + n + 1) * P]).then_inc(beside_in, 16)
        for n, (phase, count, units) in enumerate(STREAM):
            following = STREAM[n + 1] if n + 1 < len(STREAM) else None

            def ahead(i, last, phase=phase, units=units, following=following):
                for u in range(units):
                    if u + RAW < units:
                        to = (phase, i, u + RAW)
                    elif not last:
                        to = (phase, i + 1, u + RAW - units)
                    elif following:
                        to = (following[0], 0, u + RAW - units)
                    else:
                        continue
                    sp.wait_ge(gemm_done, used_up(phase, i, u))
                    loads_of(sp, *to)

            if count == 1:
                ahead(0, True)
            else:
                last_peeled(sp, count, ahead)
        for c in range(KC):
            sp.wait_ge(fin_copy, c + 1)
            sp.dma_start(a["out"][0, :, c * P:(c + 1) * P].rearrange("(b p) n -> p b n", p=P),
                         ost[c % 4].rearrange("p (b n) -> p b n", b=TB)).then_inc(out_sent[c % 4], 16)
        for k in range(4):
            sp.wait_ge(out_sent[k], 16 * (KC // 4))

    class Unit:

        def __init__(self, r0, b0, i, r_per, b_per, ru, bu):
            assert r_per % RAW == 0 and b_per % 2 == 0
            self.slot = (r0 + ru) % RAW
            self.landed = 16 * (i * (r_per // RAW) + (r0 + ru) // RAW + 1)
            self.par = (b0 + bu) % 2
            self.b = b0 + bu + i * b_per

    def hi_of(act, unit):
        act.wait_ge(raw_in[unit.slot], unit.landed)
        act.activation(whi[:, unit.par, :], raw[:, unit.slot, :], ACT.Copy).then_inc(w_hi, 1)

    def lo_of(dve, unit):
        dve.wait_ge(w_hi, unit.b + 1)
        dve.tensor_tensor(wlo[:, unit.par, :], raw[:, unit.slot, :], whi[:, unit.par, :].bitcast(F32),
                          ALU.subtract).then_inc(w_lo, 1)

    def u_lat(bu):
        return Unit(R_LAT, B_LAT, 0, 4, 2, bu, bu)

    def u_att(i, bu):
        return Unit(R_ATT, B_ATT, i, 4, 4, bu, bu)

    def u_ssm(i, k):
        return Unit(R_SSM, B_SSM, i, 12, 8, SSM_UNITS[k] if k < 8 else 12 + k - 8, k)

    def u_run(r0, b0, per, i, bu):
        return Unit(r0, b0, i, per, per, bu, bu)

    def conv_chunk(i, k):
        return (SSM_IN // P + GROUPS + i, SSM_IN // P + i, 2 * i, 2 * i + 1)[k]

    def conv_dst(k):
        return (c_t[:, :], b_t[:, :], uu[:, 0, :], uu[:, 1, :])[k]

    def product(pe, out, pairs, first=True, last=True):
        n = 3 * len(pairs)
        k = 0
        for sh, sl, mh, ml in pairs:
            for s, m in ((sh, mh), (sh, ml), (sl, mh)):
                ins = pe.matmul(out, s, m, start=first and k == 0, stop=last and k == n - 1)
                k += 1
        return ins

    def weights(par, k, n=P):
        return whi[:, par, k * P:k * P + n], wlo[:, par, k * P:k * P + n]

    def gemm(pe, job, b, par, moving, first=True, last=True, ready=None):
        pe.wait_ge(w_lo, b + 1)
        if first:
            free_job(pe, job)
        for k in range(KC):
            if ready:
                ready(k)
            ins = product(pe, g_of(job)[:, :], [weights(par, k) + (moving[0][:, k, :], moving[1][:, k, :])],
                          first and k == 0, last and k == KC - 1)
        ins.then_inc(gemm_done, 1)

    def gemm_pair(pe, jobs, b, pars, base):
        for job in jobs:
            free_job(pe, job)
        pe.wait_ge(w_lo, b + 2)
        for k in range(KC):
            pe.wait_ge(nm_l, base + k + 1)
            for job, par in zip(jobs, pars):
                ins = product(pe, G[job.bank][:, :], [weights(par, k) + (ahi[:, k, :], alo[:, k, :])],
                              k == 0, k == KC - 1)
                if k == KC - 1:
                    ins.then_inc(gemm_done, 1)

    class Head:

        def __init__(self, i, e):
            self.e = e
            if i is None:
                self.h = e
                q, r1, r2, k, v = (Job(J_ATT, 0, 2, 5 * e + n) for n in range(5))
                self.kv, self.next_q = u_att(0, 2 * e + 1), u_att(0, 2 * e + 2)
            else:
                self.h = 2 * i + 2 + e
                q, r1, r2, k, _, v = (Job(J_TURNS, i, 12, 6 * e + n) for n in range(6))
                self.kv, self.next_q = u_att(i, 2 * e + 5), u_att(i, 2 * e + 6)
            self.q, self.r1, self.r2, self.k, self.v = q, r1, r2, k, v
            self.g = G_ATT + 5 * self.h
            loads = 1 + e if i is None else i + 2 + e
            self.rope = (rope_in[1 - e], ROPE_DMAS * loads)

    def attended(i, e):
        return Job(J_TURNS, i, 12, 6 * e + 4) if not (isinstance(i, int) and i == 3) \
            else Job(J_TURNS, 3, 12, e)

    class Job:

        def __init__(self, j0, i, per, k):
            assert per % 2 == 0
            self.bank = (j0 + k) % 2
            self.before = i * (per // 2) + (j0 + k) // 2

    def free_job(pe, job):
        wait(pe, g_free[job.bank], job.before)

    def g_of(job):
        return G[job.bank]

    def rms_pe(pe, r, rbank, sources, waits):
        for w in waits:
            pe.wait_ge(*w)
        for n, s in enumerate(sources):
            for tb in range(TB):
                ins = pe.matmul(rbank[:, tb:tb + 1], s[:, tb * P:(tb + 1) * P], ones[:, 0:1],
                                start=(n == 0 and tb == 0), stop=(n == len(sources) - 1),
                                skip_group_check=True)
        ins.then_inc(ssq_done, 1)

    def rms_rep(pe, r, rbank):
        pe.wait_ge(diag_done, 4 * r + 4)
        pe.matmul(rbank[:, :], ones, diag[:, :], start=True, stop=True).then_inc(rep_done, 1)

    def rms_mean(dve, r, rbank, n):
        dve.wait_ge(ssq_done, r + 1)
        dve.tensor_scalar(ms[:, :], rbank[:, 0:TB], 1.0 / n, EPS, ALU.mult, ALU.add).then_inc(ms_done, 1)

    def rms_diag(dve, r):
        wait(dve, rep_done, r)
        dve.wait_ge(rstd_done, r + 1)
        for tb in range(TB):
            dve.tensor_scalar(diag[:, tb * P:(tb + 1) * P], ident, rstd[:, tb:tb + 1], None, ALU.mult)\
               .then_inc(diag_done, 1)

    def rms_dve(dve, r, rbank, n):
        rms_mean(dve, r, rbank, n)
        rms_diag(dve, r)

    def rms_pool(pool, r):
        pool.wait_ge(ms_done, r + 1)
        pool.tensor_tensor(rstd[:, :], ms[:, :], minus_half[:, :], ALU.pow).then_inc(rstd_done, 1)

    def square_into(act, q, par, source):
        wait(act, sq_added, q - 1)
        act.activation(sq[:, par, :], source, ACT.Square).then_inc(sq_full, 1)

    def clear_sum(pool, n):
        wait(pool, ssq_done, n)
        pool.memset(ssum, 0.0).then_inc(sq_zero, 1)

    def add_square(pool, q, par, cleared=0):
        wait(pool, sq_zero, cleared)
        wait(pool, sq_added, q)
        pool.wait_ge(sq_full, q + 1)
        pool.tensor_tensor(ssum, ssum, sq[:, par, :], ALU.add).then_inc(sq_added, 1)

    def modulate_dve(dve, m, source, rbank, between=None):
        for c in range(KC):
            n = m * KC + c
            wait(dve, nm_u, n - 1)
            dve.tensor_tensor(tt[:, c % 2, :], source[:, c, :], rbank[:, :], ALU.mult).then_inc(nm_t, 1)
            if c:
                lo_mod(dve, n - 1, c - 1)
                if between:
                    between(c - 1)
        lo_mod(dve, m * KC + KC - 1, KC - 1)

    def lo_mod(dve, n, c):
        dve.wait_ge(nm_h, n + 1)
        dve.tensor_tensor(alo[:, c, :], uu[:, c % 2, :], ahi[:, c, :].bitcast(F32), ALU.subtract)\
           .then_inc(nm_l, 1)

    def modulate_act(act, m, gain, shift, between=None):
        for c in range(KC):
            n = m * KC + c
            act.wait_ge(nm_t, n + 1)
            wait(act, nm_l, n - 1)
            act.activation(uu[:, c % 2, :], tt[:, c % 2, :], ACT.Identity, scale=gain[:, c:c + 1],
                           bias=mod[:, shift + c:shift + c + 1]).then_inc(nm_u, 1)
            act.wait_ge(nm_u, n + 1)
            act.activation(ahi[:, c, :], uu[:, c % 2, :], ACT.Copy).then_inc(nm_h, 1)
            if between:
                between(c)

    @block.tensor
    def _(pe):
        pe.wait_ge(small_in, SMALL)
        pe.transpose(bank[7][:, 0:VEC_ROWS], vec_rows, ident[0:VEC_ROWS, 0:VEC_ROWS]).then_inc(vec_t, 1)
        pe.wait_ge(x_in, 16)
        for c in range(KC):
            wait(pe, sq_full, c - 3)
            for tb in range(TB):
                ins = pe.transpose(bank[1 + c % 4][:, tb * P:(tb + 1) * P],
                                   x_tok_all[:, tb, c * P:(c + 1) * P], ident)
            ins.then_inc(xt_full, 1)
        def beside_column(n):
            for k in range(KC):
                ins = pe.matmul(bank[5][:, R_LAT + n:R_LAT + n + 1], beside[:, n, k * P:(k + 1) * P],
                                silu_c[:, k:k + 1], start=(k == 0), stop=(k == KC - 1))
            if n == ADA_BESIDE - 1:
                ins.then_inc(beside_done, 1)

        for p in range(R_LAT // 2):
            pe.wait_ge(ada_step, KC * (p + 1))
            for u in (2 * p, 2 * p + 1):
                pe.matmul(bank[5][:, u:u + 1], raw[:, u % RAW, 0:P], ones[:, 0:1], start=True, stop=True)\
                  .then_inc(gemm_done, 1)
            if p == 1:
                pe.wait_ge(tables_in, TABLES)
                pe.wait_ge(silu_done, 1)
                pe.wait_ge(vec_c, 1)
                pe.transpose(bank[7][:, P:P + XBC // P], convb_rows, ident[0:XBC // P, 0:XBC // P])
                pe.transpose(bank[7][:, 2 * P:3 * P], convw_rows, ident).then_inc(vec_t, 1)
                pe.wait_ge(beside_in, 16 * ADA_BESIDE)
            if p == 2:
                rms_pe(pe, RMS_X, bank[0], [ssum], [(sq_added, KC)])
            if 1 <= p < 1 + ADA_BESIDE:
                beside_column(p - 1)
        rms_rep(pe, RMS_X, bank[0])

        h_act = (ahi, alo)
        gemm_pair(pe, [Job(J_LAT, 0, 2, k) for k in range(2)], B_LAT, (0, 1), 0)
        for k in range(2, 4):
            gemm(pe, Job(J_LAT, 0, 2, k), B_LAT + k, k % 2, h_act)
        rms_pe(pe, RMS_Q, bank[0], [sq[:, 0, :], sq[:, 1, :]], [(lat_sq, 2)])
        gemm(pe, Job(J_LAT, 0, 2, 4), B_LAT + 4, 0, h_act)
        rms_rep(pe, RMS_Q, bank[0])
        rms_pe(pe, RMS_KV, bank[1], [tt[:, 0, :], tt[:, 1, :]], [(lat_sq, 4)])
        gemm(pe, Job(J_LAT, 0, 2, 5), B_LAT + 5, 1, h_act)
        rms_rep(pe, RMS_KV, bank[1])
        pe.wait_ge(w_lo, B_LAT + 7)
        job = Job(J_LAT, 0, 2, 6)
        free_job(pe, job)
        product(pe, g_of(job)[0:SH, :], [weights(0, k, SH) + (ahi[:, k, :], alo[:, k, :])
                                         for k in range(KC)]).then_inc(gemm_done, 1)

        pe.wait_ge(lat_l, 4)
        pe.wait_ge(kr_v, 2)
        pe.sem_inc(pv_done, 2)

        Q_PAR, KV_PAR = B_ATT % 2, (B_ATT + 1) % 2

        def queries_keys(x):
            pe.wait_ge(w_lo, B_ATT + 2 * x.h + 1)
            for k, job in enumerate((x.q, x.r1, x.r2)):
                free_job(pe, job)
                pairs = [(whi[:, Q_PAR, c * 3 * P + k * P:c * 3 * P + (k + 1) * P],
                          wlo[:, Q_PAR, c * 3 * P + k * P:c * 3 * P + (k + 1) * P],
                          lathi[:, c, :], latlo[:, c, :]) for c in range(2)]
                product(pe, g_of(job)[:, :], pairs).then_inc(gemm_done, 1)
            pe.wait_ge(w_lo, B_ATT + 2 * x.h + 2)
            free_job(pe, x.k)
            pairs = [(whi[:, KV_PAR, c * 2 * P:c * 2 * P + P], wlo[:, KV_PAR, c * 2 * P:c * 2 * P + P],
                      lathi[:, 2 + c, :], latlo[:, 2 + c, :]) for c in range(2)]
            product(pe, g_of(x.k)[:, :], pairs).then_inc(gemm_done, 1)

        def head_values(x):
            free_job(pe, x.v)
            for tb in range(TB):
                pairs = [(lathi[:, 2 + c, tb * P:(tb + 1) * P], latlo[:, 2 + c, tb * P:(tb + 1) * P],
                          whi[:, KV_PAR, c * 2 * P + P:(c + 1) * 2 * P],
                          wlo[:, KV_PAR, c * 2 * P + P:(c + 1) * 2 * P]) for c in range(2)]
                ins = product(pe, g_of(x.v)[:, tb * P:(tb + 1) * P], pairs)
            ins.then_inc(gemm_done, 1)

        def scores(x):
            pe.wait_ge(proj_l, x.h + 1)
            for job in (x.r2, x.k):
                pe.wait_ge(g_free[job.bank], job.before + 1)
            for qb in range(TB):
                n = (qb + 1) * P
                pe.wait_ge(s_exp, 4 * x.h + qb + 1)
                out = bank[qb][:, 0:n]
                blk = slice(qb * P, n)
                product(pe, out, [(qn_hi[:, x.e, blk], qn_lo[:, x.e, blk], kn_hi[:, x.e, 0:n],
                                   kn_lo[:, x.e, 0:n])], last=False)
                pe.matmul(out, q_rope[:, x.e, blk], kr_hi[:, 0:n], start=False, stop=False)
                pe.matmul(out, q_rope[:, x.e, blk], kr_lo[:, 0:n], start=False, stop=True)\
                  .then_inc(s_full, 1)

        def turn(h, e, j):
            if j == 0:
                pe.wait_ge(p_norm, 4 * h + 4)
            pe.wait_ge(pt_l, 4 * h + j + 1)
            for qb in range(j, TB):
                ins = pe.transpose(bank[4 + j % 2][:, qb * P:(qb + 1) * P],
                                   probs[:, e, qb, j * P:(j + 1) * P], ident)
            ins.then_inc(pt_full, 1)

        def attend_values(h, e, j, job, v_split):
            pe.wait_ge(pt_l, 4 * h + j + 3)
            if j == 0:
                v_split()
                free_job(pe, job)
            kb = slice(j * P, (j + 1) * P)
            product(pe, g_of(job)[:, j * P:T],
                    [(v_hi[:, e, kb], v_lo[:, e, kb], pthi[:, j % 2, j * P:T],
                      ptlo[:, j % 2, j * P:T])], first=(j == 0), last=(j == TB - 1)).then_inc(pv_done, 1)

        for e in range(2):
            x = Head(None, e)
            queries_keys(x)
            head_values(x)
            if e:
                turn(0, 0, 0)
                turn(0, 0, 1)
            pe.wait_ge(g_free[x.v.bank], x.v.before + 1)
            scores(x)

        def attend(i, e, x):
            h, job = 2 * i + e, attended(i, e)

            def v_split():
                v = Job(J_TURNS, i, 12, 6 * e + 5 - 12)
                pe.wait_ge(g_free[v.bank], v.before + 1)

            if x:
                queries_keys(x)
            attend_values(h, e, 0, job, v_split)
            turn(h, e, 2)
            attend_values(h, e, 1, job, v_split)
            turn(h, e, 3)
            if x:
                head_values(x)
            attend_values(h, e, 2, job, v_split)
            attend_values(h, e, 3, job, v_split)
            if x or e == 0:
                turn(h + 1, 1 - e, 0)
                turn(h + 1, 1 - e, 1)
            if x:
                scores(x)

        with pe.Fori(0, HEADS // 2 - 1) as i:
            for e in range(2):
                attend(i, e, Head(i, e))
        for e in range(2):
            attend(HEADS // 2 - 1, e, None)

        pe.wait_ge(dt_copied, 1)
        for ch in range(TB):
            ins = pe.transpose(bank[2][:, 3 * P + ch * SH:3 * P + (ch + 1) * SH],
                               dt_feat[:, ch * P:(ch + 1) * P], ident[0:SH, 0:SH])
        ins.then_inc(dt_tok, 1)

        def heads_split(k):
            if k >= HEADS - 2:
                final = attended(3, k - (HEADS - 2))
                pe.wait_ge(g_free[final.bank], final.before + 1)

        def oa(i, last):
            for k in range(4):
                gemm(pe, Job(J_OA, i, 4, k), B_OA + 4 * i + k, (B_OA + k) % 2,
                     (fhi[:, 0:KC, :], flo[:, 0:KC, :]), ready=heads_split if i == 0 and k == 0 else None)

        oa(0, False)
        pe.wait_ge(dt_v, 3)
        for n, left in enumerate((tri, strict, ones)):
            for ch in range(TB):
                ins = pe.matmul(bank[2][:, n * P + ch * SH:n * P + (ch + 1) * SH], left,
                                dta[:, ch * SH:(ch + 1) * SH], start=True, stop=True)
        ins.then_inc(dt_mm, 1)
        oa(1, True)

        pe.sem_inc(seg_done, 1)
        pe.sem_inc(yd_done, 2)
        pe.sem_inc(yt_done, 1)

        def projection(i, k, start, end):
            job, par = Job(J_SSM, i, 8, k), (B_SSM + k) % 2
            if start == 0:
                pe.wait_ge(w_lo, B_SSM + 8 * i + k + 1)
                free_job(pe, job)
            ins = product(pe, g_of(job)[:, :], [weights(par, c) + (ahi[:, c, :], alo[:, c, :])
                                                for c in range(start, end)], start == 0, end == KC)
            if end == KC:
                ins.then_inc(gemm_done, 1)

        projection(0, 0, 0, KC // 2)

        def group(i, last):
            def blk(k, start=0, end=KC):
                projection(i, k, start, end)

            def ada(j):
                unit = Unit(R_SSM, 0, i, 12, 0, ADA_UNITS[j], 0)
                pe.wait_ge(ada_sum, 4 * i + j + 1)
                if j == 0:
                    pe.wait_ge(ada_out, i + 1)
                    pe.wait_ge(h_done, 3 * i + 1)
                elif j == 3:
                    pe.wait_ge(h_done, 3 * i + 4)
                pe.matmul(bank[3][:, GF + j:GF + j + 1], raw[:, unit.slot, 0:P], ones[:, 0:1],
                          start=True, stop=True).then_inc(gemm_done, 1)

            def turn_in(n, source, to, conv):
                pe.wait_ge(cv_out, 2 + 4 * i + conv + 1)
                for ch in range(TB):
                    ins = pe.transpose(to[:, ch * P:(ch + 1) * P], source[:, ch * P:(ch + 1) * P], ident)
                ins.then_inc(tin_done, 1)

            def decays(ch):
                n = 4 * i + ch
                blk_ = slice(ch * P, (ch + 1) * P)
                pe.wait_ge(cbm_done, n + 1)
                if ch == 0:
                    pe.wait_ge(yg_l, 2 * i + 1)
                pe.matmul(bank[1][:, 0:P], b_t[:, blk_], c_t[:, blk_], start=True, stop=True)\
                  .then_inc(cb_done, 1)
                pe.wait_ge(rm_done, n + 1)
                pe.wait_ge(e_done, n + 1)
                pe.matmul(bank[0][:, :], strict_r[:, :], rm_hi[:, :], start=True, stop=False)
                pe.matmul(bank[0][:, :], strict_r[:, :], rm_lo[:, :], start=False, stop=True)\
                  .then_inc(seg_done, 1)

            def outputs(ch):
                n = 4 * i + ch
                pe.wait_ge(y_done, n + 1)
                if ch:
                    pe.wait_ge(h_done, 3 * i + ch + 1)
                    pe.matmul(bank[2][:, 0:GF], c_t[:, ch * P:(ch + 1) * P], state[:, :],
                              start=True, stop=True)
                pe.wait_ge(m_done, n + 2)
                pe.wait_ge(xd_done, n + 1)
                for h in range(GH):
                    ins = pe.matmul(bank[2][:, GF + h * HD:GF + (h + 1) * HD],
                                    sq[:, ch % 2, h * P:(h + 1) * P], xdt[:, h * HD:(h + 1) * HD],
                                    start=True, stop=True)
                ins.then_inc(yd_done, 1)
                if ch < TB - 1:
                    pe.wait_ge(h_done, 3 * i + ch + 1)
                    pe.matmul(bank[3][:, 0:GF], b_tok[:, ch * P:(ch + 1) * P], xend[:, :],
                              start=True, stop=True).then_inc(s_done, 1)

            def turn_y(ch):
                pe.wait_ge(y_done, 4 * i + ch + 2)
                if ch == 0:
                    pe.wait_ge(tin_copied, 3 * i + 3)
                for f in range(2):
                    ins = pe.transpose(bank[4 + f][:, ch * P:(ch + 1) * P], y[:, f * P:(f + 1) * P], ident)
                ins.then_inc(yt_done, 1)

            blk(0, KC // 2)
            blk(1)
            blk(2)
            pe.wait_ge(gt_done, 2 * i + 1)
            turn_in(0, b_t, bank[4], 1)
            ada(0)
            blk(3)
            decays(0)
            blk(4)
            turn_in(1, uu[:, 0, :], bank[5], 2)
            pe.wait_ge(tin_copied, 3 * i + 1)
            turn_in(2, uu[:, 1, :], bank[4], 3)
            ada(1)
            decays(1)
            blk(5)
            ada(2)
            pe.wait_ge(tin_copied, 3 * i + 3)
            outputs(0)
            decays(2)
            blk(6, 0, 4)
            turn_y(0)
            outputs(1)
            decays(3)
            blk(6, 4)
            turn_y(1)
            outputs(2)
            blk(7, 0, 2)
            turn_y(2)
            outputs(3)
            blk(7, 2, 4)
            turn_y(3)
            blk(7, 4)
            rms_pe(pe, None, bank[1], [sq[:, 0, :], sq[:, 1, :]], [(gsq_done, 2 * i + 2)])
            ada(3)
            if not last:
                projection(i + 1, 0, 0, KC // 2)
            rms_rep(pe, RMS_G + i, bank[1])

        last_peeled(pe, GROUPS, group)

        def os_(i, first=False):
            for c in range(2):
                job = Job(J_OS, i, 2, c)
                for half in range(2):
                    k = 2 * c + half

                    def gated(n, half=half):
                        pe.wait_ge(yg_l, 1 + KC * half + n + 1)

                    gemm(pe, job, B_OS + 4 * i + k, (B_OS + k) % 2,
                         (fhi[:, KC * half:KC * (half + 1), :], flo[:, KC * half:KC * (half + 1), :]),
                         first=(half == 0), last=(half == 1), ready=gated if first and c == 0 else None)

        os_(0, True)
        with pe.Fori(1, 4) as i:
            os_(i)

        def merged(n):
            pe.wait_ge(mg_l, 1 + n + 1)

        for i in range(2):
            for k in range(4):
                gemm(pe, Job(J_OUT, i, 4, k), B_OUT + 4 * i + k, (B_OUT + k) % 2, h_act,
                     ready=merged if i == 0 and k == 0 else None)
        rms_pe(pe, RMS_MIX, bank[0], [ssum], [(sq_added, 2 * KC)])
        rms_rep(pe, RMS_MIX, bank[0])
        rms_pe(pe, RMS_MLP, bank[1], [ssum], [(sq_added, 3 * KC)])
        rms_rep(pe, RMS_MLP, bank[1])

        gemm_pair(pe, [Job(J_FF, 0, 4, k) for k in range(2)], B_FF, (B_FF % 2, 1 - B_FF % 2), KC)
        for half in range(2):
            b0 = B_FF + 32 * half
            j0 = J_FF + J_HALF * half

            def up(i, k0=0, b0=b0, j0=j0):
                for k in range(k0, 4):
                    gemm(pe, Job(j0, i, 4, k), b0 + 4 * i + k, (b0 + k) % 2, h_act)

            up(0, 0 if half else 2)
            with pe.Fori(1, 4) as i:
                up(i)

            def down(i, first=False, b0=b0 + 16, j0=j0 + 16, half=half):
                for c in range(2):
                    job = Job(j0, i, 2, c)
                    for part in range(2):
                        k = 2 * c + part

                        def hidden(n, part=part):
                            pe.wait_ge(ff_l, 1 + 16 * half + KC * part + n + 1)

                        gemm(pe, job, b0 + 4 * i + k, (b0 + k) % 2,
                             (fhi[:, KC * part:KC * (part + 1), :], flo[:, KC * part:KC * (part + 1), :]),
                             first=(part == 0), last=(part == 1), ready=hidden if first and c == 0 else None)

            down(0, True)
            with pe.Fori(1, 4) as i:
                down(i)
        rms_pe(pe, RMS_FF, bank[0], [ssum], [(sq_added, 4 * KC)])
        rms_rep(pe, RMS_FF, bank[0])
        for c in range(KC):
            pe.wait_ge(fin_done[c % 2], c // 2 + 1)
            wait(pe, fin_copy, c - 1)
            for tb in range(TB):
                ins = pe.transpose(bank[2 + c % 2][:, tb * P:(tb + 1) * P],
                                   buf2[:, c, tb * P:(tb + 1) * P], ident)
            ins.then_inc(fin_tr, 1)


    @block.scalar
    def _(act):
        act.sem_inc(s_exp, 4)
        act.sem_inc(e_done, 1)
        for name in list(VEC)[1::2]:
            load_vector(act, name)
        act.dma_start(convb_rows, a["conv_b"].rearrange("l (r n) -> (l r) n", n=P)).then_inc(tables_in, 16)
        act.dma_start(convw_rows, a["conv_w"].rearrange("l k (r n) -> (l k r) n", n=P))\
           .then_inc(tables_in, 16)
        for dst, name in ((dt_bias, "dt_bias"), (a_log, "a_log"), (d_half, "d_skip")):
            act.dma_start(dst[:, :], a[name].broadcast_to([P, SH])).then_inc(tables_in, 16)
        act.wait_ge(vec_t, 1)
        row, rows = VEC["c"]
        act.activation(silu_c[:, :], bank[7][:, row:row + rows], ACT.Silu).then_inc(silu_done, 1)
        act.activation(vec[:, :], bank[7][:, 0:VEC_ROWS], ACT.Copy).then_inc(vec_c, 1)
        for c in range(KC):
            act.wait_ge(xt_full, c + 1)
            act.activation(xt[:, c, :], bank[1 + c % 4][:, :], ACT.Copy).then_inc(xt_copied, 1)
            square_into(act, c, c % 2, bank[1 + c % 4][:, :])
        act.wait_ge(vec_t, 2)
        act.activation(convb[:, :], bank[7][:, P:P + XBC // P], ACT.Copy).then_inc(vec_c, 1)
        act.activation(convw[:, :], bank[7][:, 2 * P:3 * P], ACT.Copy).then_inc(vec_c, 1)
        act.wait_ge(setup, 4)
        act.wait_ge(xt_copied, KC)
        act.dma_start(xt_dram, buf2[:, :, :].rearrange("p k n -> p (k n)")).then_inc(stash, 16)

        def first_units(c):
            if c < 2:
                hi_of(act, u_lat(c))

        modulate_act(act, 0, g_mix, 0, first_units)
        act.wait_ge(stash, 16)
        act.wait_ge(nm_l, KC)
        act.dma_start(pos_i, a["positions"].broadcast_to([P, T])).then_inc(pos_in, 16)

        for k in range(4):
            job = Job(J_LAT, 0, 2, k)
            act.wait_ge(gemm_done, G_LAT + k + 1)
            if k == 0:
                act.wait_ge(sq_added, KC)
            act.activation(sq[:, k, :] if k < 2 else tt[:, k - 2, :], g_of(job)[:, :], ACT.Square)\
               .then_inc(lat_sq, 1)
            act.activation(lat[:, k, :], g_of(job)[:, :], ACT.Copy).then_inc(g_free[job.bank], 1)
            if k == 2:
                act.wait_ge(krope_in, 16 * 4)
            hi_of(act, u_lat(k + 2))
        act.wait_ge(setup, 4 + SET_TRIG)
        act.activation(sin, sin, ACT.Sin).then_inc(trig, 1)
        act.activation(cos, cos, ACT.Sin).then_inc(trig, 1)
        act.wait_ge(gemm_done, G_LAT + 5)
        hi_of(act, u_lat(6))
        for k in range(4):
            if k == 2:
                act.wait_ge(gemm_done, G_LAT + 6)
                act.wait_ge(rope_in[0], ROPE_DMAS)
                hi_of(act, u_att(0, 0))
            act.wait_ge(lat_u, k + 1)
            act.activation(lathi[:, k, :], uu[:, k % 2, :], ACT.Copy).then_inc(lat_h, 1)
        act.wait_ge(kr_v, 1)
        act.activation(kr_hi, rope1, ACT.Copy).then_inc(kr_h, 1)
        job = Job(J_LAT, 0, 2, 6)
        act.wait_ge(gemm_done, G_LAT + 7)
        act.wait_ge(ssq_done, RMS_KV + 1)
        act.activation(dt_feat, g_of(job)[0:SH, :], ACT.Copy).then_inc(g_free[job.bank], 1)
        act.wait_ge(g_free[job.bank], job.before + 1)
        act.sem_inc(dt_copied, 1)

        def queries_keys(x, rope):
            act.wait_ge(gemm_done, x.g + 1)
            act.activation(qn_hi[:, x.e, :], g_of(x.q)[:, :], ACT.Copy).then_inc(proj_h, 1)
            hi_of(act, x.kv)
            act.wait_ge(gemm_done, x.g + 3)
            if rope:
                act.wait_ge(*x.rope)
            hi_of(act, x.next_q)
            act.wait_ge(rot, x.h + 1)
            act.activation(q_rope[:, x.e, :], rope1, ACT.Copy).then_inc(proj_h, 1)
            act.wait_ge(gemm_done, x.g + 4)
            act.activation(kn_hi[:, x.e, :], g_of(x.k)[:, :], ACT.Copy).then_inc(proj_h, 1)

        def head_values(x):
            act.wait_ge(gemm_done, x.g + 5)
            act.activation(v_hi[:, x.e, :], g_of(x.v)[:, :], ACT.Copy).then_inc(proj_h, 1)

        def exps(x):
            for qb in range(TB):
                n, c = (qb + 1) * P, x.e * TB + qb
                act.wait_ge(s_neg, 4 * x.h + qb + 1)
                act.activation(probs[:, x.e, qb, 0:n], bank[qb][:, 0:n], ACT.Exp, scale=SCALE,
                               bias=negmax[:, c:c + 1], accum_out=rowsum[:, c:c + 1]).then_inc(s_exp, 1)

        def turned(h, j):
            act.wait_ge(pt_full, 4 * h + j + 1)
            act.wait_ge(pv_done, 4 * h + j + 1)
            act.activation(pthi[:, j % 2, j * P:T], bank[4 + j % 2][:, j * P:T], ACT.Copy)\
               .then_inc(pt_h, 1)

        def attend(i, e, x, rope):
            h = 2 * i + e
            if x:
                queries_keys(x, rope)
            turned(h, 2)
            turned(h, 3)
            act.wait_ge(pv_done, 2 + 4 * h + 4)
            act.activation(at(fhi, h), g_of(attended(i, e))[:, :], ACT.Copy).then_inc(o_h, 1)
            if x:
                head_values(x)
            if x or e == 0:
                turned(h + 1, 0)
                turned(h + 1, 1)
            if x:
                exps(x)

        for e in range(2):
            x = Head(None, e)
            queries_keys(x, True)
            head_values(x)
            if e:
                turned(0, 0)
                turned(0, 1)
            exps(x)

        def att(i, last):
            for e in range(2):
                attend(i, e, Head(i, e), not (last and e == 1))

        last_peeled(act, HEADS // 2 - 1, att)
        for e in range(2):
            attend(HEADS // 2 - 1, e, None, False)
            if e == 0:
                hi_of(act, u_run(R_OA, B_OA, 4, 0, 1))

        act.activation(a_log[:, :], a_log[:, :], ACT.Exp).then_inc(dt_a, 1)
        act.wait_ge(dt_v, 1)
        act.activation(dtneg, dtneg, ACT.Exp).then_inc(dt_a, 1)
        act.wait_ge(dt_a, 2)
        act.activation(dtneg, dtneg, ACT.Ln, bias=1.0).then_inc(dt_a, 1)

        def oa(i, last):
            for k in range(4):
                job = Job(J_OA, i, 4, k)
                act.wait_ge(gemm_done, G_OA + 4 * i + k + 1)
                act.activation(at(buf1, 4 * i + k), g_of(job)[:, :], ACT.Copy, scale=0.5)\
                   .then_inc(g_free[job.bank], 1)
                hi_of(act, u_run(R_OA, B_OA, 4, i, k + 2))

        oa(0, False)
        act.wait_ge(dt_mm, 1)
        act.activation(decay[:, :, :].rearrange("p a n -> p (a n)"), bank[2][:, 0:3 * P], ACT.Exp)\
           .then_inc(dt_a, 1)
        oa(1, True)

        def group(i, last):
            def stream(k):
                act.wait_ge(gemm_done, G_SSM + 12 * i + SSM_UNITS[k] + 1)
                return Job(J_SSM, i, 8, k)

            def refill(k):
                hi_of(act, u_ssm(i, k + 2))

            def conv(k):
                v = 4 * i + k
                cc = conv_chunk(i, k)
                job = stream(k)
                act.wait_ge(cv_out, v + 1)
                act.activation(tt[:, k % 2, :], g_of(job)[:, :], ACT.Identity,
                               scale=cols(convw, (TAPS - 1) * (XBC // P) + cc, 1),
                               bias=cols(convb, cc, 1)).then_inc(cv_acc, 1)
                refill(k)
                act.wait_ge(g_free[job.bank], job.before + 1)
                if k == 2:
                    act.wait_ge(yg_l, 2 * i + 1)
                act.activation(conv_dst(k), tt[:, k % 2, :], ACT.Tanh, scale=0.5).then_inc(cv_tanh, 1)

            def copy_in(n, dst, src):
                act.wait_ge(tin_done, 3 * i + n + 1)
                act.activation(dst, src, ACT.Copy).then_inc(tin_copied, 1)

            def exp_decay(ch):
                n = 4 * i + ch
                act.wait_ge(seg_done, n + 2)
                act.wait_ge(yd_done, n + 1)
                act.activation(sq[:, ch % 2, :], bank[0][:, :], ACT.Exp).then_inc(e_done, 1)

            def z_gate(f):
                job = stream(4 + f)
                act.activation(zs[:, f, :], g_of(job)[:, :], ACT.Tanh, scale=0.5).then_inc(z_tanh, 1)

            conv(0)
            conv(1)
            conv(2)
            copy_in(0, b_tok[:, :], bank[4][:, :])
            conv(3)
            exp_decay(0)
            z_gate(0)
            copy_in(1, x_tok[:, :, 0:P], bank[5][:, :].rearrange("p (a n) -> p a n", a=TB))
            copy_in(2, x_tok[:, :, P:GF], bank[4][:, :].rearrange("p (a n) -> p a n", a=TB))
            exp_decay(1)
            refill(4)
            z_gate(1)
            exp_decay(2)
            refill(5)
            exp_decay(3)
            job = stream(6)
            act.activation(uu[:, 0, :], g_of(job)[:, :], ACT.Tanh, scale=0.5).then_inc(g_free[job.bank], 1)
            refill(6)
            for f in range(2):
                act.wait_ge(gt_done, 2 * i + f + 2)
                act.activation(sq[:, f, :], zs[:, f, :], ACT.Square).then_inc(gsq_done, 1)
            job = stream(7)
            act.activation(at(buf2, i), g_of(job)[:, :], ACT.Tanh, scale=0.5).then_inc(g_free[job.bank], 1)
            refill(7)
            for f in range(2):
                act.wait_ge(yg_u, 2 * i + f + 1)
                act.activation(at(fhi, 2 * i + f), uu[:, f, :], ACT.Copy).then_inc(yg_h, 1)

        last_peeled(act, GROUPS, group)

        def os_(i, last):
            for c in range(2):
                for half in range(2):
                    k = 2 * c + half
                    act.wait_ge(gemm_done, G_OS + 4 * i + k + 1)
                    hi_of(act, u_run(R_OS, B_OS, 4, i, k + 2))
                act.wait_ge(mg_u, 2 * i + c + 1)
                act.activation(at(ahi, 2 * i + c), uu[:, c, :], ACT.Copy).then_inc(mg_h, 1)

        last_peeled(act, 4, os_)
        act.wait_ge(mg_l, 1 + KC)
        act.dma_start(buf1[:, :, :].rearrange("p k n -> p (k n)"), xt_dram).then_inc(xt_in, 16)

        def out_(i, last):
            for k in range(4):
                c = 4 * i + k
                job = Job(J_OUT, i, 4, k)
                act.wait_ge(gemm_done, G_OUT + c + 1)
                square_into(act, KC + c, k % 2, g_of(job)[:, :])
                act.activation(at(buf2, c), g_of(job)[:, :], ACT.Copy).then_inc(g_free[job.bank], 1)
                hi_of(act, u_run(R_OUT, B_OUT, 4, i, k + 2))

        last_peeled(act, 2, out_)
        for c in range(KC):
            act.wait_ge(x1_done, c + 1)
            square_into(act, 2 * KC + c, c % 2, buf1[:, c, :])
        modulate_act(act, 1, g_mlp, 24)

        for half in range(2):
            r0, b0, g0, j0 = R_FF + 32 * half, B_FF + 32 * half, G_FF + 32 * half, J_FF + J_HALF * half

            def up(i, last, r0=r0, b0=b0, g0=g0, j0=j0, half=half):
                for k in range(4):
                    f = 16 * half + 4 * i + k
                    job = Job(j0, i, 4, k)
                    act.wait_ge(gemm_done, g0 + 4 * i + k + 1)
                    act.wait_ge(ff_q, f + 1)
                    act.activation(tt[:, k % 2, :], g_of(job)[:, :], ACT.Relu).then_inc(g_free[job.bank], 1)
                    hi_of(act, u_run(r0, b0, 4, i, k + 2))
                    act.wait_ge(ff_q, f + 2)
                    act.activation(at(fhi, 4 * i + k), uu[:, k % 2, :], ACT.Copy).then_inc(ff_h, 1)

            last_peeled(act, 4, up)

            def down(i, last, r0=r0 + 16, b0=b0 + 16, g0=g0 + 16, j0=j0 + 16, half=half):
                for c in range(2):
                    job = Job(j0, i, 2, c)
                    for part in range(2):
                        k = 2 * c + part
                        act.wait_ge(gemm_done, g0 + 4 * i + k + 1)
                        if not (half == 1 and last and k >= 2):
                            hi_of(act, u_run(r0, b0, 4, i, k + 2))
                    if half == 0:
                        act.activation(at(buf2, 2 * i + c), g_of(job)[:, :], ACT.Copy)\
                           .then_inc(g_free[job.bank], 1)
                    else:
                        act.wait_ge(g_free[job.bank], job.before + 1)
                        square_into(act, 3 * KC + 2 * i + c, c % 2, at(buf2, 2 * i + c))

            last_peeled(act, 4, down)
        for c in range(KC):
            act.wait_ge(fin_tr, c + 1)
            if c >= 4:
                act.wait_ge(out_sent[c % 4], 16 * (c // 4))
            act.activation(ost[c % 4], bank[2 + c % 2][:, :], ACT.Copy).then_inc(fin_copy, 1)

    @block.vector
    def _(dve):
        dve.sem_inc(pt_l, 2)
        dve.sem_inc(cv_out, 2)
        for s in (ada_out, cbm_done, m_done, h_done, y_done, gt_done, yg_l, mg_l, ff_l):
            dve.sem_inc(s, 1)
        dve.wait_ge(small_in, SMALL)
        dve.tensor_copy(strict_r[:, :], strict).then_inc(setup, 1)
        dve.wait_ge(silu_done, 1)

        def ada_pair(p):
            pair = raw[:, 2 * (p % 2):2 * (p % 2) + 2, :]
            for k in range(2):
                dve.wait_ge(raw_in[2 * (p % 2) + k], 16 * (p // 2 + 1))
            total = pair[:, :, 0:P]
            for k in range(KC):
                if k:
                    dve.wait_ge(ada_step, KC * p + k)
                    ins = dve.scalar_tensor_tensor(total, pair[:, :, k * P:(k + 1) * P], silu_c[:, k:k + 1],
                                                   total, ALU.mult, ALU.add)
                else:
                    ins = dve.tensor_scalar(total, total, silu_c[:, 0:1], None, ALU.mult)
                ins.then_inc(ada_step, 1)

        for p in range(3):
            ada_pair(p)
        rms_mean(dve, RMS_X, bank[0], D)
        for p in range(3, R_LAT // 2):
            ada_pair(p)
        rms_diag(dve, RMS_X)
        dve.wait_ge(vec_c, 1)
        dve.tensor_scalar(d_half[:, :], d_half[:, :], 0.5, None, ALU.mult).then_inc(setup, 1)
        dve.wait_ge(gemm_done, G_LAT)
        dve.wait_ge(beside_done, 1)
        dve.tensor_tensor(mod[:, 0:16], bank[5][:, 0:16], vec[:, 0:16], ALU.add).then_inc(setup, 1)
        dve.wait_ge(setup, 3)
        row = VEC["g_pre_mix"][0]
        dve.scalar_tensor_tensor(g_mix[:, :], mod[:, 8:16], 1.0, vec[:, row:row + 8], ALU.add, ALU.mult)\
           .then_inc(setup, 1)
        dve.wait_ge(xt_copied, KC)
        dve.wait_ge(rep_done, RMS_X + 1)

        def first_units(c):
            if c < 2:
                lo_of(dve, u_lat(c))

        modulate_dve(dve, 0, xt, bank[0], first_units)

        step = [4]

        def chain(ins):
            ins.then_inc(setup, 1)
            step[0] += 1
            dve.wait_ge(setup, step[0])

        def reduced(out, quarter):
            turns = rope2
            chain(dve.tensor_scalar(turns, rope1, 1.0 / (2 * np.pi), quarter, ALU.mult, ALU.add))
            chain(dve.tensor_scalar(turns, turns, MAGIC, -MAGIC, ALU.add, ALU.add))
            chain(dve.scalar_tensor_tensor(out, turns, -TWO_PI_1, rope1, ALU.mult, ALU.add))
            chain(dve.scalar_tensor_tensor(out, turns, -TWO_PI_2, out, ALU.mult, ALU.add))
            chain(dve.scalar_tensor_tensor(out, turns, -TWO_PI_3, out, ALU.mult, ALU.add))
            chain(dve.tensor_scalar(out, out, quarter * 2 * np.pi, PI_IN, ALU.add, ALU.min))
            chain(dve.tensor_scalar(out, out, -PI_IN, None, ALU.max))

        lo_of(dve, u_lat(2))
        dve.wait_ge(pos_in, 16)
        chain(dve.tensor_copy(rope2, pos_i))
        chain(dve.tensor_scalar(rope1, rope2, con[:, CON_FREQ:CON_FREQ + 1], None, ALU.mult))
        lo_of(dve, u_lat(3))
        reduced(sin, 0.0)
        lo_of(dve, u_lat(4))
        reduced(cos, 0.25)
        assert step[0] == 4 + SET_TRIG
        rms_dve(dve, RMS_Q, bank[0], RANK)
        lo_of(dve, u_lat(5))
        dve.wait_ge(trig, 2)
        chain(dve.tensor_scalar(sin, sin, con[:, CON_SIGN:CON_SIGN + 1], None, ALU.mult))

        job = Job(J_LAT, 0, 2, 4)
        dve.wait_ge(gemm_done, G_LAT + 5)
        dve.tensor_tensor(rope1, g_of(job)[:, :], cos, ALU.mult).then_inc(g_free[job.bank], 1)

        def latents(k0, gain, rbank, r):
            dve.wait_ge(rep_done, r + 1)
            row = VEC[gain][0]
            for k in range(k0, k0 + 2):
                wait(dve, lat_l, k - 1)
                dve.scalar_tensor_tensor(uu[:, k % 2, :], lat[:, k, :], vec[:, row + k - k0:row + k - k0 + 1],
                                         rbank[:, :], ALU.mult, ALU.mult).then_inc(lat_u, 1)
            for k in range(k0, k0 + 2):
                dve.wait_ge(lat_h, k + 1)
                dve.tensor_tensor(latlo[:, k, :], uu[:, k % 2, :], lathi[:, k, :].bitcast(F32),
                                  ALU.subtract).then_inc(lat_l, 1)

        rms_mean(dve, RMS_KV, bank[1], RANK)
        latents(0, "g_q_lat", bank[0], RMS_Q)
        rms_diag(dve, RMS_KV)
        lo_of(dve, u_lat(6))
        job = Job(J_LAT, 0, 2, 5)
        dve.wait_ge(gemm_done, G_LAT + 6)
        dve.tensor_tensor(rope2, g_of(job)[:, :], sin, ALU.mult).then_inc(g_free[job.bank], 1)
        dve.wait_ge(g_free[1], 3)
        dve.wait_ge(g_free[0], 3)
        dve.tensor_tensor(rope1, rope1, rope2, ALU.add).then_inc(kr_v, 1)
        lo_of(dve, u_att(0, 0))
        latents(2, "g_kv_lat", bank[1], RMS_KV)
        dve.wait_ge(kr_h, 1)
        dve.tensor_tensor(kr_lo, rope1, kr_hi.bitcast(F32), ALU.subtract).then_inc(kr_v, 1)

        def low(x, dst, job, hi, n):
            dve.wait_ge(proj_h, 4 * x.h + n)
            dve.tensor_tensor(dst, g_of(job)[:, :], hi.bitcast(F32), ALU.subtract)\
               .then_inc(g_free[job.bank], 1)

        def queries_keys(x):
            low(x, qn_lo[:, x.e, :], x.q, qn_hi[:, x.e, :], 1)
            dve.wait_ge(gemm_done, x.g + 2)
            dve.tensor_tensor(rope1, g_of(x.r1)[:, :], cos, ALU.mult).then_inc(g_free[x.r1.bank], 1)
            lo_of(dve, x.kv)
            dve.wait_ge(gemm_done, x.g + 3)
            dve.tensor_tensor(rope2, g_of(x.r2)[:, :], sin, ALU.mult).then_inc(g_free[x.r2.bank], 1)
            dve.wait_ge(g_free[x.r1.bank], x.r1.before + 1)
            dve.wait_ge(g_free[x.r2.bank], x.r2.before + 1)
            dve.tensor_tensor(rope1, rope1, rope2, ALU.add).then_inc(rot, 1)
            lo_of(dve, x.next_q)
            dve.wait_ge(proj_h, 4 * x.h + 2)
            dve.tensor_tensor(q_rope[ROPE:P, x.e, :], rope1[ROPE:P], q_rope[ROPE:P, x.e, :].bitcast(F32),
                              ALU.subtract).then_inc(proj_l, 1)
            low(x, kn_lo[:, x.e, :], x.k, kn_hi[:, x.e, :], 3)

        def head_values(x):
            low(x, v_lo[:, x.e, :], x.v, v_hi[:, x.e, :], 4)

        def softmax(x):
            for qb in range(TB):
                c = x.e * TB + qb
                dve.wait_ge(s_full, 4 * x.h + qb + 1)
                blk = bank[qb][:, qb * P:(qb + 1) * P]
                dve.tensor_tensor(blk, blk, mask, ALU.add).then_inc(s_masked, 1)
                dve.wait_ge(s_masked, 4 * x.h + qb + 1)
                dve.tensor_reduce(rowmax[:, c:c + 1], bank[qb][:, 0:(qb + 1) * P], AX.X, ALU.max)\
                   .then_inc(s_max, 1)
                dve.wait_ge(s_max, 4 * x.h + qb + 1)
                dve.tensor_scalar(negmax[:, c:c + 1], rowmax[:, c:c + 1], -SCALE, None, ALU.mult)\
                   .then_inc(s_neg, 1)

        def inverse(h, e):
            dve.wait_ge(s_exp, 4 + 4 * h + 4)
            dve.reciprocal(rowinv[:, e * TB:(e + 1) * TB], rowsum[:, e * TB:(e + 1) * TB])\
               .then_inc(s_inv, 1)

        def turned(h, j):
            dve.wait_ge(pt_h, 4 * h + j + 1)
            dve.tensor_tensor(ptlo[:, j % 2, j * P:T], bank[4 + j % 2][:, j * P:T],
                              pthi[:, j % 2, j * P:T].bitcast(F32), ALU.subtract).then_inc(pt_l, 1)

        def attend(i, e, x):
            h, job = 2 * i + e, attended(i, e)
            if x or e == 0:
                inverse(h + 1, 1 - e)
            if x:
                queries_keys(x)
            turned(h, 2)
            turned(h, 3)
            dve.wait_ge(o_h, h + 1)
            dve.tensor_tensor(at(flo, h), g_of(job)[:, :], at(fhi, h).bitcast(F32), ALU.subtract)\
               .then_inc(g_free[job.bank], 1)
            if x:
                head_values(x)
            if x:
                softmax(x)
            if x or e == 0:
                turned(h + 1, 0)
                turned(h + 1, 1)

        for e in range(2):
            x = Head(None, e)
            if e:
                inverse(0, 0)
            queries_keys(x)
            head_values(x)
            softmax(x)
            if e:
                turned(0, 0)
                turned(0, 1)
        with dve.Fori(0, HEADS // 2 - 1) as i:
            for e in range(2):
                attend(i, e, Head(i, e))
        for e in range(2):
            attend(HEADS // 2 - 1, e, None)
            if e == 0:
                lo_of(dve, u_run(R_OA, B_OA, 4, 0, 1))

        dve.wait_ge(dt_tok, 1)
        dve.tensor_tensor(dtx.rearrange("p (a n) -> p a n", a=TB),
                          bank[2][:, 3 * P:4 * P].rearrange("p (a n) -> p a n", a=TB),
                          dt_bias[:, :].unsqueeze(1).broadcast_to([P, TB, SH]), ALU.add)\
           .then_inc(dt_x, 1)
        dve.wait_ge(dt_x, 1)
        dve.scalar_tensor_tensor(dtneg, dtx, -1.0, dtx, ALU.mult, ALU.min).then_inc(dt_v, 1)
        dve.wait_ge(dt_a, 3)
        dve.scalar_tensor_tensor(dtx, dtx, 0.0, dtneg, ALU.max, ALU.add).then_inc(dt_v, 1)
        dve.wait_ge(dt_v, 2)
        dve.scalar_tensor_tensor(dta[:, :].rearrange("p (a n) -> p a n", a=TB),
                                 dtx.rearrange("p (a n) -> p a n", a=TB), -1.0,
                                 a_log[:, :].unsqueeze(1).broadcast_to([P, TB, SH]), ALU.mult, ALU.mult)\
           .then_inc(dt_v, 1)
        dve.tensor_scalar(dt_half[:, :], dtx, 0.5, None, ALU.mult).then_inc(dt_v, 1)
        dve.wait_ge(dt_v, 4)
        dve.tensor_copy(dta_hi[:, :], dta[:, :]).then_inc(dt_v, 1)
        dve.wait_ge(dt_v, 5)
        dve.tensor_tensor(dta_lo[:, :], dta[:, :], dta_hi[:, :].bitcast(F32), ALU.subtract)\
           .then_inc(dt_v, 1)

        def oa(i, last):
            for k in range(4):
                lo_of(dve, u_run(R_OA, B_OA, 4, i, k + 2))

        oa(0, False)
        dve.wait_ge(dt_a, 4)
        dve.scalar_tensor_tensor(dt_end[:, :], dt_half[:, :], 0.5, decay[:, 1, :], ALU.mult, ALU.mult)\
           .then_inc(dt_v, 1)
        dve.tensor_scalar(decay[:, 0, :], decay[:, 0, :], 0.5, None, ALU.mult).then_inc(dt_v, 1)
        oa(1, True)

        def group(i, last):
            def heads(table, ch):
                return cols(table, ch * SH + GH * i, GH)

            def refill(k):
                lo_of(dve, u_ssm(i, k + 2))

            def conv(k):
                v = 4 * i + k
                cc = conv_chunk(i, k)
                job = Job(J_SSM, i, 8, k)
                acc, src = tt[:, k % 2, :], g_of(job)
                dve.wait_ge(cv_acc, v + 1)
                for n, tap in enumerate((2, 1, 0)):
                    s = TAPS - 1 - tap
                    if n:
                        dve.wait_ge(cv_tap, 2 * v + n)
                    ins = dve.scalar_tensor_tensor(acc[:, s:T], src[:, 0:T - s],
                                                   cols(convw, tap * (XBC // P) + cc, 1), acc[:, s:T],
                                                   ALU.mult, ALU.add)
                    if n < 2:
                        ins.then_inc(cv_tap, 1)
                    else:
                        ins.then_inc(g_free[job.bank], 1)
                refill(k)
                dve.wait_ge(cv_tanh, v + 1)
                dve.scalar_tensor_tensor(conv_dst(k), conv_dst(k), 1.0, acc, ALU.add, ALU.mult)\
                   .then_inc(cv_out, 1)

            def masked(ch):
                n = 4 * i + ch
                dve.wait_ge(cb_done, n + 1)
                dve.wait_ge(m_done, n + 1)
                dve.scalar_tensor_tensor(cbm[:, :], bank[1][:, 0:P], 0.25, tri, ALU.mult, ALU.mult)\
                   .then_inc(cbm_done, 1)
                dve.wait_ge(cbm_done, n + 2)
                dve.wait_ge(e_done, n + 2)
                e = sq[:, ch % 2, :].rearrange("p (h l) -> p h l", h=GH)
                dve.tensor_tensor(e, e, cbm[:, :].unsqueeze(1).broadcast_to([P, GH, P]), ALU.mult)\
                   .then_inc(m_done, 1)

            def outputs(ch):
                n = 4 * i + ch
                off, diag_ = bank[2][:, 0:GF], bank[2][:, GF:2 * GF]
                dve.wait_ge(yd_done, 2 + n + 1)
                dve.wait_ge(yt_done, n + 1)
                if ch == 0:
                    dve.wait_ge(xd_done, n + 1)
                    dve.tensor_tensor(y[:, :], diag_, xd[:, :], ALU.add).then_inc(y_done, 1)
                else:
                    m = 6 * i + 2 * (ch - 1)
                    dve.tensor_tensor(y[:, :].rearrange("p (h d) -> p h d", h=GH),
                                      off.rearrange("p (h d) -> p h d", h=GH),
                                      heads(decay[:, 0, :], ch).unsqueeze(2).broadcast_to([P, GH, HD]),
                                      ALU.mult).then_inc(y_part, 1)
                    dve.wait_ge(y_part, m + 1)
                    dve.tensor_tensor(y[:, :], diag_, y[:, :], ALU.add).then_inc(y_part, 1)
                    dve.wait_ge(y_part, m + 2)
                    dve.tensor_tensor(y[:, :], y[:, :], xd[:, :], ALU.add).then_inc(y_done, 1)

            def advance(ch):
                dve.wait_ge(s_done, 3 * i + ch + 1)
                if ch == 0:
                    dve.tensor_copy(state[:, :], bank[3][:, 0:GF]).then_inc(h_done, 1)
                else:
                    st = state[:, :].rearrange("p (h d) -> p h d", h=GH)
                    dve.tensor_tensor(st, st, heads(decay[:, 2, :], ch).unsqueeze(2)
                                      .broadcast_to([P, GH, HD]), ALU.mult).then_inc(h_scaled, 1)
                    dve.wait_ge(h_scaled, 2 * i + ch)
                    dve.tensor_tensor(state[:, :], bank[3][:, 0:GF], state[:, :], ALU.add)\
                       .then_inc(h_done, 1)

            def z_gate(f):
                job = Job(J_SSM, i, 8, 4 + f)
                dve.wait_ge(z_tanh, 2 * i + f + 1)
                dve.scalar_tensor_tensor(zs[:, f, :], zs[:, f, :], 1.0, g_of(job)[:, :], ALU.add, ALU.mult)\
                   .then_inc(g_free[job.bank], 1)

            for k in range(4):
                conv(k)
            masked(0)
            z_gate(0)
            masked(1)
            refill(4)
            outputs(0)
            advance(0)
            z_gate(1)
            masked(2)
            refill(5)
            outputs(1)
            advance(1)
            masked(3)
            job = Job(J_SSM, i, 8, 6)
            dve.wait_ge(g_free[job.bank], job.before + 1)
            dve.scalar_tensor_tensor(at(buf1, i), uu[:, 0, :], 1.0, at(buf1, i), ALU.add, ALU.mult)\
               .then_inc(ga_out, 1)
            refill(6)
            outputs(2)
            advance(2)
            outputs(3)
            for f in range(2):
                if f == 0:
                    dve.wait_ge(yt_done, 1 + 4 * i + 4)
                dve.scalar_tensor_tensor(zs[:, f, :], bank[4 + f][:, :], 0.5, zs[:, f, :], ALU.mult,
                                         ALU.mult).then_inc(gt_done, 1)
            rms_dve(dve, RMS_G + i, bank[1], GF)
            dve.wait_ge(gemm_done, G_SSM + 12 * i + ADA_UNITS[3] + 1)
            dve.tensor_tensor(cols(mod, 16 + 4 * i, 4), bank[3][:, GF:GF + 4], cols(vec, 16 + 4 * i, 4),
                              ALU.add).then_inc(ada_out, 1)
            refill(7)
            dve.wait_ge(rep_done, RMS_G + i + 1)
            dve.wait_ge(ga_out, i + 1)
            row = VEC["g_ssm_out"][0]
            for f in range(2):
                dve.scalar_tensor_tensor(uu[:, f, :], zs[:, f, :], cols(vec, row + 2 * i + f, 1),
                                         bank[1][:, :], ALU.mult, ALU.mult).then_inc(yg_u, 1)
            for f in range(2):
                dve.wait_ge(yg_h, 2 * i + f + 1)
                dve.tensor_tensor(at(flo, 2 * i + f), uu[:, f, :], at(fhi, 2 * i + f).bitcast(F32),
                                  ALU.subtract).then_inc(yg_l, 1)

        last_peeled(dve, GROUPS, group)

        dve.wait_ge(ada_out, 1 + GROUPS)
        row = VEC["g_pre_mlp"][0]
        dve.scalar_tensor_tensor(g_mlp[:, :], mod[:, 32:40], 1.0, vec[:, row:row + 8], ALU.add, ALU.mult)\
           .then_inc(mod_done, 1)
        row = VEC["g_post_mix"][0]
        dve.tensor_tensor(gp_mix[:, :], mod[:, 16:24], vec[:, row:row + 8], ALU.mult).then_inc(mod_done, 1)
        row = VEC["g_post_mlp"][0]
        dve.tensor_tensor(gp_mlp[:, :], mod[:, 40:48], vec[:, row:row + 8], ALU.mult).then_inc(mod_done, 1)

        def os_(i, last):
            for c in range(2):
                n = 2 * i + c
                job = Job(J_OS, i, 2, c)
                lo_of(dve, u_run(R_OS, B_OS, 4, i, 2 * c + 2))
                dve.wait_ge(gemm_done, G_OS + 4 * i + 2 * c + 2)
                dve.wait_ge(mg_l, n + 1)
                dve.scalar_tensor_tensor(tt[:, c, :], at(buf2, n), 1.0, g_of(job)[:, :], ALU.add,
                                         ALU.mult).then_inc(g_free[job.bank], 1)
                dve.wait_ge(g_free[job.bank], job.before + 1)
                dve.scalar_tensor_tensor(uu[:, c, :], tt[:, c, :], 0.5, at(buf1, n), ALU.mult, ALU.add)\
                   .then_inc(mg_u, 1)
                lo_of(dve, u_run(R_OS, B_OS, 4, i, 2 * c + 3))
                dve.wait_ge(mg_h, n + 1)
                dve.tensor_tensor(at(alo, n), uu[:, c, :], at(ahi, n).bitcast(F32), ALU.subtract)\
                   .then_inc(mg_l, 1)

        last_peeled(dve, 4, os_)

        def out_(i, last):
            for k in range(4):
                lo_of(dve, u_run(R_OUT, B_OUT, 4, i, k + 2))

        last_peeled(dve, 2, out_)
        rms_dve(dve, RMS_MIX, bank[0], D)
        dve.wait_ge(rep_done, RMS_MIX + 1)
        dve.wait_ge(xt_in, 16)
        dve.wait_ge(mod_done, 3)

        def add_x(c):
            dve.wait_ge(x1_t, c + 1)
            dve.tensor_tensor(buf1[:, c, :], tt[:, c % 2, :], buf1[:, c, :], ALU.add).then_inc(x1_done, 1)

        for c in range(KC):
            wait(dve, x1_done, c - 1)
            dve.scalar_tensor_tensor(tt[:, c % 2, :], buf2[:, c, :], gp_mix[:, c:c + 1], bank[0][:, :],
                                     ALU.mult, ALU.mult).then_inc(x1_t, 1)
            if c:
                add_x(c - 1)
        add_x(KC - 1)
        dve.wait_ge(x1_done, KC)
        rms_dve(dve, RMS_MLP, bank[1], D)
        dve.wait_ge(rep_done, RMS_MLP + 1)
        modulate_dve(dve, 1, buf1, bank[1])

        for half in range(2):
            r0, b0, g0, j0 = R_FF + 32 * half, B_FF + 32 * half, G_FF + 32 * half, J_FF + J_HALF * half

            def up(i, last, r0=r0, b0=b0, half=half):
                for k in range(4):
                    f = 16 * half + 4 * i + k
                    lo_of(dve, u_run(r0, b0, 4, i, k + 2))
                    dve.wait_ge(ff_h, f + 1)
                    dve.tensor_tensor(at(flo, 4 * i + k), uu[:, k % 2, :], at(fhi, 4 * i + k).bitcast(F32),
                                      ALU.subtract).then_inc(ff_l, 1)

            last_peeled(dve, 4, up)

            def down(i, last, r0=r0 + 16, b0=b0 + 16, g0=g0 + 16, j0=j0 + 16, half=half):
                for c in range(2):
                    job = Job(j0, i, 2, c)
                    for part in range(2):
                        if not (half == 1 and last and c == 1):
                            lo_of(dve, u_run(r0, b0, 4, i, 2 * c + part + 2))
                    if half == 1:
                        dve.wait_ge(gemm_done, g0 + 4 * i + 2 * c + 2)
                        dve.tensor_tensor(at(buf2, 2 * i + c), g_of(job)[:, :], at(buf2, 2 * i + c),
                                          ALU.add).then_inc(g_free[job.bank], 1)

            last_peeled(dve, 4, down)
        rms_dve(dve, RMS_FF, bank[0], D)
        dve.wait_ge(rep_done, RMS_FF + 1)
        for c in range(KC):
            if c >= 2:
                dve.wait_ge(fin_done[c % 2], c // 2)
            dve.scalar_tensor_tensor(tt[:, c % 2, :], buf2[:, c, :], gp_mlp[:, c:c + 1], bank[0][:, :],
                                     ALU.mult, ALU.mult).then_inc(fin_t, 1)
            if c % 2 == 1:
                dve.wait_ge(fin_t, c)
                dve.tensor_tensor(buf2[:, c - 1, :], tt[:, 0, :], buf1[:, c - 1, :], ALU.add)\
                   .then_inc(fin_done[0], 1)

    @block.gpsimd
    def _(pool):
        pool.sem_inc(ff_q, 1)
        pool.memset(minus_half[:, :], -0.5).then_inc(pool_setup, 1)
        pool.wait_ge(pool_setup, 1)
        clear_sum(pool, 0)
        for c in range(KC):
            add_square(pool, c, c % 2, 1)
        for r in (RMS_X, RMS_Q, RMS_KV):
            rms_pool(pool, r)

        def att(i, last):
            for e in range(2):
                h = 2 * i + e
                pool.wait_ge(s_inv, h + 1)
                for qb in range(TB):
                    blk = probs[:, e, qb, 0:(qb + 1) * P]
                    inv = rowinv[:, e * TB + qb:e * TB + qb + 1]
                    if qb == 0:
                        ins = pool.tensor_tensor(blk, blk, inv.broadcast_to([P, P]), ALU.mult)
                    else:
                        ins = pool.tensor_scalar(blk, blk, inv, 1.0, ALU.mult, ALU.mult)
                    ins.then_inc(p_norm, 1)

        last_peeled(pool, HEADS // 2, att)
        pool.wait_ge(gemm_done, G_SSM)
        pool.wait_ge(dt_v, 8)

        def group(i, last):
            def ramps(ch):
                pool.wait_ge(seg_done, 4 * i + ch + 1)
                for dst, table in ((rm_hi, dta_hi), (rm_lo, dta_lo)):
                    col = cols(table, ch * SH + GH * i, GH)
                    if table is dta_hi:
                        col = col.bitcast(F32)
                    ins = pool.tensor_tensor(dst[:, :].rearrange("p (h l) -> p h l", h=GH),
                                             tri.unsqueeze(1).broadcast_to([P, GH, P]),
                                             col.unsqueeze(2).broadcast_to([P, GH, P]), ALU.mult)
                ins.then_inc(rm_done, 1)

            def scaled(ch):
                if ch == 0:
                    pool.wait_ge(tin_copied, 3 * i + 3)
                else:
                    pool.wait_ge(s_done, 3 * i + ch)
                    pool.wait_ge(y_done, 4 * i + ch + 1)
                src = x_tok[:, ch, :].rearrange("p (h d) -> p h d", h=GH)
                for dst, table in ((xdt, cols(dt_half, ch * SH + GH * i, GH)),
                                   (xend, cols(dt_end, ch * SH + GH * i, GH)),
                                   (xd, cols(d_half, GH * i, GH))):
                    ins = pool.tensor_tensor(dst[:, :].rearrange("p (h d) -> p h d", h=GH), src,
                                             table.unsqueeze(2).broadcast_to([P, GH, HD]), ALU.mult)
                ins.then_inc(xd_done, 1)

            def ada(j):
                unit = Unit(R_SSM, 0, i, 12, 0, ADA_UNITS[j], 0)
                pool.wait_ge(raw_in[unit.slot], unit.landed)
                w = raw[:, unit.slot, :]
                w3 = w.rearrange("p (k n) -> p k n", k=KC)
                pool.tensor_tensor(w3, w3, silu_c[:, :].unsqueeze(2).broadcast_to([P, KC, P]), ALU.mult)\
                    .then_inc(ada_part, 1)
                for n, width in enumerate((4 * P, 2 * P, P)):
                    pool.wait_ge(ada_part, 3 * (4 * i + j) + n + 1)
                    pool.tensor_tensor(w[:, 0:width], w[:, 0:width], w[:, width:2 * width], ALU.add)\
                        .then_inc(ada_part if n < 2 else ada_sum, 1)

            ada(0)
            ramps(0)
            ada(1)
            ramps(1)
            ada(2)
            scaled(0)
            ramps(2)
            scaled(1)
            ramps(3)
            scaled(2)
            scaled(3)
            ada(3)
            rms_pool(pool, RMS_G + i)

        last_peeled(pool, GROUPS, group)

        clear_sum(pool, RMS_G + GROUPS)

        def out_(i, last):
            for k in range(4):
                add_square(pool, KC + 4 * i + k, k % 2, 2)

        last_peeled(pool, 2, out_)
        rms_pool(pool, RMS_MIX)
        clear_sum(pool, RMS_MIX + 1)
        for c in range(KC):
            add_square(pool, 2 * KC + c, c % 2, 3)
        rms_pool(pool, RMS_MLP)
        for half in range(2):
            def up(i, last, half=half):
                for k in range(4):
                    f = 16 * half + 4 * i + k
                    job = Job(J_FF + J_HALF * half, i, 4, k)
                    pool.wait_ge(g_free[job.bank], job.before + 1)
                    pool.wait_ge(ff_l, f + 1)
                    pool.tensor_tensor(uu[:, k % 2, :], tt[:, k % 2, :], tt[:, k % 2, :], ALU.mult)\
                        .then_inc(ff_q, 1)

            last_peeled(pool, 4, up)
        clear_sum(pool, RMS_MLP + 1)

        def down(i, last):
            for c in range(2):
                add_square(pool, 3 * KC + 2 * i + c, c, 4)

        last_peeled(pool, 4, down)
        rms_pool(pool, RMS_FF)
        for c in range(1, KC, 2):
            pool.wait_ge(fin_t, c + 1)
            pool.tensor_tensor(buf2[:, c, :], tt[:, 1, :], buf1[:, c, :], ALU.add).then_inc(fin_done[1], 1)


NAMES = ("x", "c", "positions", "w_ada", "b_ada", "g_pre_mix", "g_post_mix", "w_in", "g_q_lat",
         "g_kv_lat", "w_uq", "w_ukv", "w_o_attn", "conv_w", "conv_b", "dt_bias", "a_log", "d_skip",
         "g_ssm_out", "w_o_ssm", "w_out", "g_pre_mlp", "g_post_mlp", "w_ff1", "w_ff2")


def kernel(**inputs):
    import concourse.bacc as bacc
    from concourse.bass_utils import run_bass_kernel_spmd

    nc = bacc.Bacc("TRN2", target_bir_lowering=False, num_devices=1)
    arrays = {f"in_{n}": np.ascontiguousarray(inputs[n]) for n in NAMES}
    arrays["in_con"] = constants()
    aps = {}
    for n, v in arrays.items():
        aps[n[3:]] = nc.dram_tensor(n, v.shape, mybir.dt.from_np(v.dtype), kind="ExternalInput").ap()
    aps["out"] = nc.dram_tensor("out", (1, T, D), F32, kind="ExternalOutput").ap()
    build(nc, aps)
    r = run_bass_kernel_spmd(nc, [arrays], core_ids=[0])
    return r.results[0]["out"]
```

```python
from contextlib import ExitStack

import numpy as np
import concourse.bass as bass
from concourse import mybir

P = 128
D = 1024
T = 512
TB = T // P
KC = D // P
HEADS = 8
NOPE = 128
ROPE = 64
RANK = 256
THETA = 10000.0
SSM_IN = 2 * D
SH = 32
GROUPS = 8
GH = SH // GROUPS
HD = SSM_IN // SH
GF = GH * HD
XBC = SSM_IN + 2 * GROUPS * P
TAPS = 4
FF = 4 * D
EPS = 1e-6
SCALE = float(NOPE + ROPE) ** -0.5
RAW = 4

COL_Q = 0
COL_KV = RANK
COL_KR = 2 * RANK
COL_Z = COL_KR + ROPE
COL_X = COL_Z + SSM_IN
COL_B = COL_X + SSM_IN
COL_C = COL_B + GROUPS * P
COL_DT = COL_X + XBC
COL_GA = COL_DT + SH
COL_GB = COL_GA + D

VEC = {}
VEC_ROWS = 0
for _name, _n in (("b_ada", 48), ("c", 8), ("g_pre_mix", 8), ("g_post_mix", 8), ("g_q_lat", 2),
                  ("g_kv_lat", 2), ("g_pre_mlp", 8), ("g_post_mlp", 8), ("g_ssm_out", 16)):
    VEC[_name] = (VEC_ROWS, _n)
    VEC_ROWS += _n

CON_IDENT, CON_TRI, CON_STRICT, CON_ONES, CON_MASK = (P * _i for _i in range(5))
CON_FREQ = 5 * P
CON_SIGN = CON_FREQ + 1
CON_COLS = CON_SIGN + 1

F32 = mybir.dt.float32
F32R = mybir.dt.float32r
I32 = mybir.dt.int32
ALU = mybir.AluOpType
ACT = mybir.ActivationFunctionType
AX = mybir.AxisListType

LAG = 3
NEXT = 5
ADA_BESIDE = 12
ADA_DVE = ((0, 1), (2, 3), (4, 5), (8, 9), (12, 13), (14, 15))
ADA_POOL = (10, 11)
ADA_PE = (6, 7)
R_ADA, R_LAT, R_ATT, R_OA, R_SSM, R_OS, R_OUT, R_FF = 0, 4, 11, 27, 35, 131, 147, 155
B_LAT, B_ATT, B_OA, B_SSM, B_OS, B_OUT, B_FF = 0, 7, 23, 31, 95, 111, 119
G_LAT, G_ATT, G_OA, G_SSM, G_OS, G_OUT, G_FF = 4, 11, 51, 59, 155, 171, 179
J_LAT, J_ATT, J_OA, J_SSM, J_OS, J_OUT, J_FF = 0, 7, 45, 53, 117, 125, 133
J_TURNS = J_ATT + 8
J_HALF = 24
SSM_UNITS = (0, 1, 2, 4, 5, 7, 9, 10)
ADA_UNITS = (3, 6, 8, 11)
SET_TRIG = 16
ROPE_DMAS = 16 * 5
SMALL = 16 * 10
TABLES = 16 * 5
MAGIC = 1.5 * 2.0 ** 23
TWO_PI_1 = 6.28125
TWO_PI_2 = float((np.float32(2 * np.pi - TWO_PI_1).view(np.uint32) & np.uint32(0xFFFFE000))
                 .view(np.float32))
TWO_PI_3 = float(2 * np.pi - TWO_PI_1 - TWO_PI_2)
PI_IN = 3.1415925
RMS_X, RMS_Q, RMS_KV, RMS_G, RMS_MIX, RMS_MLP, RMS_FF = 0, 1, 2, 3, 11, 12, 13


def constants():
    j = np.arange(P)[:, None]
    l = np.arange(P)[None, :]
    con = np.zeros((P, CON_COLS), np.float32)
    con[:, CON_IDENT:CON_IDENT + P] = j == l
    con[:, CON_TRI:CON_TRI + P] = j <= l
    con[:, CON_STRICT:CON_STRICT + P] = j > l
    con[:, CON_ONES:CON_ONES + P] = 1.0
    con[:, CON_MASK:CON_MASK + P] = np.where(l > j, -1e30, 0.0)
    half = ROPE // 2
    freq = np.float32(THETA) ** (-np.arange(half, dtype=np.float32) / np.float32(half))
    con[:, CON_FREQ] = np.tile(freq.astype(np.float32), P // half)
    con[:, CON_SIGN] = np.where(np.arange(P) % ROPE < half, -1.0, 1.0)
    return con


def at(tensor, i):
    if isinstance(i, int):
        return tensor[:, i, :]
    return tensor[:, bass.ds(i, 1), :].rearrange("p a n -> p (a n)")


def cols(tensor, i, n):
    if isinstance(i, int):
        return tensor[:, i:i + n]
    return tensor[:, bass.ds(i, n)]


def wait(eng, semaphore, value):
    if not (isinstance(value, int) and value <= 0):
        eng.wait_ge(semaphore, value)


def last_peeled(eng, count, body):
    with eng.Fori(0, count - 1) as i:
        body(i, False)
    body(count - 1, True)


def build(nc, a):
    with ExitStack() as ctx:
        program(nc, a, ctx)


def program(nc, a, ctx):
    def sb(name, shape, dt=F32, stack=ctx):
        return stack.enter_context(nc.sbuf_tensor(name, shape, dt))

    def sem(name):
        return ctx.enter_context(nc.semaphore(name))

    raw = sb("raw", [P, RAW, KC * P])
    whi = sb("whi", [P, 2, KC * P], F32R)
    wlo = sb("wlo", [P, 2, KC * P], F32R)
    ahi = sb("ahi", [P, KC, T], F32R)
    alo = sb("alo", [P, KC, T], F32R)
    with ExitStack() as start:
        beside = sb("beside", [P, ADA_BESIDE, KC * P], F32, start)
    fhi = sb("fhi", [P, 2 * KC, T], F32R)
    flo = sb("flo", [P, 2 * KC, T], F32R)
    buf1 = sb("buf1", [P, KC, T])
    buf2 = sb("buf2", [P, KC, T])
    sq = sb("sq", [P, 2, T])
    tt = sb("tt", [P, 2, T])
    uu = sb("uu", [P, 2, T])

    con = sb("con", [P, CON_COLS])
    strict_r = sb("strict_r", [P, P], F32R)
    vec = sb("vec", [P, VEC_ROWS])
    convb = sb("convb", [P, XBC // P])
    convw = sb("convw", [P, TAPS * XBC // P])
    silu_c = sb("silu_c", [P, KC])
    mod = sb("mod", [P, 48])
    g_mix = sb("g_mix", [P, KC])
    g_mlp = sb("g_mlp", [P, KC])
    gp_mix = sb("gp_mix", [P, KC])
    gp_mlp = sb("gp_mlp", [P, KC])
    minus_half = sb("minus_half", [P, TB])
    ms = sb("ms", [P, TB])
    rstd = sb("rstd", [P, TB])
    rowmax = sb("rowmax", [P, 2 * TB])
    negmax = sb("negmax", [P, 2 * TB])
    rowsum = sb("rowsum", [P, 2 * TB])
    rowinv = sb("rowinv", [P, 2 * TB])
    dt_bias = sb("dt_bias", [P, SH])
    a_log = sb("a_log", [P, SH])
    d_half = sb("d_half", [P, SH])
    dt_half = sb("dt_half", [P, TB * SH])
    dta = sb("dta", [P, TB * SH])
    dta_hi = sb("dta_hi", [P, TB * SH], F32R)
    dta_lo = sb("dta_lo", [P, TB * SH])
    dt_end = sb("dt_end", [P, TB * SH])
    decay = sb("decay", [P, 3, TB * SH])
    ident = con[:, CON_IDENT:CON_IDENT + P]
    tri = con[:, CON_TRI:CON_TRI + P]
    strict = con[:, CON_STRICT:CON_STRICT + P]
    ones = con[:, CON_ONES:CON_ONES + P]
    mask = con[:, CON_MASK:CON_MASK + P]

    with ExitStack() as att:
        lathi = sb("lathi", [P, 4, T], F32R, att)
        latlo = sb("latlo", [P, 4, T], F32R, att)
        pthi = sb("pthi", [P, 2, T], F32R, att)
        ptlo = sb("ptlo", [P, 2, T], F32R, att)
    ssm = ctx.enter_context(ExitStack())
    c_t = sb("c_t", [P, T], F32, ssm)
    b_t = sb("b_t", [P, T], F32, ssm)
    b_tok = sb("b_tok", [P, T], F32, ssm)
    x_tok = sb("x_tok", [P, TB, GF], F32, ssm)
    zs = sb("zs", [P, 2, T], F32, ssm)
    cbm = sb("cbm", [P, P], F32, ssm)
    rm_hi = sb("rm_hi", [P, GH * P], F32R, ssm)
    rm_lo = sb("rm_lo", [P, GH * P], F32R, ssm)
    xdt = sb("xdt", [P, 2, GF], F32, ssm)
    xend = sb("xend", [P, 2, GF], F32, ssm)
    xd = sb("xd", [P, 2, GF], F32, ssm)
    state = sb("state", [P, GF], F32, ssm)
    y = sb("y", [P, GF], F32, ssm)
    ssum = c_t[:, :]

    x_tok_all = buf1[:, :, :].rearrange("p (a k) n -> p a (k n)", a=TB)
    xt = buf2
    lat = buf2[:, 0:4, :]
    cos, sin, rope1, rope2 = (buf2[:, i, :] for i in range(4, 8))
    probs = buf1[:, :, :].rearrange("p (a b) n -> p a b n", a=2)
    qn_hi, kn_hi, v_hi = fhi[:, 8:10, :], fhi[:, 10:12, :], fhi[:, 12:14, :]
    qn_lo, kn_lo, v_lo = flo[:, 8:10, :], flo[:, 10:12, :], flo[:, 12:14, :]
    q_rope = fhi[:, 14:16, :]
    kr_hi, kr_lo = flo[:, 14, :], flo[:, 15, :]
    dt_feat = tt[0:SH, 0, :]
    dtx = tt[:, 1, 0:TB * SH]
    dtneg = tt[:, 1, TB * SH:2 * TB * SH]
    pos_i = buf2[:, 6, :].bitcast(I32)
    ost = [sq[:, 0, :], sq[:, 1, :], uu[:, 0, :], uu[:, 1, :]]
    vec_rows = uu[0:VEC_ROWS, 0, 0:P]
    convb_rows = uu[0:XBC // P, 0, P:2 * P]
    convw_rows = uu[:, 0, 2 * P:3 * P]

    bank = [ctx.enter_context(nc.psum_tensor(f"bank{i}", [P, T], F32)) for i in range(8)]
    G = bank[6:8] + bank[0:2]

    small_in = sem("small_in")
    tables_in = sem("tables_in")
    x_in = sem("x_in")
    beside_in = [sem(f"beside_in{n}") for n in range(ADA_BESIDE // 2)]
    raw_in = [sem(f"raw_in{i}") for i in range(RAW)]
    rope_in = [sem(f"rope_in{i}") for i in range(2)]
    krope_in = sem("krope_in")
    pos_in = sem("pos_in")
    stash = sem("stash")
    xt_in = sem("xt_in")
    out_sent = [sem(f"out_sent{i}") for i in range(4)]
    w_hi = sem("w_hi")
    w_lo = sem("w_lo")
    gemm_done = sem("gemm_done")
    g_free = [sem(f"g_free{i}") for i in range(4)]
    vec_t = sem("vec_t")
    vec_c = sem("vec_c")
    silu_done = sem("silu_done")
    ada_step = sem("ada_step")
    pool_step = sem("pool_step")
    columns = sem("columns")
    ada_part = sem("ada_part")
    ada_sum = sem("ada_sum")
    ada_out = sem("ada_out")
    setup = sem("setup")
    pool_setup = sem("pool_setup")
    trig = sem("trig")
    xt_full = sem("xt_full")
    xt_copied = sem("xt_copied")
    sq_full = sem("sq_full")
    sq_zero = sem("sq_zero")
    sq_added = sem("sq_added")
    ssq_done = sem("ssq_done")
    ms_done = sem("ms_done")
    rstd_done = sem("rstd_done")
    rep_done = sem("rep_done")
    nm_t = sem("nm_t")
    nm_u = sem("nm_u")
    nm_h = sem("nm_h")
    nm_l = sem("nm_l")
    lat_sq = sem("lat_sq")
    lat_u = sem("lat_u")
    lat_h = sem("lat_h")
    lat_l = sem("lat_l")
    kr_v = sem("kr_v")
    kr_h = sem("kr_h")
    dt_x = sem("dt_x")
    dt_v, dt_a = sem("dt_v"), sem("dt_a")
    dt_copied = sem("dt_copied")
    dt_tok = sem("dt_tok")
    dt_mm = sem("dt_mm")
    proj_h = sem("proj_h")
    proj_l = sem("proj_l")
    rot = sem("rot")
    s_full = sem("s_full")
    s_masked = sem("s_masked")
    s_max = sem("s_max")
    s_neg = sem("s_neg")
    s_exp = sem("s_exp")
    s_inv = sem("s_inv")
    p_norm = sem("p_norm")
    pt_full = sem("pt_full")
    pt_h = sem("pt_h")
    pt_l = sem("pt_l")
    pv_done = sem("pv_done")
    o_h = sem("o_h")
    mod_done = sem("mod_done")
    cv_acc = sem("cv_acc")
    cv_tap = sem("cv_tap")
    cv_tanh = sem("cv_tanh")
    cv_out = sem("cv_out")
    tin_done = sem("tin_done")
    tin_copied = sem("tin_copied")
    z_tanh = sem("z_tanh")
    ga_out = sem("ga_out")
    rm_done = sem("rm_done")
    cb_done = sem("cb_done")
    seg_done = sem("seg_done")
    cbm_done = sem("cbm_done")
    e_done = sem("e_done")
    m_done = sem("m_done")
    xd_done = sem("xd_done")
    yd_done = sem("yd_done")
    s_done = sem("s_done")
    h_scaled = sem("h_scaled")
    h_done = sem("h_done")
    y_part = sem("y_part")
    y_done = sem("y_done")
    yt_done = sem("yt_done")
    gt_done = sem("gt_done")
    gsq_done = sem("gsq_done")
    gsq_added = sem("gsq_added")
    yg_u = sem("yg_u")
    yg_h = sem("yg_h")
    yg_l = sem("yg_l")
    mg_u = sem("mg_u")
    mg_h = sem("mg_h")
    mg_l = sem("mg_l")
    x1_t = sem("x1_t")
    x1_done = sem("x1_done")
    ff_q = sem("ff_q")
    ff_h = sem("ff_h")
    ff_l = sem("ff_l")
    fin_t = sem("fin_t")
    fin_done = [sem("fin_done0"), sem("fin_done1")]
    fin_tr = sem("fin_tr")
    fin_copy = sem("fin_copy")

    xt_dram = nc.dram_tensor("xt_stash", (P, KC * T), F32, kind="Internal").ap()

    w_k = {n: a[n].rearrange("l (k p) n -> p (l k) n", p=P)
           for n in ("w_ada", "w_in", "w_uq", "w_ukv", "w_o_attn", "w_o_ssm", "w_out", "w_ff1", "w_ff2")}
    block = ctx.enter_context(nc.Block())

    def unit_dst(r, kc, n):
        return raw[:, r % RAW, 0:kc * n].rearrange("p (k n) -> p k n", k=kc)

    def loads_of(sp, phase, i, u):
        first = {"ada": R_ADA, "lat": R_LAT, "att": R_ATT, "oa": R_OA, "ssm": R_SSM, "os": R_OS,
                 "out": R_OUT}
        r = (R_FF + 16 * phase[1] if isinstance(phase, tuple) else first[phase]) + u
        slot, landed = r % RAW, raw_in[r % RAW]

        def whole(name, row, col):
            sp.dma_start(unit_dst(r, KC, P),
                         w_k[name][:, row:row + KC, bass.ds(col, P)]).then_inc(landed, 16)

        if phase == "ada":
            whole("w_ada", 0, u * P)
        elif phase == "lat":
            if u < 4:
                whole("w_in", 0, u * P)
            elif u < 6:
                dst = raw[:, slot, :].rearrange("p (k d n) -> p k d n", k=KC, d=2)
                src = w_k["w_in"][:, :, COL_KR:COL_KR + ROPE]
                halves = [(0, 0)] if u == 4 else [(0, 32), (32, 0)]
                width = ROPE if u == 4 else ROPE // 2
                n = 0
                for to, of in halves:
                    for d in range(2):
                        sp.dma_start(dst[:, :, d, to:to + width], src[:, :, of:of + width])\
                          .then_inc(landed if n == 0 else krope_in, 16)
                        n += 1
            else:
                sp.dma_start(unit_dst(r, KC, P)[:, :, 0:SH],
                             w_k["w_in"][:, :, COL_DT:COL_DT + SH]).then_inc(landed, 16)
        elif phase == "att":
            if u in (0, 2):
                h = 2 * i + u // 2
                extra = rope_in[u // 2]
                dst = unit_dst(r, 2, 3 * P)
                col = h * (NOPE + ROPE)
                sp.dma_start(dst[:, :, 0:NOPE + ROPE],
                             w_k["w_uq"][:, :, bass.ds(col, NOPE + ROPE)]).then_inc(landed, 16)
                sp.dma_start(dst[:, :, NOPE + ROPE:2 * P],
                             w_k["w_uq"][:, :, bass.ds(col + NOPE, ROPE)]).then_inc(extra, 16)
                for to, of in ((0, 32), (32, 0), (64, 32), (96, 0)):
                    sp.dma_start(dst[:, :, 2 * P + to:2 * P + to + 32],
                                 w_k["w_uq"][:, :, bass.ds(col + NOPE + of, 32)]).then_inc(extra, 16)
            else:
                h = 2 * i + u // 2
                sp.dma_start(unit_dst(r, 2, 2 * P),
                             w_k["w_ukv"][:, :, bass.ds(h * 2 * P, 2 * P)]).then_inc(landed, 16)
        elif phase == "oa":
            whole("w_o_attn", 0, (4 * i + u) * P)
        elif phase == "ssm":
            if u in ADA_UNITS:
                whole("w_ada", 0, (16 + 4 * i + ADA_UNITS.index(u)) * P)
            else:
                col = (COL_C + i * P, COL_B + i * P, COL_X + i * GF, COL_X + i * GF + P, COL_Z + i * GF,
                       COL_Z + i * GF + P, COL_GA + i * P, COL_GB + i * P)[SSM_UNITS.index(u)]
                whole("w_in", 0, col)
        elif phase == "os":
            whole("w_o_ssm", KC * (u % 2), (2 * i + u // 2) * P)
        elif phase == "out":
            whole("w_out", 0, (4 * i + u) * P)
        else:
            _, part = phase
            if part % 2 == 0:
                whole("w_ff1", 0, (16 * (part // 2) + 4 * i + u) * P)
            else:
                whole("w_ff2", 2 * KC * (part // 2) + KC * (u % 2), (2 * i + u // 2) * P)

    ATT_STEPS = (3, 5, 8, 10)
    STREAM = [("ada", 1, R_LAT), ("lat", 1, 7), ("att", 4, 4), ("oa", 2, 4), ("ssm", 8, 12), ("os", 4, 4),
              ("out", 2, 4)] + [(("ff", part), 4, 4) for part in range(4)]

    def used_up(phase, i, u):
        if phase in ("ada", "lat"):
            return (R_ADA if phase == "ada" else R_LAT) + u + 1
        if phase == "att":
            return G_ATT + 10 * i + ATT_STEPS[u]
        first = {"oa": G_OA, "ssm": G_SSM, "os": G_OS, "out": G_OUT}
        g = G_FF + 16 * phase[1] if isinstance(phase, tuple) else first[phase]
        return g + (12 if phase == "ssm" else 4) * i + u + 1

    def load_vector(eng, name):
        row, rows = VEC[name]
        eng.dma_start(uu[row:row + rows, 0, 0:P], a[name].rearrange("l (r n) -> (l r) n", n=P))\
           .then_inc(small_in, 16)

    @block.sync
    def _(sp):
        sp.dma_start(con[:, :], a["con"]).then_inc(small_in, 16)
        for name in list(VEC)[0::2]:
            load_vector(sp, name)
        for u in range(2):
            loads_of(sp, "ada", 0, u)
        sp.dma_start(x_tok_all, a["x"][0].rearrange("(b p) n -> p b n", p=P)).then_inc(x_in, 16)
        for u in range(2, RAW):
            loads_of(sp, "ada", 0, u)
        for n in range(ADA_BESIDE):
            sp.dma_start(beside[:, n, :].rearrange("p (k n) -> p k n", k=KC),
                         w_k["w_ada"][:, :, (R_LAT + n) * P:(R_LAT + n + 1) * P])\
              .then_inc(beside_in[n // 2], 16)
        for n, (phase, count, units) in enumerate(STREAM):
            following = STREAM[n + 1] if n + 1 < len(STREAM) else None

            def ahead(i, last, phase=phase, units=units, following=following):
                for u in range(units):
                    if u + RAW < units:
                        to = (phase, i, u + RAW)
                    elif not last:
                        to = (phase, i + 1, u + RAW - units)
                    elif following:
                        to = (following[0], 0, u + RAW - units)
                    else:
                        continue
                    sp.wait_ge(gemm_done, used_up(phase, i, u))
                    loads_of(sp, *to)

            if count == 1:
                ahead(0, True)
            else:
                last_peeled(sp, count, ahead)
        for c in range(KC):
            sp.wait_ge(fin_copy, c + 1)
            sp.dma_start(a["out"][0, :, c * P:(c + 1) * P].rearrange("(b p) n -> p b n", p=P),
                         ost[c % 4].rearrange("p (b n) -> p b n", b=TB)).then_inc(out_sent[c % 4], 16)
        for k in range(4):
            sp.wait_ge(out_sent[k], 16 * (KC // 4))

    class Unit:

        def __init__(self, r0, b0, i, r_per, b_per, ru, bu):
            assert r_per % RAW == 0 and b_per % 2 == 0
            self.slot = (r0 + ru) % RAW
            self.landed = 16 * (i * (r_per // RAW) + (r0 + ru) // RAW + 1)
            self.par = (b0 + bu) % 2
            self.b = b0 + bu + i * b_per

    def ada_units(first, count):
        return raw[:, first:first + count, :] if first < R_LAT else \
            beside[:, first - R_LAT:first - R_LAT + count, :]

    def wait_ada(eng, first, count):
        if first < R_LAT:
            for u in range(first, first + count):
                eng.wait_ge(raw_in[u], 16)
        else:
            eng.wait_ge(beside_in[(first - R_LAT) // 2], 32)

    def hi_of(act, unit):
        act.wait_ge(raw_in[unit.slot], unit.landed)
        act.activation(whi[:, unit.par, :], raw[:, unit.slot, :], ACT.Copy).then_inc(w_hi, 1)

    def lo_of(dve, unit):
        dve.wait_ge(w_hi, unit.b + 1)
        dve.tensor_tensor(wlo[:, unit.par, :], raw[:, unit.slot, :], whi[:, unit.par, :].bitcast(F32),
                          ALU.subtract).then_inc(w_lo, 1)

    def u_lat(bu):
        return Unit(R_LAT, B_LAT, 0, 4, 2, bu, bu)

    def u_att(i, bu):
        return Unit(R_ATT, B_ATT, i, 4, 4, bu, bu)

    def u_ssm(i, k):
        return Unit(R_SSM, B_SSM, i, 12, 8, SSM_UNITS[k] if k < 8 else 12 + k - 8, k)

    def u_run(r0, b0, per, i, bu):
        return Unit(r0, b0, i, per, per, bu, bu)

    def conv_chunk(i, k):
        return (SSM_IN // P + GROUPS + i, SSM_IN // P + i, 2 * i, 2 * i + 1)[k]

    def conv_dst(k):
        return (c_t[:, :], b_t[:, :], uu[:, 0, :], uu[:, 1, :])[k]

    def product(pe, out, pairs, first=True, last=True):
        n = 3 * len(pairs)
        k = 0
        for sh, sl, mh, ml in pairs:
            for s, m in ((sh, mh), (sh, ml), (sl, mh)):
                ins = pe.matmul(out, s, m, start=first and k == 0, stop=last and k == n - 1)
                k += 1
        return ins

    def weights(par, k, n=P):
        return whi[:, par, k * P:k * P + n], wlo[:, par, k * P:k * P + n]

    def gemm(pe, job, b, par, moving, first=True, last=True, ready=None, start=0):
        pe.wait_ge(w_lo, b + 1)
        if first and start == 0:
            free_job(pe, job)
        for k in range(start, KC):
            if ready:
                ready(k)
            ins = product(pe, g_of(job)[:, :], [weights(par, k) + (moving[0][:, k, :], moving[1][:, k, :])],
                          first and k == 0, last and k == KC - 1)
        ins.then_inc(gemm_done, 1)

    def gemm_pair(pe, jobs, b, pars, base):
        for job in jobs:
            free_job(pe, job)
        pe.wait_ge(w_lo, b + 1)
        for k in range(KC + LAG):
            if k == LAG:
                pe.wait_ge(w_lo, b + 2)
            if k < KC:
                pe.wait_ge(nm_l, base + k + 1)
            for job, par, c in zip(jobs, pars, (k, k - LAG)):
                if 0 <= c < KC:
                    ins = product(pe, G[job.bank][:, :], [weights(par, c) + (ahi[:, c, :], alo[:, c, :])],
                                  c == 0, c == KC - 1)
                    if c == KC - 1:
                        ins.then_inc(gemm_done, 1)

    class Head:

        def __init__(self, i, e):
            self.e = e
            if i is None:
                self.h = e
                q, r1, k, v = (Job(J_ATT, 0, 2, 4 * e + n) for n in range(4))
                self.next_q, self.next_kv = u_att(0, 2 * e + 2), u_att(0, 2 * e + 3)
            else:
                self.h = 2 * i + 2 + e
                q, r1, k, _, v = (Job(J_TURNS, i, 10, 5 * e + n) for n in range(5))
                self.next_q, self.next_kv = u_att(i, 2 * e + 6), u_att(i, 2 * e + 7)
            self.q, self.r1, self.r2, self.k, self.v = q, r1, SideJob(2, self.h), k, v
            self.g = G_ATT + 5 * self.h
            loads = 1 + e if i is None else i + 2 + e
            self.rope = (rope_in[1 - e], ROPE_DMAS * loads)

    def attended(i, e):
        if isinstance(i, int) and i == HEADS // 2 - 1:
            return SideJob(3, 0) if e else SideJob(2, HEADS)
        return Job(J_TURNS, i, 10, 5 * e + 3)

    class Job:

        def __init__(self, j0, i, per, k):
            assert per % 2 == 0
            self.bank = (j0 + k) % 2
            self.before = i * (per // 2) + (j0 + k) // 2

    class SideJob:

        def __init__(self, bank, before):
            self.bank, self.before = bank, before

    def free_job(pe, job):
        wait(pe, g_free[job.bank], job.before)

    def g_of(job):
        return G[job.bank]

    def rms_pe(pe, rbank, sources, waits, last_square=None):
        for w in waits:
            pe.wait_ge(*w)
        for n, s in enumerate(sources):
            if n and last_square is not None:
                pe.wait_ge(sq_full, last_square + 1)
            for tb in range(TB):
                ins = pe.matmul(rbank[:, tb:tb + 1], s[:, tb * P:(tb + 1) * P], ones[:, 0:1],
                                start=(n == 0 and tb == 0), stop=(n == len(sources) - 1),
                                skip_group_check=True)
        ins.then_inc(ssq_done, 1)

    def rms_rep(pe, r, rbank):
        pe.wait_ge(rstd_done, r + 1)
        for tb in range(TB):
            ins = pe.matmul(rbank[:, tb * P:(tb + 1) * P], rstd[:, tb:tb + 1].broadcast_to([P, P]), ident,
                            start=True, stop=True)
        ins.then_inc(rep_done, 1)

    def rms_dve(dve, r, rbank, n):
        dve.wait_ge(ssq_done, r + 1)
        dve.tensor_scalar(ms[:, :], rbank[:, 0:TB], 1.0 / n, EPS, ALU.mult, ALU.add).then_inc(ms_done, 1)

    def rms_pool(pool, r):
        pool.wait_ge(ms_done, r + 1)
        wait(pool, rep_done, r)
        pool.tensor_tensor(rstd[:, :], ms[:, :], minus_half[:, :], ALU.pow).then_inc(rstd_done, 1)

    def square_into(act, q, par, source):
        wait(act, sq_added, q - 1)
        act.activation(sq[:, par, :], source, ACT.Square).then_inc(sq_full, 1)

    def clear_sum(pool, n):
        if n:
            pool.wait_ge(ssq_done, n)
            if n > RMS_MIX:
                pool.sem_inc(sq_added, 1)
        pool.memset(ssum, 0.0).then_inc(sq_zero, 1)

    def add_square(pool, q, par, cleared=0):
        wait(pool, sq_zero, cleared)
        wait(pool, sq_added, q)
        pool.wait_ge(sq_full, q + 1)
        pool.tensor_tensor(ssum, ssum, sq[:, par, :], ALU.add).then_inc(sq_added, 1)

    def modulate_dve(dve, m, source, rbank, between=None):
        for c in range(KC):
            n = m * KC + c
            wait(dve, nm_u, n - 1)
            dve.tensor_tensor(tt[:, c % 2, :], source[:, c, :], rbank[:, :], ALU.mult).then_inc(nm_t, 1)
            if c:
                lo_mod(dve, n - 1, c - 1)
            if between:
                between(c - 1)
        lo_mod(dve, m * KC + KC - 1, KC - 1)

    def lo_mod(dve, n, c):
        dve.wait_ge(nm_h, n + 1)
        dve.tensor_tensor(alo[:, c, :], uu[:, c % 2, :], ahi[:, c, :].bitcast(F32), ALU.subtract)\
           .then_inc(nm_l, 1)

    def modulate_act(act, m, gain, shift, between=None):
        for c in range(KC):
            n = m * KC + c
            act.wait_ge(nm_t, n + 1)
            wait(act, nm_l, n - 1)
            act.activation(uu[:, c % 2, :], tt[:, c % 2, :], ACT.Identity, scale=gain[:, c:c + 1],
                           bias=mod[:, shift + c:shift + c + 1]).then_inc(nm_u, 1)
            act.wait_ge(nm_u, n + 1)
            act.activation(ahi[:, c, :], uu[:, c % 2, :], ACT.Copy).then_inc(nm_h, 1)
            if between:
                between(c)

    @block.tensor
    def _(pe):
        pe.wait_ge(small_in, SMALL)
        pe.transpose(bank[7][:, 0:VEC_ROWS], vec_rows, ident[0:VEC_ROWS, 0:VEC_ROWS]).then_inc(vec_t, 1)

        def columns_of(first, count):
            for u in range(first, first + count):
                ins = pe.matmul(bank[5][:, u:u + 1], ada_units(u, 1)[:, 0, 0:P], ones[:, 0:1],
                                start=True, stop=True)
                if u < R_LAT:
                    ins.then_inc(gemm_done, 1)
                elif u == ADA_DVE[-1][-1]:
                    ins.then_inc(columns, 1)

        def vector_columns(n):
            pe.wait_ge(ada_step, KC * (n + 1))
            columns_of(ADA_DVE[n][0], len(ADA_DVE[n]))

        def direct_column(u):
            for k in range(KC):
                pe.matmul(bank[5][:, u:u + 1], ada_units(u, 1)[:, 0, k * P:(k + 1) * P],
                          silu_c[:, k:k + 1], start=(k == 0), stop=(k == KC - 1))

        vector_columns(0)
        pe.wait_ge(x_in, 16)
        for c in range(KC):
            wait(pe, sq_full, c - 3)
            for tb in range(TB):
                ins = pe.transpose(bank[1 + c % 4][:, tb * P:(tb + 1) * P],
                                   x_tok_all[:, tb, c * P:(c + 1) * P], ident)
            ins.then_inc(xt_full, 1)
        vector_columns(1)
        pe.wait_ge(tables_in, TABLES)
        pe.wait_ge(vec_c, 1)
        pe.transpose(bank[7][:, P:P + XBC // P], convb_rows, ident[0:XBC // P, 0:XBC // P])
        pe.transpose(bank[7][:, 2 * P:3 * P], convw_rows, ident).then_inc(vec_t, 1)
        pe.wait_ge(silu_done, 1)
        wait_ada(pe, ADA_PE[0], 2)
        direct_column(ADA_PE[0])
        direct_column(ADA_PE[1])
        vector_columns(2)
        rms_pe(pe, bank[0], [ssum], [(sq_added, KC)])
        vector_columns(3)
        rms_rep(pe, RMS_X, bank[0])
        vector_columns(4)
        pe.wait_ge(pool_step, 4)
        columns_of(ADA_POOL[0], 2)
        vector_columns(5)

        h_act = (ahi, alo)
        gemm_pair(pe, [Job(J_LAT, 0, 2, k) for k in range(2)], B_LAT, (0, 1), 0)
        for k in range(2, 4):
            gemm(pe, Job(J_LAT, 0, 2, k), B_LAT + k, k % 2, h_act)
        rms_pe(pe, bank[0], [sq[:, 0, :], sq[:, 1, :]], [(lat_sq, 2)])
        gemm(pe, Job(J_LAT, 0, 2, 4), B_LAT + 4, 0, h_act)
        rms_rep(pe, RMS_Q, bank[0])
        rms_pe(pe, bank[1], [tt[:, 0, :], tt[:, 1, :]], [(lat_sq, 4)])
        gemm(pe, Job(J_LAT, 0, 2, 5), B_LAT + 5, 1, h_act)
        rms_rep(pe, RMS_KV, bank[1])
        pe.wait_ge(w_lo, B_LAT + 7)
        job = Job(J_LAT, 0, 2, 6)
        free_job(pe, job)
        product(pe, g_of(job)[0:SH, :], [weights(0, k, SH) + (ahi[:, k, :], alo[:, k, :])
                                         for k in range(KC)]).then_inc(gemm_done, 1)

        pe.wait_ge(lat_l, 4)
        pe.wait_ge(kr_v, 2)
        pe.sem_inc(pv_done, 2)

        Q_PAR, KV_PAR = B_ATT % 2, (B_ATT + 1) % 2

        def queries_keys(x, meanwhile=None):
            pe.wait_ge(w_lo, B_ATT + 2 * x.h + 1)
            for k, job in enumerate((x.q, x.r1, x.r2)):
                if k == 2:
                    if meanwhile:
                        meanwhile()
                    pe.wait_ge(s_exp, 4 * x.h + 1)
                free_job(pe, job)
                pairs = [(whi[:, Q_PAR, c * 3 * P + k * P:c * 3 * P + (k + 1) * P],
                          wlo[:, Q_PAR, c * 3 * P + k * P:c * 3 * P + (k + 1) * P],
                          lathi[:, c, :], latlo[:, c, :]) for c in range(2)]
                product(pe, g_of(job)[:, :], pairs).then_inc(gemm_done, 1)
            pe.wait_ge(w_lo, B_ATT + 2 * x.h + 2)
            free_job(pe, x.k)
            pairs = [(whi[:, KV_PAR, c * 2 * P:c * 2 * P + P], wlo[:, KV_PAR, c * 2 * P:c * 2 * P + P],
                      lathi[:, 2 + c, :], latlo[:, 2 + c, :]) for c in range(2)]
            product(pe, g_of(x.k)[:, :], pairs).then_inc(gemm_done, 1)

        def head_values(x):
            free_job(pe, x.v)
            for tb in range(TB):
                pairs = [(lathi[:, 2 + c, tb * P:(tb + 1) * P], latlo[:, 2 + c, tb * P:(tb + 1) * P],
                          whi[:, KV_PAR, c * 2 * P + P:(c + 1) * 2 * P],
                          wlo[:, KV_PAR, c * 2 * P + P:(c + 1) * 2 * P]) for c in range(2)]
                ins = product(pe, g_of(x.v)[:, tb * P:(tb + 1) * P], pairs)
            ins.then_inc(gemm_done, 1)

        def scores(x):
            pe.wait_ge(proj_l, x.h + 1)
            for job in (x.r2, x.k):
                pe.wait_ge(g_free[job.bank], job.before + 1)
            for qb in range(TB):
                n = (qb + 1) * P
                pe.wait_ge(s_exp, 4 * x.h + qb + 1)
                out = bank[qb][:, 0:n]
                blk = slice(qb * P, n)
                product(pe, out, [(qn_hi[:, x.e, blk], qn_lo[:, x.e, blk], kn_hi[:, x.e, 0:n],
                                   kn_lo[:, x.e, 0:n])], last=False)
                pe.matmul(out, q_rope[:, x.e, blk], kr_hi[:, 0:n], start=False, stop=False)
                pe.matmul(out, q_rope[:, x.e, blk], kr_lo[:, 0:n], start=False, stop=True)\
                  .then_inc(s_full, 1)

        def turn(h, e, j):
            if j == 0:
                pe.wait_ge(p_norm, 4 * h + 4)
            pe.wait_ge(pt_l, 4 * h + j + 1)
            for qb in range(j, TB):
                ins = pe.transpose(bank[4 + j % 2][:, qb * P:(qb + 1) * P],
                                   probs[:, e, qb, j * P:(j + 1) * P], ident)
            ins.then_inc(pt_full, 1)

        def attend_values(h, e, j, job):
            pe.wait_ge(pt_l, 4 * h + j + 3)
            if j == 0:
                free_job(pe, job)
            kb = slice(j * P, (j + 1) * P)
            product(pe, g_of(job)[:, j * P:T],
                    [(v_hi[:, e, kb], v_lo[:, e, kb], pthi[:, j % 2, j * P:T],
                      ptlo[:, j % 2, j * P:T])], first=(j == 0), last=(j == TB - 1)).then_inc(pv_done, 1)

        for e in range(2):
            x = Head(None, e)
            queries_keys(x)
            head_values(x)
            if e:
                turn(0, 0, 0)
            pe.wait_ge(g_free[x.v.bank], x.v.before + 1)
            scores(x)

        def oa_unit(i, k, start=0, end=KC):
            job, par = Job(J_OA, i, 4, k), (B_OA + k) % 2
            if start == 0:
                pe.wait_ge(w_lo, B_OA + 4 * i + k + 1)
                free_job(pe, job)
            for c in range(start, end):
                if i == 0 and k == 0 and c >= HEADS - 2:
                    head = attended(HEADS // 2 - 1, c - (HEADS - 2))
                    pe.wait_ge(g_free[head.bank], head.before + 1)
                ins = product(pe, g_of(job)[:, :], [weights(par, c) + (fhi[:, c, :], flo[:, c, :])],
                              c == 0, c == KC - 1)
            if end == KC:
                ins.then_inc(gemm_done, 1)

        def attend(i, e, x):
            h, job = 2 * i + e, attended(i, e)

            def beside(n):
                if not x:
                    oa_unit(0, 0, 3 * e + n, 3 * e + n + 1)

            if x:
                queries_keys(x, lambda: turn(h, e, 1))
            else:
                turn(h, e, 1)
                beside(0)
                pe.wait_ge(s_exp, 4 * HEADS + e + 1)
            attend_values(h, e, 0, job)
            turn(h, e, 2)
            beside(1)
            attend_values(h, e, 1, job)
            turn(h, e, 3)
            if x:
                head_values(x)
            beside(2)
            attend_values(h, e, 2, job)
            attend_values(h, e, 3, job)
            if x or e == 0:
                turn(h + 1, 1 - e, 0)
            if x:
                scores(x)

        with pe.Fori(0, HEADS // 2 - 1) as i:
            for e in range(2):
                attend(i, e, Head(i, e))
        for e in range(2):
            attend(HEADS // 2 - 1, e, None)
        pe.wait_ge(dt_copied, 1)
        for ch in range(TB):
            ins = pe.transpose(bank[2][:, 3 * P + ch * SH:3 * P + (ch + 1) * SH],
                               dt_feat[:, ch * P:(ch + 1) * P], ident[0:SH, 0:SH])
        ins.then_inc(dt_tok, 1)

        def oa(i):
            for k in range(4):
                if i == 0 and k == 0:
                    oa_unit(i, k, HEADS - 2)
                else:
                    oa_unit(i, k)

        oa(0)
        pe.wait_ge(dt_v, 3)
        for n, left in enumerate((tri, strict, ones)):
            for ch in range(TB):
                ins = pe.matmul(bank[2][:, n * P + ch * SH:n * P + (ch + 1) * SH], left,
                                dta[:, ch * SH:(ch + 1) * SH], start=True, stop=True)
        ins.then_inc(dt_mm, 1)
        oa(1)

        pe.sem_inc(seg_done, 1)
        pe.sem_inc(yd_done, 2)
        pe.sem_inc(yt_done, 1)

        def projection(i, k, start, end, moving=h_act):
            job, par = Job(J_SSM, i, 8, k), (B_SSM + k) % 2
            if start == 0:
                pe.wait_ge(w_lo, B_SSM + 8 * i + k + 1)
                free_job(pe, job)
            ins = product(pe, g_of(job)[:, :], [weights(par, c) + (moving[0][:, c, :], moving[1][:, c, :])
                                                for c in range(start, end)], start == 0, end == KC)
            if end == KC:
                ins.then_inc(gemm_done, 1)

        projection(0, 0, 0, NEXT)

        def group(i, last):
            def blk(k, start=0, end=KC):
                projection(i, k, start, end)

            def ada(j):
                unit = Unit(R_SSM, 0, i, 12, 0, ADA_UNITS[j], 0)
                pe.wait_ge(ada_sum, 4 * i + j + 1)
                if j == 0:
                    pe.wait_ge(ada_out, i + 1)
                    pe.wait_ge(h_done, 3 * i + 1)
                elif j == 3:
                    pe.wait_ge(h_done, 3 * i + 4)
                pe.matmul(bank[3][:, GF + j:GF + j + 1], raw[:, unit.slot, 0:P], ones[:, 0:1],
                          start=True, stop=True).then_inc(gemm_done, 1)

            def turn_in(source, to, conv):
                pe.wait_ge(cv_out, 2 + 4 * i + conv + 1)
                for ch in range(TB):
                    ins = pe.transpose(to[:, ch * P:(ch + 1) * P], source[:, ch * P:(ch + 1) * P], ident)
                ins.then_inc(tin_done, 1)

            def decays(ch):
                n = 4 * i + ch
                blk_ = slice(ch * P, (ch + 1) * P)
                pe.wait_ge(cbm_done, n + 1)
                if ch == 0:
                    pe.wait_ge(yg_l, 2 * i + 1)
                pe.matmul(bank[1][:, 0:P], b_t[:, blk_], c_t[:, blk_], start=True, stop=True)\
                  .then_inc(cb_done, 1)
                pe.wait_ge(rm_done, n + 1)
                pe.wait_ge(e_done, n + 1)
                pe.matmul(bank[0][:, :], strict_r[:, :], rm_hi[:, :], start=True, stop=False)
                pe.matmul(bank[0][:, :], strict_r[:, :], rm_lo[:, :], start=False, stop=True)\
                  .then_inc(seg_done, 1)

            def outputs(ch):
                n = 4 * i + ch
                pe.wait_ge(y_done, n + 1)
                if ch:
                    pe.wait_ge(h_done, 3 * i + ch + 1)
                    pe.matmul(bank[2][:, 0:GF], c_t[:, ch * P:(ch + 1) * P], state[:, :],
                              start=True, stop=True)
                pe.wait_ge(m_done, n + 2)
                pe.wait_ge(xd_done, n + 1)
                for h in range(GH):
                    ins = pe.matmul(bank[2][:, GF + h * HD:GF + (h + 1) * HD],
                                    sq[:, ch % 2, h * P:(h + 1) * P], xdt[:, ch % 2, h * HD:(h + 1) * HD],
                                    start=True, stop=True)
                ins.then_inc(yd_done, 1)
                if ch < TB - 1:
                    pe.wait_ge(h_done, 3 * i + ch + 1)
                    pe.matmul(bank[3][:, 0:GF], b_tok[:, ch * P:(ch + 1) * P], xend[:, ch % 2, :],
                              start=True, stop=True).then_inc(s_done, 1)

            def turn_y(ch):
                pe.wait_ge(y_done, 4 * i + ch + 2)
                if ch == 0:
                    pe.wait_ge(tin_copied, 3 * i + 3)
                for f in range(2):
                    ins = pe.transpose(bank[4 + f][:, ch * P:(ch + 1) * P], y[:, f * P:(f + 1) * P], ident)
                ins.then_inc(yt_done, 1)

            blk(0, NEXT)
            blk(1)
            blk(2)
            ada(0)
            blk(3)
            pe.wait_ge(gt_done, 2 * i + 1)
            turn_in(b_t, bank[4], 1)
            decays(0)
            blk(4)
            turn_in(uu[:, 0, :], bank[5], 2)
            pe.wait_ge(tin_copied, 3 * i + 1)
            turn_in(uu[:, 1, :], bank[4], 3)
            ada(1)
            decays(1)
            blk(5)
            ada(2)
            pe.wait_ge(tin_copied, 3 * i + 3)
            outputs(0)
            decays(2)
            blk(6, 0, 4)
            turn_y(0)
            outputs(1)
            decays(3)
            blk(6, 4)
            turn_y(1)
            outputs(2)
            blk(7, 0, 3)
            turn_y(2)
            outputs(3)
            blk(7, 3, 6)
            turn_y(3)
            blk(7, 6)
            ada(3)
            following = (fhi, flo) if last else h_act
            projection(i + 1, 0, 0, 3, following)
            rms_pe(pe, bank[1], [sq[:, 0, :]], [(gsq_added, i + 1)])
            projection(i + 1, 0, 3, NEXT, following)
            rms_rep(pe, RMS_G + i, bank[1])

        last_peeled(pe, GROUPS, group)

        def os_(i, first=False):
            for c in range(2):
                job = Job(J_OS, i, 2, c)
                for half in range(2):
                    k = 2 * c + half

                    def gated(n, half=half):
                        pe.wait_ge(yg_l, 1 + KC * half + n + 1)

                    gemm(pe, job, B_OS + 4 * i + k, (B_OS + k) % 2,
                         (fhi[:, KC * half:KC * (half + 1), :], flo[:, KC * half:KC * (half + 1), :]),
                         first=(half == 0), last=(half == 1), ready=gated if first and c == 0 else None,
                         start=NEXT if first and k == 0 else 0)

        os_(0, True)
        with pe.Fori(1, 4) as i:
            os_(i)

        def merged(n):
            pe.wait_ge(mg_l, 1 + n + 1)

        for i in range(2):
            for k in range(4):
                gemm(pe, Job(J_OUT, i, 4, k), B_OUT + 4 * i + k, (B_OUT + k) % 2, h_act,
                     ready=merged if i == 0 and k == 0 else None)
        rms_pe(pe, bank[0], [ssum, sq[:, 1, :]], [(sq_added, 2 * KC - 1)], 15)
        rms_rep(pe, RMS_MIX, bank[0])
        rms_pe(pe, bank[1], [ssum, sq[:, 1, :]], [(sq_added, 3 * KC - 1)], 23)
        rms_rep(pe, RMS_MLP, bank[1])

        gemm_pair(pe, [Job(J_FF, 0, 4, k) for k in range(2)], B_FF, (B_FF % 2, 1 - B_FF % 2), KC)
        for half in range(2):
            b0 = B_FF + 32 * half
            j0 = J_FF + J_HALF * half

            def up(i, k0=0, b0=b0, j0=j0):
                for k in range(k0, 4):
                    gemm(pe, Job(j0, i, 4, k), b0 + 4 * i + k, (b0 + k) % 2, h_act)

            up(0, 0 if half else 2)
            with pe.Fori(1, 4) as i:
                up(i)

            def down(i, first=False, b0=b0 + 16, j0=j0 + 16, half=half):
                for c in range(2):
                    job = Job(j0, i, 2, c)
                    for part in range(2):
                        k = 2 * c + part

                        def hidden(n, part=part):
                            pe.wait_ge(ff_l, 1 + 16 * half + KC * part + n + 1)

                        gemm(pe, job, b0 + 4 * i + k, (b0 + k) % 2,
                             (fhi[:, KC * part:KC * (part + 1), :], flo[:, KC * part:KC * (part + 1), :]),
                             first=(part == 0), last=(part == 1), ready=hidden if first and c == 0 else None)

            down(0, True)
            with pe.Fori(1, 4) as i:
                down(i)
        rms_pe(pe, bank[0], [ssum, sq[:, 1, :]], [(sq_added, 4 * KC - 1)], 31)
        rms_rep(pe, RMS_FF, bank[0])
        for c in range(KC):
            pe.wait_ge(fin_done[c % 2], c // 2 + 1)
            wait(pe, fin_copy, c - 1)
            for tb in range(TB):
                ins = pe.transpose(bank[2 + c % 2][:, tb * P:(tb + 1) * P],
                                   buf2[:, c, tb * P:(tb + 1) * P], ident)
            ins.then_inc(fin_tr, 1)

    @block.scalar
    def _(act):
        act.sem_inc(s_exp, 4)
        act.sem_inc(e_done, 1)
        for name in list(VEC)[1::2]:
            load_vector(act, name)
        act.dma_start(convb_rows, a["conv_b"].rearrange("l (r n) -> (l r) n", n=P)).then_inc(tables_in, 16)
        act.dma_start(convw_rows, a["conv_w"].rearrange("l k (r n) -> (l k r) n", n=P))\
           .then_inc(tables_in, 16)
        for dst, name in ((dt_bias, "dt_bias"), (a_log, "a_log"), (d_half, "d_skip")):
            act.dma_start(dst[:, :], a[name].broadcast_to([P, SH])).then_inc(tables_in, 16)
        act.wait_ge(vec_t, 1)
        row, rows = VEC["c"]
        act.activation(silu_c[:, :], bank[7][:, row:row + rows], ACT.Silu).then_inc(silu_done, 1)
        act.activation(vec[:, :], bank[7][:, 0:VEC_ROWS], ACT.Copy).then_inc(vec_c, 1)
        for c in range(KC):
            act.wait_ge(xt_full, c + 1)
            act.activation(xt[:, c, :], bank[1 + c % 4][:, :], ACT.Copy).then_inc(xt_copied, 1)
            square_into(act, c, c % 2, bank[1 + c % 4][:, :])
        act.wait_ge(vec_t, 2)
        act.activation(convb[:, :], bank[7][:, P:P + XBC // P], ACT.Copy).then_inc(vec_c, 1)
        act.activation(convw[:, :], bank[7][:, 2 * P:3 * P], ACT.Copy).then_inc(vec_c, 1)
        act.wait_ge(setup, 4)
        act.wait_ge(xt_copied, KC)
        act.dma_start(xt_dram, buf2[:, :, :].rearrange("p k n -> p (k n)")).then_inc(stash, 16)

        def first_units(c):
            if c == 1:
                hi_of(act, u_lat(1))

        hi_of(act, u_lat(0))
        modulate_act(act, 0, g_mix, 0, first_units)
        act.wait_ge(stash, 16)
        act.wait_ge(nm_l, KC)
        act.dma_start(pos_i, a["positions"].broadcast_to([P, T])).then_inc(pos_in, 16)

        for k in range(4):
            job = Job(J_LAT, 0, 2, k)
            act.wait_ge(gemm_done, G_LAT + k + 1)
            if k == 0:
                act.wait_ge(ssq_done, RMS_X + 1)
            act.activation(sq[:, k, :] if k < 2 else tt[:, k - 2, :], g_of(job)[:, :], ACT.Square)\
               .then_inc(lat_sq, 1)
            act.activation(lat[:, k, :], g_of(job)[:, :], ACT.Copy).then_inc(g_free[job.bank], 1)
            if k == 2:
                act.wait_ge(krope_in, 16 * 4)
            hi_of(act, u_lat(k + 2))
        act.wait_ge(setup, 4 + SET_TRIG)
        act.activation(sin, sin, ACT.Sin).then_inc(trig, 1)
        act.activation(cos, cos, ACT.Sin).then_inc(trig, 1)
        act.wait_ge(gemm_done, G_LAT + 5)
        hi_of(act, u_lat(6))
        for k in range(4):
            if k == 2:
                act.wait_ge(gemm_done, G_LAT + 6)
                act.wait_ge(rope_in[0], ROPE_DMAS)
                hi_of(act, u_att(0, 0))
            act.wait_ge(lat_u, k + 1)
            act.activation(lathi[:, k, :], uu[:, k % 2, :], ACT.Copy).then_inc(lat_h, 1)
        act.wait_ge(kr_v, 1)
        act.activation(kr_hi, rope1, ACT.Copy).then_inc(kr_h, 1)
        job = Job(J_LAT, 0, 2, 6)
        act.wait_ge(gemm_done, G_LAT + 7)
        act.wait_ge(ssq_done, RMS_KV + 1)
        act.activation(dt_feat, g_of(job)[0:SH, :], ACT.Copy).then_inc(g_free[job.bank], 1)
        act.wait_ge(g_free[job.bank], job.before + 1)
        act.sem_inc(dt_copied, 1)
        hi_of(act, u_att(0, 1))

        def queries_keys(x, last_exp=None):
            act.wait_ge(gemm_done, x.g + 1)
            act.activation(qn_hi[:, x.e, :], g_of(x.q)[:, :], ACT.Copy).then_inc(proj_h, 1)
            if last_exp:
                exps(*last_exp, SPLIT, TB)
                turned(last_exp[0] - 1, 1)
            act.wait_ge(gemm_done, x.g + 4)
            act.activation(kn_hi[:, x.e, :], g_of(x.k)[:, :], ACT.Copy).then_inc(proj_h, 1)
            act.wait_ge(rot, x.h + 1)
            act.activation(q_rope[:, x.e, :], rope1, ACT.Copy).then_inc(proj_h, 1)

        def head_values(x):
            act.wait_ge(gemm_done, x.g + 5)
            act.activation(v_hi[:, x.e, :], g_of(x.v)[:, :], ACT.Copy).then_inc(proj_h, 1)

        def next_queries(x, rope):
            if rope:
                act.wait_ge(*x.rope)
            hi_of(act, x.next_q)

        SPLIT = 2

        def exps(h, e, start, end):
            for qb in range(start, end):
                n, c = (qb + 1) * P, e * TB + qb
                act.wait_ge(s_neg, 4 * h + qb + 1)
                act.activation(probs[:, e, qb, 0:n], bank[qb][:, 0:n], ACT.Exp, scale=SCALE,
                               bias=negmax[:, c:c + 1], accum_out=rowsum[:, c:c + 1]).then_inc(s_exp, 1)

        def turned(h, j):
            act.wait_ge(pt_full, 4 * h + j + 1)
            act.wait_ge(pv_done, 4 * h + j + 1)
            act.activation(pthi[:, j % 2, j * P:T], bank[4 + j % 2][:, j * P:T], ACT.Copy)\
               .then_inc(pt_h, 1)

        def attend(i, e, x, rope):
            h = 2 * i + e
            if x:
                queries_keys(x, (h + 1, 1 - e))
            else:
                if e == 0:
                    exps(h + 1, 1, SPLIT, TB)
                turned(h, 1)
            turned(h, 2)
            turned(h, 3)
            if x:
                next_queries(x, rope)
            act.wait_ge(pv_done, 2 + 4 * h + 4)
            act.activation(at(fhi, h), g_of(attended(i, e))[:, :], ACT.Copy).then_inc(o_h, 1)
            if x:
                head_values(x)
            if x or e == 0:
                turned(h + 1, 0)
            if x:
                hi_of(act, x.next_kv)
                exps(x.h, x.e, 0, SPLIT)

        for e in range(2):
            x = Head(None, e)
            queries_keys(x)
            next_queries(x, True)
            head_values(x)
            if e:
                turned(0, 0)
            hi_of(act, x.next_kv)
            exps(x.h, e, 0, SPLIT if e else TB)

        def att(i, last):
            for e in range(2):
                attend(i, e, Head(i, e), not (last and e == 1))

        last_peeled(act, HEADS // 2 - 1, att)
        for e in range(2):
            attend(HEADS // 2 - 1, e, None, False)

        act.activation(a_log[:, :], a_log[:, :], ACT.Exp).then_inc(dt_a, 1)
        act.wait_ge(dt_v, 1)
        act.activation(dtneg, dtneg, ACT.Exp).then_inc(dt_a, 1)
        act.wait_ge(dt_a, 2)
        act.activation(dtneg, dtneg, ACT.Ln, bias=1.0).then_inc(dt_a, 1)

        def oa(i, last):
            for k in range(4):
                job = Job(J_OA, i, 4, k)
                act.wait_ge(gemm_done, G_OA + 4 * i + k + 1)
                act.activation(at(buf1, 4 * i + k), g_of(job)[:, :], ACT.Copy, scale=0.5)\
                   .then_inc(g_free[job.bank], 1)
                hi_of(act, u_run(R_OA, B_OA, 4, i, k + 2))

        oa(0, False)
        act.wait_ge(dt_mm, 1)
        act.activation(decay[:, :, :].rearrange("p a n -> p (a n)"), bank[2][:, 0:3 * P], ACT.Exp)\
           .then_inc(dt_a, 1)
        oa(1, True)

        def group(i, last):
            def stream(k):
                act.wait_ge(gemm_done, G_SSM + 12 * i + SSM_UNITS[k] + 1)
                return Job(J_SSM, i, 8, k)

            def refill(k):
                hi_of(act, u_ssm(i, k + 2))

            def conv(k):
                v = 4 * i + k
                cc = conv_chunk(i, k)
                job = stream(k)
                act.wait_ge(cv_out, v + 1)
                act.activation(tt[:, k % 2, :], g_of(job)[:, :], ACT.Identity,
                               scale=cols(convw, (TAPS - 1) * (XBC // P) + cc, 1),
                               bias=cols(convb, cc, 1)).then_inc(cv_acc, 1)
                refill(k)
                act.wait_ge(g_free[job.bank], job.before + 1)
                if k == 2:
                    act.wait_ge(yg_l, 2 * i + 1)
                act.activation(conv_dst(k), tt[:, k % 2, :], ACT.Tanh, scale=0.5).then_inc(cv_tanh, 1)

            def copy_in(n, dst, src):
                act.wait_ge(tin_done, 3 * i + n + 1)
                act.activation(dst, src, ACT.Copy).then_inc(tin_copied, 1)

            def exp_decay(ch):
                n = 4 * i + ch
                act.wait_ge(seg_done, n + 2)
                act.wait_ge(yd_done, n + 1)
                act.activation(sq[:, ch % 2, :], bank[0][:, :], ACT.Exp).then_inc(e_done, 1)

            def z_gate(f):
                job = stream(4 + f)
                act.activation(zs[:, f, :], g_of(job)[:, :], ACT.Tanh, scale=0.5).then_inc(z_tanh, 1)

            conv(0)
            conv(1)
            conv(2)
            conv(3)
            copy_in(0, b_tok[:, :], bank[4][:, :])
            exp_decay(0)
            z_gate(0)
            copy_in(1, x_tok[:, :, 0:P], bank[5][:, :].rearrange("p (a n) -> p a n", a=TB))
            copy_in(2, x_tok[:, :, P:GF], bank[4][:, :].rearrange("p (a n) -> p a n", a=TB))
            exp_decay(1)
            refill(4)
            z_gate(1)
            exp_decay(2)
            refill(5)
            exp_decay(3)
            job = stream(6)
            act.activation(uu[:, 0, :], g_of(job)[:, :], ACT.Tanh, scale=0.5).then_inc(g_free[job.bank], 1)
            refill(6)
            for f in range(2):
                act.wait_ge(gt_done, 2 * i + f + 2)
                act.activation(sq[:, f, :], zs[:, f, :], ACT.Square).then_inc(gsq_done, 1)
            job = stream(7)
            act.activation(at(buf2, i), g_of(job)[:, :], ACT.Tanh, scale=0.5).then_inc(g_free[job.bank], 1)
            refill(7)
            for f in range(2):
                act.wait_ge(yg_u, 2 * i + f + 1)
                act.activation(at(fhi, 2 * i + f), uu[:, f, :], ACT.Copy).then_inc(yg_h, 1)

        last_peeled(act, GROUPS, group)

        def os_(i, last):
            for c in range(2):
                for half in range(2):
                    k = 2 * c + half
                    act.wait_ge(gemm_done, G_OS + 4 * i + k + 1)
                    hi_of(act, u_run(R_OS, B_OS, 4, i, k + 2))
                act.wait_ge(mg_u, 2 * i + c + 1)
                act.activation(at(ahi, 2 * i + c), uu[:, c, :], ACT.Copy).then_inc(mg_h, 1)

        last_peeled(act, 4, os_)
        act.wait_ge(mg_l, 1 + KC)
        act.dma_start(buf1[:, :, :].rearrange("p k n -> p (k n)"), xt_dram).then_inc(xt_in, 16)

        def out_(i, last):
            for k in range(4):
                c = 4 * i + k
                job = Job(J_OUT, i, 4, k)
                act.wait_ge(gemm_done, G_OUT + c + 1)
                square_into(act, KC + c, k % 2, g_of(job)[:, :])
                act.activation(at(buf2, c), g_of(job)[:, :], ACT.Copy).then_inc(g_free[job.bank], 1)
                hi_of(act, u_run(R_OUT, B_OUT, 4, i, k + 2))

        last_peeled(act, 2, out_)
        for c in range(KC):
            act.wait_ge(x1_done, c + 1)
            square_into(act, 2 * KC + c, c % 2, buf1[:, c, :])
        modulate_act(act, 1, g_mlp, 24)

        for half in range(2):
            r0, b0, g0, j0 = R_FF + 32 * half, B_FF + 32 * half, G_FF + 32 * half, J_FF + J_HALF * half

            def up(i, last, r0=r0, b0=b0, g0=g0, j0=j0, half=half):
                for k in range(4):
                    f = 16 * half + 4 * i + k
                    job = Job(j0, i, 4, k)
                    act.wait_ge(gemm_done, g0 + 4 * i + k + 1)
                    act.wait_ge(ff_q, f + 1)
                    act.activation(tt[:, k % 2, :], g_of(job)[:, :], ACT.Relu).then_inc(g_free[job.bank], 1)
                    hi_of(act, u_run(r0, b0, 4, i, k + 2))
                    act.wait_ge(ff_q, f + 2)
                    act.activation(at(fhi, 4 * i + k), uu[:, k % 2, :], ACT.Copy).then_inc(ff_h, 1)

            last_peeled(act, 4, up)

            def down(i, last, r0=r0 + 16, b0=b0 + 16, g0=g0 + 16, j0=j0 + 16, half=half):
                for c in range(2):
                    job = Job(j0, i, 2, c)
                    for part in range(2):
                        k = 2 * c + part
                        act.wait_ge(gemm_done, g0 + 4 * i + k + 1)
                        if not (half == 1 and last and k >= 2):
                            hi_of(act, u_run(r0, b0, 4, i, k + 2))
                    if half == 0:
                        act.activation(at(buf2, 2 * i + c), g_of(job)[:, :], ACT.Copy)\
                           .then_inc(g_free[job.bank], 1)
                    else:
                        act.wait_ge(g_free[job.bank], job.before + 1)
                        square_into(act, 3 * KC + 2 * i + c, c % 2, at(buf2, 2 * i + c))

            last_peeled(act, 4, down)
        for c in range(KC):
            act.wait_ge(fin_tr, c + 1)
            if c >= 4:
                act.wait_ge(out_sent[c % 4], 16 * (c // 4))
            act.activation(ost[c % 4], bank[2 + c % 2][:, :], ACT.Copy).then_inc(fin_copy, 1)

    @block.vector
    def _(dve):
        dve.sem_inc(pt_l, 2)
        dve.sem_inc(cv_out, 2)
        for s in (ada_out, cbm_done, m_done, h_done, y_done, gt_done, yg_l, mg_l, ff_l):
            dve.sem_inc(s, 1)
        dve.wait_ge(small_in, SMALL)
        dve.tensor_copy(strict_r[:, :], strict).then_inc(setup, 1)
        dve.wait_ge(silu_done, 1)

        def ada_rows(n):
            first, count = ADA_DVE[n][0], len(ADA_DVE[n])
            wait_ada(dve, first, count)
            w = ada_units(first, count)
            total = w[:, :, 0:P]
            for k in range(KC):
                if k:
                    dve.wait_ge(ada_step, KC * n + k)
                    ins = dve.scalar_tensor_tensor(total, w[:, :, k * P:(k + 1) * P], silu_c[:, k:k + 1],
                                                   total, ALU.mult, ALU.add)
                else:
                    ins = dve.tensor_scalar(total, total, silu_c[:, 0:1], None, ALU.mult)
                ins.then_inc(ada_step, 1)

        for n in range(4):
            ada_rows(n)
        rms_dve(dve, RMS_X, bank[0], D)
        for n in range(4, len(ADA_DVE)):
            ada_rows(n)
        dve.wait_ge(vec_c, 1)
        dve.tensor_scalar(d_half[:, :], d_half[:, :], 0.5, None, ALU.mult).then_inc(setup, 1)
        dve.wait_ge(columns, 1)
        dve.tensor_tensor(mod[:, 0:16], bank[5][:, 0:16], vec[:, 0:16], ALU.add).then_inc(setup, 1)
        dve.wait_ge(setup, 3)
        row = VEC["g_pre_mix"][0]
        dve.scalar_tensor_tensor(g_mix[:, :], mod[:, 8:16], 1.0, vec[:, row:row + 8], ALU.add, ALU.mult)\
           .then_inc(setup, 1)
        dve.wait_ge(xt_copied, KC)
        dve.wait_ge(rep_done, RMS_X + 1)

        def first_units(c):
            if c in (-1, 1):
                lo_of(dve, u_lat(max(c, 0)))

        modulate_dve(dve, 0, xt, bank[0], first_units)

        step = [4]

        def chain(ins):
            ins.then_inc(setup, 1)
            step[0] += 1
            dve.wait_ge(setup, step[0])

        def reduced(out, quarter):
            turns = rope2
            chain(dve.tensor_scalar(turns, rope1, 1.0 / (2 * np.pi), quarter, ALU.mult, ALU.add))
            chain(dve.tensor_scalar(turns, turns, MAGIC, -MAGIC, ALU.add, ALU.add))
            chain(dve.scalar_tensor_tensor(out, turns, -TWO_PI_1, rope1, ALU.mult, ALU.add))
            chain(dve.scalar_tensor_tensor(out, turns, -TWO_PI_2, out, ALU.mult, ALU.add))
            chain(dve.scalar_tensor_tensor(out, turns, -TWO_PI_3, out, ALU.mult, ALU.add))
            chain(dve.tensor_scalar(out, out, quarter * 2 * np.pi, PI_IN, ALU.add, ALU.min))
            chain(dve.tensor_scalar(out, out, -PI_IN, None, ALU.max))

        lo_of(dve, u_lat(2))
        dve.wait_ge(pos_in, 16)
        chain(dve.tensor_copy(rope2, pos_i))
        chain(dve.tensor_scalar(rope1, rope2, con[:, CON_FREQ:CON_FREQ + 1], None, ALU.mult))
        lo_of(dve, u_lat(3))
        reduced(sin, 0.0)
        lo_of(dve, u_lat(4))
        reduced(cos, 0.25)
        assert step[0] == 4 + SET_TRIG
        rms_dve(dve, RMS_Q, bank[0], RANK)
        lo_of(dve, u_lat(5))
        dve.wait_ge(trig, 2)
        chain(dve.tensor_scalar(sin, sin, con[:, CON_SIGN:CON_SIGN + 1], None, ALU.mult))

        job = Job(J_LAT, 0, 2, 4)
        dve.wait_ge(gemm_done, G_LAT + 5)
        dve.tensor_tensor(rope1, g_of(job)[:, :], cos, ALU.mult).then_inc(g_free[job.bank], 1)

        def latents(k0, gain, rbank, r):
            dve.wait_ge(rep_done, r + 1)
            row = VEC[gain][0]
            for k in range(k0, k0 + 2):
                wait(dve, lat_l, k - 1)
                dve.scalar_tensor_tensor(uu[:, k % 2, :], lat[:, k, :], vec[:, row + k - k0:row + k - k0 + 1],
                                         rbank[:, :], ALU.mult, ALU.mult).then_inc(lat_u, 1)
            for k in range(k0, k0 + 2):
                dve.wait_ge(lat_h, k + 1)
                dve.tensor_tensor(latlo[:, k, :], uu[:, k % 2, :], lathi[:, k, :].bitcast(F32),
                                  ALU.subtract).then_inc(lat_l, 1)

        rms_dve(dve, RMS_KV, bank[1], RANK)
        latents(0, "g_q_lat", bank[0], RMS_Q)
        lo_of(dve, u_lat(6))
        job = Job(J_LAT, 0, 2, 5)
        dve.wait_ge(gemm_done, G_LAT + 6)
        dve.tensor_tensor(rope2, g_of(job)[:, :], sin, ALU.mult).then_inc(g_free[job.bank], 1)
        dve.wait_ge(g_free[1], 3)
        dve.wait_ge(g_free[0], 3)
        dve.tensor_tensor(rope1, rope1, rope2, ALU.add).then_inc(kr_v, 1)
        lo_of(dve, u_att(0, 0))
        latents(2, "g_kv_lat", bank[1], RMS_KV)
        dve.wait_ge(kr_h, 1)
        dve.tensor_tensor(kr_lo, rope1, kr_hi.bitcast(F32), ALU.subtract).then_inc(kr_v, 1)

        def low(x, dst, job, hi, n):
            dve.wait_ge(proj_h, 4 * x.h + n)
            dve.tensor_tensor(dst, g_of(job)[:, :], hi.bitcast(F32), ALU.subtract)\
               .then_inc(g_free[job.bank], 1)

        def queries(x):
            low(x, qn_lo[:, x.e, :], x.q, qn_hi[:, x.e, :], 1)

        def rotation(x, meanwhile=None):
            dve.wait_ge(gemm_done, x.g + 2)
            dve.tensor_tensor(rope1, g_of(x.r1)[:, :], cos, ALU.mult).then_inc(g_free[x.r1.bank], 1)
            if meanwhile:
                meanwhile()
            dve.wait_ge(gemm_done, x.g + 3)
            dve.tensor_tensor(rope2, g_of(x.r2)[:, :], sin, ALU.mult).then_inc(g_free[x.r2.bank], 1)
            dve.wait_ge(g_free[x.r1.bank], x.r1.before + 1)
            dve.wait_ge(g_free[x.r2.bank], x.r2.before + 1)
            dve.tensor_tensor(rope1, rope1, rope2, ALU.add).then_inc(rot, 1)

        def keys(x):
            low(x, kn_lo[:, x.e, :], x.k, kn_hi[:, x.e, :], 2)
            dve.wait_ge(proj_h, 4 * x.h + 3)
            dve.tensor_tensor(q_rope[ROPE:P, x.e, :], rope1[ROPE:P], q_rope[ROPE:P, x.e, :].bitcast(F32),
                              ALU.subtract).then_inc(proj_l, 1)

        def head_values(x):
            low(x, v_lo[:, x.e, :], x.v, v_hi[:, x.e, :], 4)

        def softmax(x):
            for qb in range(TB):
                c = x.e * TB + qb
                dve.wait_ge(s_full, 4 * x.h + qb + 1)
                blk = bank[qb][:, qb * P:(qb + 1) * P]
                dve.tensor_tensor(blk, blk, mask, ALU.add).then_inc(s_masked, 1)
                dve.wait_ge(s_masked, 4 * x.h + qb + 1)
                dve.tensor_reduce(rowmax[:, c:c + 1], bank[qb][:, 0:(qb + 1) * P], AX.X, ALU.max)\
                   .then_inc(s_max, 1)
                dve.wait_ge(s_max, 4 * x.h + qb + 1)
                dve.tensor_scalar(negmax[:, c:c + 1], rowmax[:, c:c + 1], -SCALE, None, ALU.mult)\
                   .then_inc(s_neg, 1)

        def inverse(h, e):
            dve.wait_ge(s_exp, 4 + 4 * h + 4)
            dve.reciprocal(rowinv[:, e * TB:(e + 1) * TB], rowsum[:, e * TB:(e + 1) * TB])\
               .then_inc(s_inv, 1)

        def turned(h, j):
            dve.wait_ge(pt_h, 4 * h + j + 1)
            dve.tensor_tensor(ptlo[:, j % 2, j * P:T], bank[4 + j % 2][:, j * P:T],
                              pthi[:, j % 2, j * P:T].bitcast(F32), ALU.subtract).then_inc(pt_l, 1)

        def attend(i, e, x):
            h, job = 2 * i + e, attended(i, e)
            if x:
                queries(x)
                rotation(x, lambda: (turned(h, 0), turned(h, 1)))
            else:
                turned(h, 0)
                turned(h, 1)
            if x or e == 0:
                inverse(h + 1, 1 - e)
            if x:
                keys(x)
            turned(h, 2)
            turned(h, 3)
            dve.wait_ge(o_h, h + 1)
            dve.tensor_tensor(at(flo, h), g_of(job)[:, :], at(fhi, h).bitcast(F32), ALU.subtract)\
               .then_inc(g_free[job.bank], 1)
            if x:
                head_values(x)
            if x:
                softmax(x)

        for e in range(2):
            x = Head(None, e)
            if e:
                inverse(0, 0)
            queries(x)
            rotation(x)
            keys(x)
            head_values(x)
            softmax(x)
        with dve.Fori(0, HEADS // 2 - 1) as i:
            for e in range(2):
                attend(i, e, Head(i, e))
        for e in range(2):
            attend(HEADS // 2 - 1, e, None)
        dve.wait_ge(w_lo, B_OA + 2)

        dve.wait_ge(dt_tok, 1)
        dve.tensor_tensor(dtx.rearrange("p (a n) -> p a n", a=TB),
                          bank[2][:, 3 * P:4 * P].rearrange("p (a n) -> p a n", a=TB),
                          dt_bias[:, :].unsqueeze(1).broadcast_to([P, TB, SH]), ALU.add)\
           .then_inc(dt_x, 1)
        dve.wait_ge(dt_x, 1)
        dve.scalar_tensor_tensor(dtneg, dtx, -1.0, dtx, ALU.mult, ALU.min).then_inc(dt_v, 1)
        dve.wait_ge(dt_a, 3)
        dve.scalar_tensor_tensor(dtx, dtx, 0.0, dtneg, ALU.max, ALU.add).then_inc(dt_v, 1)
        dve.wait_ge(dt_v, 2)
        dve.scalar_tensor_tensor(dta[:, :].rearrange("p (a n) -> p a n", a=TB),
                                 dtx.rearrange("p (a n) -> p a n", a=TB), -1.0,
                                 a_log[:, :].unsqueeze(1).broadcast_to([P, TB, SH]), ALU.mult, ALU.mult)\
           .then_inc(dt_v, 1)
        dve.tensor_scalar(dt_half[:, :], dtx, 0.5, None, ALU.mult).then_inc(dt_v, 1)
        dve.wait_ge(dt_v, 4)
        dve.tensor_copy(dta_hi[:, :], dta[:, :]).then_inc(dt_v, 1)
        dve.wait_ge(dt_v, 5)
        dve.tensor_tensor(dta_lo[:, :], dta[:, :], dta_hi[:, :].bitcast(F32), ALU.subtract)\
           .then_inc(dt_v, 1)

        def oa(i, last):
            for k in range(4):
                lo_of(dve, u_run(R_OA, B_OA, 4, i, k + 2))

        oa(0, False)
        dve.wait_ge(dt_a, 4)
        dve.scalar_tensor_tensor(dt_end[:, :], dt_half[:, :], 0.5, decay[:, 1, :], ALU.mult, ALU.mult)\
           .then_inc(dt_v, 1)
        dve.tensor_scalar(decay[:, 0, :], decay[:, 0, :], 0.5, None, ALU.mult).then_inc(dt_v, 1)
        oa(1, True)

        def group(i, last):
            def heads(table, ch):
                return cols(table, ch * SH + GH * i, GH)

            def refill(k):
                lo_of(dve, u_ssm(i, k + 2))

            def conv(k):
                v = 4 * i + k
                cc = conv_chunk(i, k)
                job = Job(J_SSM, i, 8, k)
                acc, src = tt[:, k % 2, :], g_of(job)
                dve.wait_ge(cv_acc, v + 1)
                for n, tap in enumerate((2, 1, 0)):
                    s = TAPS - 1 - tap
                    if n:
                        dve.wait_ge(cv_tap, 2 * v + n)
                    ins = dve.scalar_tensor_tensor(acc[:, s:T], src[:, 0:T - s],
                                                   cols(convw, tap * (XBC // P) + cc, 1), acc[:, s:T],
                                                   ALU.mult, ALU.add)
                    if n < 2:
                        ins.then_inc(cv_tap, 1)
                    else:
                        ins.then_inc(g_free[job.bank], 1)
                refill(k)
                dve.wait_ge(cv_tanh, v + 1)
                dve.scalar_tensor_tensor(conv_dst(k), conv_dst(k), 1.0, acc, ALU.add, ALU.mult)\
                   .then_inc(cv_out, 1)

            def masked(ch):
                n = 4 * i + ch
                dve.wait_ge(cb_done, n + 1)
                dve.wait_ge(m_done, n + 1)
                dve.scalar_tensor_tensor(cbm[:, :], bank[1][:, 0:P], 0.25, tri, ALU.mult, ALU.mult)\
                   .then_inc(cbm_done, 1)
                dve.wait_ge(cbm_done, n + 2)
                dve.wait_ge(e_done, n + 2)
                e = sq[:, ch % 2, :].rearrange("p (h l) -> p h l", h=GH)
                dve.tensor_tensor(e, e, cbm[:, :].unsqueeze(1).broadcast_to([P, GH, P]), ALU.mult)\
                   .then_inc(m_done, 1)

            def outputs(ch):
                n = 4 * i + ch
                off, diag = bank[2][:, 0:GF], bank[2][:, GF:2 * GF]
                dve.wait_ge(yd_done, 2 + n + 1)
                dve.wait_ge(yt_done, n + 1)
                if ch == 0:
                    dve.wait_ge(xd_done, n + 1)
                    dve.tensor_tensor(y[:, :], diag, xd[:, ch % 2, :], ALU.add).then_inc(y_done, 1)
                else:
                    m = 6 * i + 2 * (ch - 1)
                    dve.tensor_tensor(y[:, :].rearrange("p (h d) -> p h d", h=GH),
                                      off.rearrange("p (h d) -> p h d", h=GH),
                                      heads(decay[:, 0, :], ch).unsqueeze(2).broadcast_to([P, GH, HD]),
                                      ALU.mult).then_inc(y_part, 1)
                    dve.wait_ge(y_part, m + 1)
                    dve.tensor_tensor(y[:, :], diag, y[:, :], ALU.add).then_inc(y_part, 1)
                    dve.wait_ge(y_part, m + 2)
                    dve.tensor_tensor(y[:, :], y[:, :], xd[:, ch % 2, :], ALU.add).then_inc(y_done, 1)

            def advance(ch):
                dve.wait_ge(s_done, 3 * i + ch + 1)
                if ch == 0:
                    dve.tensor_copy(state[:, :], bank[3][:, 0:GF]).then_inc(h_done, 1)
                else:
                    st = state[:, :].rearrange("p (h d) -> p h d", h=GH)
                    dve.tensor_tensor(st, st, heads(decay[:, 2, :], ch).unsqueeze(2)
                                      .broadcast_to([P, GH, HD]), ALU.mult).then_inc(h_scaled, 1)
                    dve.wait_ge(h_scaled, 2 * i + ch)
                    dve.tensor_tensor(state[:, :], bank[3][:, 0:GF], state[:, :], ALU.add)\
                       .then_inc(h_done, 1)

            def z_gate(f):
                job = Job(J_SSM, i, 8, 4 + f)
                dve.wait_ge(z_tanh, 2 * i + f + 1)
                dve.scalar_tensor_tensor(zs[:, f, :], zs[:, f, :], 1.0, g_of(job)[:, :], ALU.add, ALU.mult)\
                   .then_inc(g_free[job.bank], 1)

            for k in range(4):
                conv(k)
            masked(0)
            z_gate(0)
            masked(1)
            refill(4)
            outputs(0)
            advance(0)
            z_gate(1)
            masked(2)
            refill(5)
            outputs(1)
            advance(1)
            masked(3)
            outputs(2)
            advance(2)
            job = Job(J_SSM, i, 8, 6)
            dve.wait_ge(g_free[job.bank], job.before + 1)
            dve.scalar_tensor_tensor(at(buf1, i), uu[:, 0, :], 1.0, at(buf1, i), ALU.add, ALU.mult)\
               .then_inc(ga_out, 1)
            refill(6)
            outputs(3)
            for f in range(2):
                if f == 0:
                    dve.wait_ge(yt_done, 1 + 4 * i + 4)
                dve.scalar_tensor_tensor(zs[:, f, :], bank[4 + f][:, :], 0.5, zs[:, f, :], ALU.mult,
                                         ALU.mult).then_inc(gt_done, 1)
            dve.wait_ge(gsq_done, 2 * i + 2)
            dve.tensor_tensor(sq[:, 0, :], sq[:, 0, :], sq[:, 1, :], ALU.add).then_inc(gsq_added, 1)
            rms_dve(dve, RMS_G + i, bank[1], GF)
            dve.wait_ge(gemm_done, G_SSM + 12 * i + ADA_UNITS[3] + 1)
            dve.tensor_tensor(cols(mod, 16 + 4 * i, 4), bank[3][:, GF:GF + 4], cols(vec, 16 + 4 * i, 4),
                              ALU.add).then_inc(ada_out, 1)
            refill(7)
            dve.wait_ge(rep_done, RMS_G + i + 1)
            dve.wait_ge(ga_out, i + 1)
            row = VEC["g_ssm_out"][0]
            for f in range(2):
                dve.scalar_tensor_tensor(uu[:, f, :], zs[:, f, :], cols(vec, row + 2 * i + f, 1),
                                         bank[1][:, :], ALU.mult, ALU.mult).then_inc(yg_u, 1)
            for f in range(2):
                dve.wait_ge(yg_h, 2 * i + f + 1)
                dve.tensor_tensor(at(flo, 2 * i + f), uu[:, f, :], at(fhi, 2 * i + f).bitcast(F32),
                                  ALU.subtract).then_inc(yg_l, 1)

        last_peeled(dve, GROUPS, group)

        dve.wait_ge(ada_out, 1 + GROUPS)
        row = VEC["g_pre_mlp"][0]
        dve.scalar_tensor_tensor(g_mlp[:, :], mod[:, 32:40], 1.0, vec[:, row:row + 8], ALU.add, ALU.mult)\
           .then_inc(mod_done, 1)
        row = VEC["g_post_mix"][0]
        dve.tensor_tensor(gp_mix[:, :], mod[:, 16:24], vec[:, row:row + 8], ALU.mult).then_inc(mod_done, 1)
        row = VEC["g_post_mlp"][0]
        dve.tensor_tensor(gp_mlp[:, :], mod[:, 40:48], vec[:, row:row + 8], ALU.mult).then_inc(mod_done, 1)

        def os_(i, last):
            for c in range(2):
                n = 2 * i + c
                job = Job(J_OS, i, 2, c)
                lo_of(dve, u_run(R_OS, B_OS, 4, i, 2 * c + 2))
                dve.wait_ge(gemm_done, G_OS + 4 * i + 2 * c + 2)
                dve.wait_ge(mg_l, n + 1)
                dve.scalar_tensor_tensor(tt[:, c, :], at(buf2, n), 1.0, g_of(job)[:, :], ALU.add,
                                         ALU.mult).then_inc(g_free[job.bank], 1)
                dve.wait_ge(g_free[job.bank], job.before + 1)
                dve.scalar_tensor_tensor(uu[:, c, :], tt[:, c, :], 0.5, at(buf1, n), ALU.mult, ALU.add)\
                   .then_inc(mg_u, 1)
                lo_of(dve, u_run(R_OS, B_OS, 4, i, 2 * c + 3))
                dve.wait_ge(mg_h, n + 1)
                dve.tensor_tensor(at(alo, n), uu[:, c, :], at(ahi, n).bitcast(F32), ALU.subtract)\
                   .then_inc(mg_l, 1)

        last_peeled(dve, 4, os_)

        def out_(i, last):
            for k in range(4):
                lo_of(dve, u_run(R_OUT, B_OUT, 4, i, k + 2))

        last_peeled(dve, 2, out_)
        rms_dve(dve, RMS_MIX, bank[0], D)
        dve.wait_ge(rep_done, RMS_MIX + 1)
        dve.wait_ge(xt_in, 16)
        dve.wait_ge(mod_done, 3)

        def add_x(c):
            dve.wait_ge(x1_t, c + 1)
            dve.tensor_tensor(buf1[:, c, :], tt[:, c % 2, :], buf1[:, c, :], ALU.add).then_inc(x1_done, 1)

        for c in range(KC):
            wait(dve, x1_done, c - 1)
            dve.scalar_tensor_tensor(tt[:, c % 2, :], buf2[:, c, :], gp_mix[:, c:c + 1], bank[0][:, :],
                                     ALU.mult, ALU.mult).then_inc(x1_t, 1)
            if c:
                add_x(c - 1)
        add_x(KC - 1)
        dve.wait_ge(x1_done, KC)
        rms_dve(dve, RMS_MLP, bank[1], D)
        dve.wait_ge(rep_done, RMS_MLP + 1)
        modulate_dve(dve, 1, buf1, bank[1])

        for half in range(2):
            r0, b0, g0, j0 = R_FF + 32 * half, B_FF + 32 * half, G_FF + 32 * half, J_FF + J_HALF * half

            def up(i, last, r0=r0, b0=b0, half=half):
                for k in range(4):
                    f = 16 * half + 4 * i + k
                    lo_of(dve, u_run(r0, b0, 4, i, k + 2))
                    dve.wait_ge(ff_h, f + 1)
                    dve.tensor_tensor(at(flo, 4 * i + k), uu[:, k % 2, :], at(fhi, 4 * i + k).bitcast(F32),
                                      ALU.subtract).then_inc(ff_l, 1)

            last_peeled(dve, 4, up)

            def down(i, last, r0=r0 + 16, b0=b0 + 16, g0=g0 + 16, j0=j0 + 16, half=half):
                for c in range(2):
                    job = Job(j0, i, 2, c)
                    for part in range(2):
                        if not (half == 1 and last and c == 1):
                            lo_of(dve, u_run(r0, b0, 4, i, 2 * c + part + 2))
                    if half == 1:
                        dve.wait_ge(gemm_done, g0 + 4 * i + 2 * c + 2)
                        dve.tensor_tensor(at(buf2, 2 * i + c), g_of(job)[:, :], at(buf2, 2 * i + c),
                                          ALU.add).then_inc(g_free[job.bank], 1)

            last_peeled(dve, 4, down)
        rms_dve(dve, RMS_FF, bank[0], D)
        dve.wait_ge(rep_done, RMS_FF + 1)
        for c in range(KC):
            if c >= 2:
                dve.wait_ge(fin_done[c % 2], c // 2)
            dve.scalar_tensor_tensor(tt[:, c % 2, :], buf2[:, c, :], gp_mlp[:, c:c + 1], bank[0][:, :],
                                     ALU.mult, ALU.mult).then_inc(fin_t, 1)
            if c % 2 == 1:
                dve.wait_ge(fin_t, c)
                dve.tensor_tensor(buf2[:, c - 1, :], tt[:, 0, :], buf1[:, c - 1, :], ALU.add)\
                   .then_inc(fin_done[0], 1)

    @block.gpsimd
    def _(pool):
        pool.sem_inc(ff_q, 1)
        pool.memset(minus_half[:, :], -0.5).then_inc(pool_setup, 1)
        pool.wait_ge(pool_setup, 1)
        clear_sum(pool, 0)
        for c in range(KC):
            add_square(pool, c, c % 2, 1)
        pool.wait_ge(silu_done, 1)
        wait_ada(pool, ADA_POOL[0], 2)
        two = ada_units(ADA_POOL[0], 2)
        w4 = two.rearrange("p u (k n) -> p u k n", k=KC)
        pool.tensor_tensor(w4, w4, silu_c[:, :].unsqueeze(1).unsqueeze(3)
                           .broadcast_to([P, 2, KC, P]), ALU.mult).then_inc(pool_step, 1)
        rms_pool(pool, RMS_X)
        for n, width in enumerate((4 * P, 2 * P, P)):
            pool.wait_ge(pool_step, n + 1)
            pool.tensor_tensor(two[:, :, 0:width], two[:, :, 0:width], two[:, :, width:2 * width],
                               ALU.add).then_inc(pool_step, 1)
        for r in (RMS_Q, RMS_KV):
            rms_pool(pool, r)

        def normalise(h, e):
            pool.wait_ge(s_inv, h + 1)
            for qb in range(TB):
                blk = probs[:, e, qb, 0:(qb + 1) * P]
                inv = rowinv[:, e * TB + qb:e * TB + qb + 1]
                if qb == 0:
                    ins = pool.tensor_tensor(blk, blk, inv.broadcast_to([P, P]), ALU.mult)
                else:
                    ins = pool.tensor_scalar(blk, blk, inv, 1.0, ALU.mult, ALU.mult)
                ins.then_inc(p_norm, 1)

        pool.wait_ge(w_lo, B_ATT + 1)
        lo_of(pool, u_att(0, 1))
        for e in range(2):
            x = Head(None, e)
            if e:
                normalise(0, 0)
            lo_of(pool, x.next_q)
            lo_of(pool, x.next_kv)
        with pool.Fori(0, HEADS // 2 - 1) as i:
            for e in range(2):
                x = Head(i, e)
                normalise(2 * i + e + 1, 1 - e)
                lo_of(pool, x.next_q)
                lo_of(pool, x.next_kv)
        normalise(HEADS - 1, 1)
        pool.wait_ge(gemm_done, G_SSM)
        pool.wait_ge(dt_v, 8)

        def group(i, last):
            def ramps(ch):
                pool.wait_ge(seg_done, 4 * i + ch + 1)
                for dst, table in ((rm_hi, dta_hi), (rm_lo, dta_lo)):
                    col = cols(table, ch * SH + GH * i, GH)
                    if table is dta_hi:
                        col = col.bitcast(F32)
                    ins = pool.tensor_tensor(dst[:, :].rearrange("p (h l) -> p h l", h=GH),
                                             tri.unsqueeze(1).broadcast_to([P, GH, P]),
                                             col.unsqueeze(2).broadcast_to([P, GH, P]), ALU.mult)
                ins.then_inc(rm_done, 1)

            def scaled(ch):
                if ch == 0:
                    pool.wait_ge(tin_copied, 3 * i + 3)
                elif ch >= 2:
                    pool.wait_ge(s_done, 3 * i + ch - 1)
                    pool.wait_ge(y_done, 4 * i + ch)
                src = x_tok[:, ch, :].rearrange("p (h d) -> p h d", h=GH)
                for dst, table in ((xdt, cols(dt_half, ch * SH + GH * i, GH)),
                                   (xend, cols(dt_end, ch * SH + GH * i, GH)),
                                   (xd, cols(d_half, GH * i, GH))):
                    ins = pool.tensor_tensor(dst[:, ch % 2, :].rearrange("p (h d) -> p h d", h=GH), src,
                                             table.unsqueeze(2).broadcast_to([P, GH, HD]), ALU.mult)
                ins.then_inc(xd_done, 1)

            def ada(j):
                unit = Unit(R_SSM, 0, i, 12, 0, ADA_UNITS[j], 0)
                pool.wait_ge(raw_in[unit.slot], unit.landed)
                w = raw[:, unit.slot, :]
                w3 = w.rearrange("p (k n) -> p k n", k=KC)
                pool.tensor_tensor(w3, w3, silu_c[:, :].unsqueeze(2).broadcast_to([P, KC, P]), ALU.mult)\
                    .then_inc(ada_part, 1)
                for n, width in enumerate((4 * P, 2 * P, P)):
                    pool.wait_ge(ada_part, 3 * (4 * i + j) + n + 1)
                    pool.tensor_tensor(w[:, 0:width], w[:, 0:width], w[:, width:2 * width], ALU.add)\
                        .then_inc(ada_part if n < 2 else ada_sum, 1)

            ada(0)
            ramps(0)
            ada(1)
            ramps(1)
            ada(2)
            scaled(0)
            ramps(2)
            scaled(1)
            ramps(3)
            scaled(2)
            scaled(3)
            ada(3)
            rms_pool(pool, RMS_G + i)

        last_peeled(pool, GROUPS, group)

        clear_sum(pool, RMS_G + GROUPS)

        def out_(i, last):
            for k in range(3 if last else 4):
                add_square(pool, KC + 4 * i + k, k % 2, 2)

        last_peeled(pool, 2, out_)
        rms_pool(pool, RMS_MIX)
        clear_sum(pool, RMS_MIX + 1)
        for c in range(KC - 1):
            add_square(pool, 2 * KC + c, c % 2, 3)
        rms_pool(pool, RMS_MLP)
        for half in range(2):
            def up(i, last, half=half):
                for k in range(4):
                    f = 16 * half + 4 * i + k
                    job = Job(J_FF + J_HALF * half, i, 4, k)
                    pool.wait_ge(g_free[job.bank], job.before + 1)
                    pool.wait_ge(ff_l, f + 1)
                    pool.tensor_tensor(uu[:, k % 2, :], tt[:, k % 2, :], tt[:, k % 2, :], ALU.mult)\
                        .then_inc(ff_q, 1)

            last_peeled(pool, 4, up)
        clear_sum(pool, RMS_MLP + 1)

        def down(i, last):
            for c in range(1 if last else 2):
                add_square(pool, 3 * KC + 2 * i + c, c, 4)

        last_peeled(pool, 4, down)
        rms_pool(pool, RMS_FF)
        for c in range(1, KC, 2):
            pool.wait_ge(fin_t, c + 1)
            pool.tensor_tensor(buf2[:, c, :], tt[:, 1, :], buf1[:, c, :], ALU.add).then_inc(fin_done[1], 1)


NAMES = ("x", "c", "positions", "w_ada", "b_ada", "g_pre_mix", "g_post_mix", "w_in", "g_q_lat",
         "g_kv_lat", "w_uq", "w_ukv", "w_o_attn", "conv_w", "conv_b", "dt_bias", "a_log", "d_skip",
         "g_ssm_out", "w_o_ssm", "w_out", "g_pre_mlp", "g_post_mlp", "w_ff1", "w_ff2")


def kernel(**inputs):
    import concourse.bacc as bacc
    from concourse.bass_utils import run_bass_kernel_spmd

    nc = bacc.Bacc("TRN2", target_bir_lowering=False, num_devices=1)
    arrays = {f"in_{n}": np.ascontiguousarray(inputs[n]) for n in NAMES}
    arrays["in_con"] = constants()
    aps = {}
    for n, v in arrays.items():
        aps[n[3:]] = nc.dram_tensor(n, v.shape, mybir.dt.from_np(v.dtype), kind="ExternalInput").ap()
    aps["out"] = nc.dram_tensor("out", (1, T, D), F32, kind="ExternalOutput").ap()
    build(nc, aps)
    r = run_bass_kernel_spmd(nc, [arrays], core_ids=[0])
    return r.results[0]["out"]
```
